# Optimizing a Trainium2 kernel written in Bass

```python
import jax
import jax.numpy as jnp
from jax import lax
import numpy as np

D_MODEL = 1024
BATCH = 1
SEQ = 1024
DEPTH = 2
DEC_BATCH = 8
DEC_SEQ = 16
PAST_LEN = 1024

CHUNK = 64
A_HEADS = 8
A_KV_HEADS = 2
A_GROUP = A_HEADS // A_KV_HEADS
HEAD_DIM = 64
A_Q = A_HEADS * HEAD_DIM
A_KV = A_KV_HEADS * HEAD_DIM
WINDOW = 128
WIN_CHUNKS = WINDOW // CHUNK
ROPE_DIM = HEAD_DIM // 4
ROPE_THETA = 500000.0
CONV_CH = D_MODEL // 2
CONV_W = 31
M_HEADS = 4
M_WIDTH = D_MODEL
M_DIM = M_WIDTH // M_HEADS
QK_CONV_W = 4
D_FF = 4 * D_MODEL
EVEN_IN = A_Q + 2 * A_KV + 2 * CONV_CH
EVEN_MIX = A_Q + CONV_CH
ODD_IN = 4 * M_WIDTH + 2 * M_HEADS
N_EVEN = (DEPTH + 1) // 2
N_ODD = DEPTH // 2
EPS = 1e-6

kernel_name = 'hybrid_streaming_swa_conformer_mlstm_step'

def rmsnorm(x, g):
    xf = x.astype(jnp.float32)
    y = xf * lax.rsqrt(jnp.mean(xf * xf, axis=-1, keepdims=True) + EPS)
    return (y * g.astype(jnp.float32)).astype(x.dtype)

def layernorm(x, g, b):
    xf = x.astype(jnp.float32)
    xc = xf - jnp.mean(xf, axis=-1, keepdims=True)
    y = xc * lax.rsqrt(jnp.mean(xc * xc, axis=-1, keepdims=True) + EPS)
    return (y * g.astype(jnp.float32) + b.astype(jnp.float32)).astype(x.dtype)

def partial_rope(x, pos):
    half = ROPE_DIM // 2
    inv = ROPE_THETA ** (-jnp.arange(half, dtype=jnp.float32) / half)
    ang = pos.astype(jnp.float32)[:, None] * inv[None, :]
    cos = jnp.cos(ang)[:, None, :]
    sin = jnp.sin(ang)[:, None, :]
    xr = x[..., :ROPE_DIM].astype(jnp.float32)
    x1, x2 = xr[..., :half], xr[..., half:]
    rot = jnp.concatenate([x1 * cos - x2 * sin, x2 * cos + x1 * sin], axis=-1)
    return jnp.concatenate([rot.astype(x.dtype), x[..., ROPE_DIM:]], axis=-1)

def causal_dwconv(u_ext, w, b):
    out = lax.conv_general_dilated(u_ext, w[:, None, :].astype(u_ext.dtype), window_strides=(1,),
                                   padding='VALID', dimension_numbers=('NWC', 'WIO', 'NWC'),
                                   feature_group_count=u_ext.shape[-1])
    return out + b.astype(out.dtype)

def sink_attention(q, k, v, mask, sink):
    b, nb, lq, _, dh = q.shape
    qg = q.reshape(b, nb, lq, A_KV_HEADS, A_GROUP, dh)
    s = jnp.einsum('bnqhgd,bnkhd->bnhgqk', qg, k, preferred_element_type=jnp.float32) * (HEAD_DIM ** -0.5)
    s = jnp.where(mask[None, :, None, None], s, -jnp.inf)
    sk = sink.astype(jnp.float32).reshape(A_KV_HEADS, A_GROUP, 1, 1)
    mx = jnp.maximum(jnp.max(s, axis=-1, keepdims=True), sk)
    p = jnp.exp(s - mx)
    p = p / (jnp.sum(p, axis=-1, keepdims=True) + jnp.exp(sk - mx))
    o = jnp.einsum('bnhgqk,bnkhd->bnqhgd', p.astype(v.dtype), v)
    return o.reshape(b, nb, lq, A_HEADS, dh)

def swa_prompt(q, k, v, sink):
    b, s_len, h, dh = q.shape
    nc = s_len // CHUNK
    pad = WIN_CHUNKS * CHUNK
    kp = jnp.pad(k, ((0, 0), (pad, 0), (0, 0), (0, 0)))
    vp = jnp.pad(v, ((0, 0), (pad, 0), (0, 0), (0, 0)))
    kb = jnp.concatenate([kp[:, j * CHUNK:j * CHUNK + s_len].reshape(b, nc, CHUNK, A_KV_HEADS, dh)
                          for j in range(WIN_CHUNKS + 1)], axis=2)
    vb = jnp.concatenate([vp[:, j * CHUNK:j * CHUNK + s_len].reshape(b, nc, CHUNK, A_KV_HEADS, dh)
                          for j in range(WIN_CHUNKS + 1)], axis=2)
    n_keys = (WIN_CHUNKS + 1) * CHUNK
    cidx = jnp.arange(nc)[:, None, None]
    kblk = (jnp.arange(n_keys) // CHUNK)[None, None, :]
    mask = jnp.broadcast_to(cidx + kblk - WIN_CHUNKS >= 0, (nc, CHUNK, n_keys))
    o = sink_attention(q.reshape(b, nc, CHUNK, h, dh), kb, vb, mask, sink)
    return o.reshape(b, s_len, h, dh)

def swa_sample(q, k_all, v_all, sink):
    t = q.shape[1]
    mask = jnp.ones((1, t, k_all.shape[1]), dtype=bool)
    return sink_attention(q[:, None], k_all[:, None], v_all[:, None], mask, sink)[:, 0]

def even_mixer(hn, pos, conv_hist, kv_hist, w_in, sink, cw, cb, lng, lnb, w_out):
    bsz, t, _ = hn.shape
    z = hn @ w_in
    q = partial_rope(z[..., :A_Q].reshape(bsz, t, A_HEADS, HEAD_DIM), pos)
    k = partial_rope(z[..., A_Q:A_Q + A_KV].reshape(bsz, t, A_KV_HEADS, HEAD_DIM), pos)
    v = z[..., A_Q + A_KV:A_Q + 2 * A_KV].reshape(bsz, t, A_KV_HEADS, HEAD_DIM)
    glu_a, glu_g = jnp.split(z[..., A_Q + 2 * A_KV:], 2, axis=-1)
    u = glu_a * jax.nn.sigmoid(glu_g)
    if kv_hist is None:
        o = swa_prompt(q, k, v, sink)
        k_all, v_all = k, v
    else:
        k_all = jnp.concatenate([kv_hist[0].astype(k.dtype), k], axis=1)
        v_all = jnp.concatenate([kv_hist[1].astype(v.dtype), v], axis=1)
        o = swa_sample(q, k_all, v_all, sink)
    u_ext = jnp.concatenate([conv_hist.astype(u.dtype), u], axis=1)
    c = jax.nn.silu(layernorm(causal_dwconv(u_ext, cw, cb), lng, lnb))
    y = jnp.concatenate([o.reshape(bsz, t, A_Q), c], axis=-1) @ w_out
    return y, k_all[:, -WINDOW:], v_all[:, -WINDOW:], u_ext[:, -(CONV_W - 1):]

def mlstm_chunk(carry, inp):
    c_st, n_st, m_st = carry
    q, k, v, ig, lf = inp
    length = q.shape[1]
    b = jnp.cumsum(lf, axis=1)
    a = b + m_st[:, None, :]
    dmat = b[:, :, None, :] - b[:, None, :, :] + ig[:, None, :, :]
    causal = jnp.tril(jnp.ones((length, length), dtype=bool))
    dmat = jnp.where(causal[None, :, :, None], dmat, -jnp.inf)
    m_t = jnp.maximum(a, jnp.max(dmat, axis=2))
    w_inter = jnp.exp(a - m_t)
    s = jnp.einsum('bthd,bshd->btsh', q, k) * jnp.exp(dmat - m_t[:, :, None, :])
    num = jnp.einsum('btsh,bshe->bthe', s, v) + w_inter[..., None] * jnp.einsum('bhed,bthd->bthe', c_st, q)
    den = jnp.sum(s, axis=2) + w_inter * jnp.einsum('bhd,bthd->bth', n_st, q)
    h = num / jnp.maximum(jnp.abs(den), jnp.exp(-m_t))[..., None]
    b_end = b[:, -1]
    dec = b_end[:, None, :] - b + ig
    m_new = jnp.maximum(b_end + m_st, jnp.max(dec, axis=1))
    w_s = jnp.exp(dec - m_new[:, None, :])
    w_c = jnp.exp(b_end + m_st - m_new)
    c_new = w_c[..., None, None] * c_st + jnp.einsum('bsh,bshe,bshd->bhed', w_s, v, k)
    n_new = w_c[..., None] * n_st + jnp.einsum('bsh,bshd->bhd', w_s, k)
    return (c_new, n_new, m_new), h

def mlstm_mixer(hn, qk_hist, c0, n0, m0, chunked, w_in, qkc_w, qkc_b, b_i, b_f, norm_g, w_out):
    bsz, t, _ = hn.shape
    z = hn @ w_in
    qk_ext = jnp.concatenate([qk_hist.astype(z.dtype), z[..., :2 * M_WIDTH]], axis=1)
    qk = jax.nn.silu(causal_dwconv(qk_ext, qkc_w, qkc_b)).astype(jnp.float32)
    q = qk[..., :M_WIDTH].reshape(bsz, t, M_HEADS, M_DIM)
    k = qk[..., M_WIDTH:].reshape(bsz, t, M_HEADS, M_DIM) * (M_DIM ** -0.5)
    v = z[..., 2 * M_WIDTH:3 * M_WIDTH].astype(jnp.float32).reshape(bsz, t, M_HEADS, M_DIM)
    o_gate = jax.nn.sigmoid(z[..., 3 * M_WIDTH:4 * M_WIDTH].astype(jnp.float32))
    gates = z[..., 4 * M_WIDTH:].astype(jnp.float32)
    ig = gates[..., :M_HEADS] + b_i.astype(jnp.float32)
    lf = jax.nn.log_sigmoid(gates[..., M_HEADS:] + b_f.astype(jnp.float32))
    carry = (c0.astype(jnp.float32), n0.astype(jnp.float32), m0.astype(jnp.float32))
    if chunked:
        nc = t // CHUNK

        def to_chunks(a):
            return jnp.swapaxes(a.reshape((bsz, nc, CHUNK) + a.shape[2:]), 0, 1)

        carry, h = lax.scan(mlstm_chunk, carry, (to_chunks(q), to_chunks(k), to_chunks(v), to_chunks(ig), to_chunks(lf)))
        h = jnp.swapaxes(h, 0, 1).reshape(bsz, t, M_HEADS, M_DIM)
    else:
        carry, h = mlstm_chunk(carry, (q, k, v, ig, lf))
    h = h * lax.rsqrt(jnp.mean(h * h, axis=-1, keepdims=True) + EPS) * norm_g.astype(jnp.float32).reshape(M_HEADS, M_DIM)
    y = (h.reshape(bsz, t, M_WIDTH) * o_gate).astype(hn.dtype) @ w_out
    return y, qk_ext[:, -(QK_CONV_W - 1):], carry[0], carry[1], carry[2]

def sq_relu_ffn(x, g, w1, w2):
    h = jax.nn.relu(rmsnorm(x, g) @ w1)
    return (h * h) @ w2

def setup_inputs(seed: int = 0) -> dict:
    key = jax.random.key(seed)
    ks = jax.random.split(key, 32)

    def nrm(k, shape, scale):
        return jax.random.normal(k, shape, jnp.float32) * scale

    swa_rows = min(WINDOW, PAST_LEN)
    return {
        'x_prompt': nrm(ks[0], (BATCH, SEQ, D_MODEL), 1.0),
        'x_sample': nrm(ks[1], (DEC_BATCH, DEC_SEQ, D_MODEL), 1.0),
        'cache_swa_k': nrm(ks[2], (N_EVEN, DEC_BATCH, swa_rows, A_KV_HEADS, HEAD_DIM), 1.0),
        'cache_swa_v': nrm(ks[3], (N_EVEN, DEC_BATCH, swa_rows, A_KV_HEADS, HEAD_DIM), 1.0),
        'state_conv': nrm(ks[4], (N_EVEN, DEC_BATCH, CONV_W - 1, CONV_CH), 0.5),
        'state_qk_conv': nrm(ks[5], (N_ODD, DEC_BATCH, QK_CONV_W - 1, 2 * M_WIDTH), 1.0),
        'state_mlstm_C': nrm(ks[6], (N_ODD, DEC_BATCH, M_HEADS, M_DIM, M_DIM), 0.05),
        'state_mlstm_n': nrm(ks[7], (N_ODD, DEC_BATCH, M_HEADS, M_DIM), 0.5),
        'state_mlstm_m': nrm(ks[8], (N_ODD, DEC_BATCH, M_HEADS), 0.5),
        'norm_mix_g': 1.0 + nrm(ks[9], (DEPTH, D_MODEL), 0.02),
        'norm_ffn_g': 1.0 + nrm(ks[10], (DEPTH, D_MODEL), 0.02),
        'norm_out_g': 1.0 + nrm(ks[11], (D_MODEL,), 0.02),
        'w_in_even': nrm(ks[12], (N_EVEN, D_MODEL, EVEN_IN), D_MODEL ** -0.5),
        'attn_sink': nrm(ks[13], (N_EVEN, A_HEADS), 0.5),
        'conv_w': nrm(ks[14], (N_EVEN, CONV_W, CONV_CH), CONV_W ** -0.5),
        'conv_b': nrm(ks[15], (N_EVEN, CONV_CH), 0.02),
        'conv_ln_g': 1.0 + nrm(ks[16], (N_EVEN, CONV_CH), 0.02),
        'conv_ln_b': nrm(ks[17], (N_EVEN, CONV_CH), 0.02),
        'w_out_even': nrm(ks[18], (N_EVEN, EVEN_MIX, D_MODEL), EVEN_MIX ** -0.5),
        'w_in_odd': nrm(ks[19], (N_ODD, D_MODEL, ODD_IN), D_MODEL ** -0.5),
        'qk_conv_w': nrm(ks[20], (N_ODD, QK_CONV_W, 2 * M_WIDTH), QK_CONV_W ** -0.5),
        'qk_conv_b': nrm(ks[21], (N_ODD, 2 * M_WIDTH), 0.02),
        'gate_b_i': nrm(ks[22], (N_ODD, M_HEADS), 0.1),
        'gate_b_f': 3.0 + nrm(ks[23], (N_ODD, M_HEADS), 0.5),
        'mlstm_norm_g': 1.0 + nrm(ks[24], (N_ODD, M_WIDTH), 0.02),
        'w_out_odd': nrm(ks[25], (N_ODD, M_WIDTH, D_MODEL), M_WIDTH ** -0.5),
        'w_ff1': nrm(ks[26], (DEPTH, D_MODEL, D_FF), D_MODEL ** -0.5),
        'w_ff2': nrm(ks[27], (DEPTH, D_FF, D_MODEL), 0.5 * D_FF ** -0.5),
    }

def reference(x_prompt, x_sample, cache_swa_k, cache_swa_v, state_conv, state_qk_conv, state_mlstm_C,
              state_mlstm_n, state_mlstm_m, norm_mix_g, norm_ffn_g, norm_out_g, w_in_even, attn_sink, conv_w,
              conv_b, conv_ln_g, conv_ln_b, w_out_even, w_in_odd, qk_conv_w, qk_conv_b, gate_b_i, gate_b_f,
              mlstm_norm_g, w_out_odd, w_ff1, w_ff2):
    bp, s_len, _ = x_prompt.shape
    bs, t_len, _ = x_sample.shape
    pos_p = jnp.arange(s_len, dtype=jnp.int32)
    pos_s = PAST_LEN + jnp.arange(t_len, dtype=jnp.int32)
    xp, xs = x_prompt, x_sample
    kp_l, vp_l, cvp_l, qkp_l, cp_l, np_l, mp_l = [], [], [], [], [], [], []
    ks_l, vs_l, cvs_l, qks_l, cs_l, ns_l, ms_l = [], [], [], [], [], [], []
    for l in range(DEPTH):
        if l % 2 == 0:
            i = l // 2
            prm = (w_in_even[i], attn_sink[i], conv_w[i], conv_b[i], conv_ln_g[i], conv_ln_b[i], w_out_even[i])
            yp, kp, vp, cvp = even_mixer(rmsnorm(xp, norm_mix_g[l]), pos_p,
                                         jnp.zeros((bp, CONV_W - 1, CONV_CH), xp.dtype), None, *prm)
            ys, ks_, vs_, cvs = even_mixer(rmsnorm(xs, norm_mix_g[l]), pos_s, state_conv[i],
                                           (cache_swa_k[i], cache_swa_v[i]), *prm)
            kp_l.append(kp); vp_l.append(vp); cvp_l.append(cvp)
            ks_l.append(ks_); vs_l.append(vs_); cvs_l.append(cvs)
        else:
            j = l // 2
            prm = (w_in_odd[j], qk_conv_w[j], qk_conv_b[j], gate_b_i[j], gate_b_f[j], mlstm_norm_g[j], w_out_odd[j])
            yp, qkp, cpn, npn, mpn = mlstm_mixer(rmsnorm(xp, norm_mix_g[l]),
                                                 jnp.zeros((bp, QK_CONV_W - 1, 2 * M_WIDTH), xp.dtype),
                                                 jnp.zeros((bp, M_HEADS, M_DIM, M_DIM), jnp.float32),
                                                 jnp.zeros((bp, M_HEADS, M_DIM), jnp.float32),
                                                 jnp.zeros((bp, M_HEADS), jnp.float32), True, *prm)
            ys, qks, csn, nsn, msn = mlstm_mixer(rmsnorm(xs, norm_mix_g[l]), state_qk_conv[j], state_mlstm_C[j],
                                                 state_mlstm_n[j], state_mlstm_m[j], False, *prm)
            qkp_l.append(qkp); cp_l.append(cpn); np_l.append(npn); mp_l.append(mpn)
            qks_l.append(qks); cs_l.append(csn); ns_l.append(nsn); ms_l.append(msn)
        xp = xp + yp
        xs = xs + ys
        xp = xp + sq_relu_ffn(xp, norm_ffn_g[l], w_ff1[l], w_ff2[l])
        xs = xs + sq_relu_ffn(xs, norm_ffn_g[l], w_ff1[l], w_ff2[l])
    y_prompt = rmsnorm(xp, norm_out_g)
    y_sample = rmsnorm(xs, norm_out_g)
    return (y_prompt, y_sample,
            jnp.stack(kp_l), jnp.stack(vp_l), jnp.stack(cvp_l), jnp.stack(qkp_l),
            jnp.stack(cp_l), jnp.stack(np_l), jnp.stack(mp_l),
            jnp.stack(ks_l), jnp.stack(vs_l), jnp.stack(cvs_l), jnp.stack(qks_l),
            jnp.stack(cs_l), jnp.stack(ns_l), jnp.stack(ms_l))


_drawn_inputs = setup_inputs


def setup_inputs(seed=0):
    import zlib

    import numpy as np

    out = dict(_drawn_inputs(seed))
    spreads = {}
    factors = {'norm_ffn_g': 2.893,
     'norm_out_g': 8.011,
     'attn_sink': 35.15,
     'conv_ln_g': 3.264,
     'conv_ln_b': 3.268,
     'mlstm_norm_g': 32.839}
    for name, (base, spread) in spreads.items():
        noise = np.random.default_rng([zlib.crc32(name.encode()), seed]).standard_normal(out[name].shape)
        drawn = base * np.exp(spread * noise) if base else spread * noise
        out[name] = jnp.asarray(drawn.astype(out[name].dtype))
    for name, factor in factors.items():
        out[name] = (out[name] * factor).astype(out[name].dtype)
    return out
```

```python
import concourse.bass as bass
from concourse import mybir
from contextlib import ExitStack

F32 = mybir.dt.float32
F32R = mybir.dt.float32r
ALU = mybir.AluOpType
ACT = mybir.ActivationFunctionType
AX = mybir.AxisListType.X

P = 128
D = 1024
KT = D // P
TP = 1024
NB, TB = 8, 16
T = TP + NB * TB
NT = 3
TN = T // NT
EPS = 1e-6
NEG = -1e30

CH = 64
NCH = TP // CH
HD = 64
WIN = 128
SK = WIN + TB
ATT_SCALE = HD ** -0.5
CW = 31
HIST = CW - 1
CT = 4
EXT = HIST + TP + NB * (HIST + TB)
MH = 4
MD = 256
MA = MD + 1
LC = 128
NLC = TP // LC
QW = 4
QH = QW - 1
QEXT = QH + TP + NB * (QH + TB)
FC = 8
FK = 4

U_IN0, U_OUT0, U_FF0 = 0, 14, 22
U_GATE = U_FF0 + FC * 8
U_HEAD = U_GATE + 1
U_OUT1 = U_HEAD + MH * 8
U_FF1 = U_OUT1 + 8
N_UNITS = U_FF1 + FC * 8
B_IN0, B_OUT0, B_FF0 = 0, 14, 22
B_GATE = B_FF0 + FC * 12
B_HEAD = B_GATE + 1
B_OUT1 = B_HEAD + MH * 8
B_FF1 = B_OUT1 + 8
B_END = B_FF1 + FC * 12
FF_BLOCKS = [1, 2, 3, 4, 6, 8, 10, 12]

C_G = 0
C_CW = C_G + 5 * KT
C_CB = C_CW + CT * CW
C_LG = C_CB + CT
C_LB = C_LG + CT
C_SINK = C_LB + CT
C_SINKS = C_SINK + 4
C_GB = C_SINKS + 1
C_BSEL = C_GB + 1
C_M0 = C_BSEL + NB
C_POW = C_M0 + NB
C_MH = C_POW + 2
NCOL = C_MH + MH * 16
K_ID, K_ONE, K_PERM, K_CAUS, K_BLK = range(5)
NK = 5
H_W, H_B, H_G, H_SEL = 0, 16, 20, 22
NH = H_SEL + P
NCS = 3
CS_USES = [len(range(s, NB, NCS)) for s in range(NCS)]
ONE = 1
NSINK = 2
GATE_TO_EXP, GATE_ROWS = 20, 21


def build(nc, t):
    es = ExitStack()
    with es:
        def sb(name, shape, dt=F32):
            return es.enter_context(nc.sbuf_tensor(name, shape, dt))

        def sem(name):
            return es.enter_context(nc.semaphore(name))

        cols = sb("cols", [P, NCOL])
        mats = sb("mats", [P, NK, P])
        head_par = sb("head_par", [P, NH])
        w_raw = sb("w_raw", [P, 2, D])
        w_hi = sb("w_hi", [P, 2, D], F32R)
        w_lo = sb("w_lo", [P, 2, D], F32R)
        a_hi = sb("a_hi", [P, KT, T], F32R)
        a_lo = sb("a_lo", [P, KT, T], F32R)
        low = sb("low", [P, KT * T])
        rbc = sb("rbc", [P, T])
        mid = sb("mid", [P, 6784])
        with nc.sbuf_tensor("h_hi", [P, FK, T], F32R) as h_hi, nc.sbuf_tensor("h_lo", [P, FK, T], F32R) as h_lo:
            pass
        high = sb("high", [P, 2 * FK * T])
        psum = es.enter_context(nc.psum_tensor("psum", [P, 8, 512], F32))

        ident = mats[:, K_ID, :]
        ones = mats[:, K_ONE, :]
        x = low[:, :].rearrange("p (k t) -> p k t", k=KT)

        def carve(buf):
            at = [0]

            def take(*shape):
                n = 1
                for s in shape:
                    n *= s
                v = buf[:, at[0]:at[0] + n]
                at[0] += n
                if len(shape) == 2:
                    v = v.rearrange("p (a b) -> p a b", a=shape[0])
                if len(shape) == 3:
                    v = v.rearrange("p (a b c) -> p a b c", a=shape[0], b=shape[1])
                return v
            return take

        take = carve(mid)
        ssq = take(T)
        sq = take(T)
        hid = take(T)
        take = carve(low)
        ext = take(CT + 1, EXT)
        vT = take(T)
        take = carve(high)
        qT = take(4, T)
        kT = take(T)
        v64 = take(NCH, P)
        kc = take(NB, SK)
        take = carve(mid)
        cos, sin, za, zs = take(T), take(T), take(T), take(T)
        vc = take(NB, P)
        v16 = take(NB, P)
        take = carve(mid)
        qs = take(2, 4, CH)
        qss = carve(mid)(NB, 4 * TB)
        pr = take(2, 2 * 192)
        pT = take(2, 6 * P)
        ob = take(2, P)
        obs = take(2, P)
        nsink = take(5)
        st = take(2, 16)
        lnsq = carve(mid)(CT, TN)
        take = carve(low)
        mq, mk, mo, mv = take(2, T), take(2, T), take(2, T), take(2, T)
        take = carve(high)
        vaug = take(NLC + 1, MA)
        qext = take(2, QEXT)
        qx = take(2, NB, P)
        cst = take(2, MA)
        csl = take(NCS, 2 * MA)
        take = carve(high)
        gz, gt, glf, gb, gg, gd, gm, gp = [take(T) for _ in range(8)]
        take = carve(mid)
        mix = take(2, T)
        mneg = take(T)
        rows = mix[:, 0, :]
        ge = mix[:, 1, :]
        eM = take(2, P)
        sT = take(2, P)
        tB = take(2, MA + 1)
        num = take(2, MA + 1)
        kw = take(2, MD)
        hn = take(2, MD)
        rtc = take(NLC + 1, 4, MH)
        rth = take(NLC + 1, 4)
        wc16 = take(16)
        wcb = take(MH, 16)
        wch = take(16)
        mend = take(16)
        ws8 = take(NB)
        sm = take(2, 8)
        wd = take(MH * 16)
        junk = take(MD)
        mixed_h = high[:, :].rearrange("p (k t) -> p k t", k=KT)
        Q_INT, Q_WS, Q_G, Q_EM = range(4)

        cols_in, mats_in, cs_tab_in, cache_in, hist_in = [sem(n) for n in (
            "cols_in", "mats_in", "cos_sin_in", "cache_in", "hist_in")]
        x_in = [sem(f"x_in{k}") for k in range(KT)]
        w_in = [sem(f"w_in{s}") for s in range(2)]
        w_taken, w_high, w_split = sem("w_taken"), sem("w_high"), sem("w_split")
        block_done, evicted = sem("block_done"), sem("evicted")
        sq_done, ssq_copy, ssq_done = sem("sq_done"), sem("ssq_copy"), sem("ssq_done")
        aux_done, aux_read, rsum_done, rbc_done = [sem(n) for n in ("aux_done", "aux_read", "rsum_done", "rbc_done")]
        hi_done, lo_done, hsq_done, h_done = [sem(n) for n in ("hi_done", "lo_done", "hsq_done", "h_done")]
        pads, sig_done, ext_done, conv_done, rope_done, v_in_place, kc_done, kv_out = [sem(n) for n in (
            "pads", "sig_done", "ext_done", "conv_done", "rope_done", "v_in_place", "kc_done", "kv_out")]
        conv_out = [sem(f"conv_state_out{j}") for j in range(CT)]
        ln_centred, ln_sq, ln_v, ln_rstd, ln_scaled, ln_y, ln_hi, ln_lo = [sem("ln_" + n) for n in (
            "centred", "sq", "var", "rstd", "scaled", "y", "hi", "lo")]
        q_staged, s_done, stat_done, m_done, p_done, t_done, pt_done, pe_step, pv_done, den_done, o_done, ot_done, \
            ahi_done, mixed = [sem("att_" + n) for n in (
                "staged", "scores", "stat", "max", "probs", "tr", "tr_copied", "step", "pv", "den", "out", "out_tr",
                "hi", "mixed")]
        spilled, gates_act, gate_rows, g_out = sem("spilled"), sem("gates_act"), sem("gate_rows"), sem("gate_out")
        par_in, head_set, qconv, qsilu, osig, vtr, vcp = [sem("m_" + n) for n in (
            "par_in", "head_set", "conv", "silu", "ogate", "vtr", "vcopied")]
        qh_in = [sem(f"m_hist_in{i}") for i in range(4)]
        qh_out = [sem(f"m_hist_out{i}") for i in range(4)]
        es_done, e_done, st_done, ktr, kw_done, ab_done, tb_done, num_done, c_done, cu_done, dn_done, ss_done, \
            sc_own, sc_done, hn_done, ht_done, mix_done = [sem("m_" + n) for n in (
                "scores", "decay", "gated", "ktr", "kw", "numer", "inter_scaled", "num", "delta", "state", "den",
                "ss", "pow", "scale", "hn", "hT", "mix")]
        cs_in = [sem(f"m_cs_in{s}") for s in range(NCS)]
        cs_out = [sem(f"m_cs_out{s}") for s in range(NCS)]
        qx_done, kwm_done, csc_done, csu_done, cp_out, mix_out, mix_in = [sem("m_" + n) for n in (
            "qx", "kwm", "sample_delta", "sample_state", "prompt_out", "mix_out", "mix_in")]
        gact_own = sem("gates_act_own")
        mix_back = [sem(f"mix_back{h}") for h in range(MH)]
        y_done, y_out = sem("y_done"), sem("y_out")

        block = es.enter_context(nc.Block())

        AX_R0, AX_KROPE, AX_V, AX_QROPE = 0, 3, 6, 12
        AX_LN = AX_QROPE + 4 * NT
        AX_R1 = AX_LN + 2 * NT
        AX_R2 = AX_R1 + NT
        AX_GT = AX_R2 + NT
        AX_WC = AX_GT + 3
        AX_R3 = AX_WC + 1
        AX_R4 = AX_R3 + NT

        def out3(b):
            s = 3 * (b % 2)
            return psum[:, s:s + 3, 0:TN]

        def by3(v):
            return v.rearrange("p (a b) -> p a b", a=NT)

        def gain(m, k):
            return cols[:, C_G + KT * m + k:C_G + KT * m + k + 1]

        def tok(i):
            return slice(i * TN, (i + 1) * TN)

        def sample(v, pre, width):
            return v.rearrange("p (b w) -> p b w", w=width)[:, :, pre:pre + TB]

        @block.sync
        def _(sp):
            def load(u, s, split):
                if split is not None:
                    sp.wait_ge(w_split, split)
                sp.dma_start(w_raw[:, s, :], t["wall"][u]).then_inc(w_in[s], 16)

            load(0, 0, None)
            load(1, 1, None)
            with sp.Fori(1, N_UNITS // 2) as i:
                for s in range(2):
                    load(2 * i + s, s, 2 * i + (s - 1))
            load(N_UNITS - 1, 0, N_UNITS - 2)

        @block.gpsimd
        def _(pool):
            def split(s, loads, units, used):
                pool.wait_ge(w_in[s], loads * 16)
                if used is not None:
                    pool.wait_ge(block_done, used)
                pool.sem_inc(w_taken, 1)
                nc.gpsimd.tensor_scalar(w_hi[:, s, :], w_raw[:, s, :], 1.0, 1.0, ALU.mult, ALU.mult)\
                    .then_inc(w_high, 1)
                pool.wait_ge(w_high, units)
                nc.gpsimd.tensor_tensor(w_lo[:, s, :], w_raw[:, s, :], w_hi[:, s, :].bitcast(F32), ALU.subtract)\
                    .then_inc(w_split, 1)

            def single(u, used):
                split(u % 2, u // 2 + 1, u + 1, used)

            def ff(u0, b0):
                before = [-1, 0] + FF_BLOCKS[:6]
                with pool.Fori(0, FC) as c:
                    for j in range(8):
                        u = u0 + j
                        split(u % 2, 4 * c + (u // 2 + 1), 8 * c + (u + 1), 12 * c + (b0 + before[j]))

            single(0, None)
            single(1, None)
            with pool.Fori(1, U_FF0 // 2) as i:
                for s in range(2):
                    split(s, i + 1, 2 * i + (s + 1), 2 * i + (s - 1))
            ff(U_FF0, B_FF0)
            single(U_GATE, B_GATE - 2)
            single(U_HEAD, B_GATE)
            single(U_HEAD + 1, B_GATE + 1)
            pool.wait_ge(cols_in, 16)
            with pool.Fori(0, MH) as h:
                def head_unit(j):
                    u = U_HEAD + j
                    split(u % 2, 4 * h + (u // 2 + 1), 8 * h + (u + 1), 8 * h + (B_HEAD + j - 1))

                for j in range(2, 8):
                    head_unit(j)
                for c in range(NLC + 1):
                    s = c % 2
                    pool.wait_ge(ss_done, 9 * h + (c + 1))
                    nc.gpsimd.tensor_tensor(sm[:, s, 4:5], sm[:, s, 3:4], cols[:, C_POW:C_POW + 1], ALU.add)\
                        .then_inc(sc_own, 1)
                    pool.wait_ge(sc_own, 18 * h + (2 * c + 1))
                    nc.gpsimd.tensor_tensor(sm[:, s, 5:6], sm[:, s, 4:5], cols[:, C_POW + 1:C_POW + 2], ALU.pow)\
                        .then_inc(sc_own, 1)
                    pool.wait_ge(sc_own, 18 * h + (2 * c + 2))
                    nc.gpsimd.tensor_tensor(sm[:, s, 6:7], sm[:, s, 5:6], sm[:, s, 2:3], ALU.mult)\
                        .then_inc(sc_done, 1)
                    if c in (4, 5):
                        head_unit(c + 4)
            with pool.Fori(0, 3) as i:
                for s in range(2):
                    u = U_OUT1 + 2 + s
                    split(u % 2, i + (u // 2 + 1), 2 * i + (u + 1), 2 * i + (B_OUT1 + s + 1))
            ff(U_FF1, B_FF1)

        @block.tensor
        def _(pe):
            mm = nc.tensor.matmul
            tr = nc.tensor.transpose

            def passes(s, k, kk, b, hi, lo, first, last):
                z = 3 * (b % 2)
                n = 0
                for w, a in ((w_hi, hi), (w_hi, lo), (w_lo, hi)):
                    for i in range(NT):
                        r = mm(psum[:, z + i, 0:TN], w[:, s, k * P:(k + 1) * P], a[:, kk, tok(i)],
                               start=first and n == 0, stop=last and n == 2)
                    n += 1
                return r

            def unit(s, units, b, free, ready=None):
                pe.wait_ge(w_split, units)
                if free is not None:
                    pe.wait_ge(evicted, free)
                for k in range(KT):
                    if ready is not None:
                        ready(k)
                    r = passes(s, k, k, b, a_hi, a_lo, k == 0, k == KT - 1)
                r.then_inc(block_done, 1)

            def aux(n, cells, done=True):
                if n >= 2:
                    pe.wait_ge(aux_read, n - 1)
                bank = 6 + n % 2
                for c in cells:
                    if len(c) == 3:
                        lo_, hi_, (a, b_, st_, sp_) = c
                        r = mm(psum[:, bank, lo_:hi_], a, b_, start=st_, stop=sp_)
                    else:
                        rows_, lo_, hi_, a = c
                        r = tr(psum[0:rows_, bank, lo_:hi_], a, ident)
                r.then_inc(aux_done, 1)

            def token_sums(n, m):
                pe.wait_ge(ssq_done, KT * (m + 1))
                for i in range(NT):
                    aux(n + i, [(0, TN, (ones, ssq[:, tok(i)], True, True))])

            def split_ready(base):
                def ready(k):
                    pe.wait_ge(lo_done, base + k + 1)
                return ready

            def ff(u0, b0, base):
                with pe.Fori(0, FC) as c:
                    for j in range(FK):
                        u, b = u0 + j, b0 + j
                        unit(u % 2, 8 * c + (u + 1), b, 12 * c + (b - 1), split_ready(base) if j == 0 else None)
                    for j in range(4):
                        u = u0 + FK + j
                        pe.wait_ge(w_split, 8 * c + (u + 1))
                        for o in range(2):
                            b = b0 + FK + 2 * j + o
                            pe.wait_ge(evicted, 12 * c + (b - 1))
                            for k in range(FK):
                                if j == 0 and o == 0:
                                    pe.wait_ge(h_done, FK * c + (FK * FC * (b0 > B_GATE) + k + 1 + ONE))
                                r = passes(u % 2, FK * o + k, k, b, h_hi, h_lo, k == 0, k == FK - 1)
                            r.then_inc(block_done, 1)

            pe.wait_ge(mats_in, 16)
            unit(0, 1, 0, None, split_ready(0))
            token_sums(AX_R0, 0)
            unit(1, 2, 1, None)
            with pe.Fori(1, 5) as i:
                for s in range(2):
                    unit(s, 2 * i + (s + 1), s, 2 * i + (s - 1))

            def rope(n, b, src):
                pe.wait_ge(evicted, b + 1)
                for i in range(NT):
                    aux(n + i, [(0, TN, (mats[:, K_PERM, :], src[:, tok(i)], True, True))])

            unit(0, 11, 10, 9)
            rope(AX_KROPE, 8, kT)
            pe.wait_ge(evicted, 10)
            for g in range(4):
                aux(AX_V + g, [(CH, P * i, P * i + P, vT[:, CH * (4 * g + i):CH * (4 * g + i + 1)]) for i in range(4)])
            for g in range(2):
                aux(AX_V + 4 + g, [(TB, P * i, P * i + P, vT[:, TP + TB * (4 * g + i):TP + TB * (4 * g + i + 1)])
                                   for i in range(4)])
            for j in range(1, 4):
                unit((10 + j) % 2, 11 + j, 10 + j, 9 + j)
                rope(AX_QROPE + NT * (j - 1), 9 + j, qT[:, j - 1, :])
            rope(AX_QROPE + NT * 3, 13, qT[:, 3, :])

            pe.wait_ge(conv_done, CT * 2 * CW)
            for i in range(NT):
                aux(AX_LN + i, [(0, TN, (ones, ext[:, j, tok(i)], j == 0, j == CT - 1)) for j in range(CT)])
            for i in range(NT):
                pe.wait_ge(ln_sq, i + 1)
                aux(AX_LN + NT + i, [(0, TN, (ones, lnsq[:, j, :], j == 0, j == CT - 1)) for j in range(CT)])

            def blocks_of(c):
                return c + 1 if isinstance(c, int) and c < 2 else 3

            def scores(c, p):
                if p == 0:
                    pe.wait_ge(q_staged, c + 1)
                if not (isinstance(c, int) and c == 0):
                    pe.wait_ge(p_done, 2 * c + p - 1)
                nb = blocks_of(c)
                for v in range(2):
                    r = mm(psum[:, p, 192 * v:192 * v + CH * nb], qs[:, v, 2 * p:2 * p + 2, :],
                           kT[:, bass.ds(CH * c - CH * (nb - 1), CH * nb)], start=True, stop=True)
                r.then_inc(s_done, 1)

            def flip(c, p):
                pe.wait_ge(p_done, 2 * c + p + 1)
                if not (isinstance(c, int) and c == 0):
                    pe.wait_ge(pt_done, 2 * c + p - 1)
                pe.sem_inc(pe_step, 1)
                nb = blocks_of(c)
                for v in range(2):
                    for i in range(nb):
                        e = 3 * v + i
                        r = tr(psum[0:CH, 2 + 2 * p + e // 4, P * (e % 4):P * (e % 4) + P],
                               pr[:, p, 192 * v + CH * i:192 * v + CH * (i + 1)], ident)
                r.then_inc(t_done, 1)

            def weigh(c, p):
                pe.wait_ge(pt_done, 2 * c + p + 1)
                if not (isinstance(c, int) and c == 0):
                    pe.wait_ge(mixed, 2 * c + p - 1)
                pe.sem_inc(pe_step, 1)
                nb = blocks_of(c)
                for v in range(2):
                    for i in range(nb):
                        e = 3 * v + i
                        r = mm(psum[:, 6 + p, HD * v:HD * v + HD], pT[0:CH, p, P * e:P * e + P],
                               v64[0:CH, c - (nb - 1) + i, HD * v:HD * v + HD], start=i == 0, stop=i == nb - 1)
                r.then_inc(pv_done, 1)

            def flip_out(n, p, src):
                pe.wait_ge(o_done, n + 1)
                tr(psum[:, 6 + p, P:2 * P], src[:, p, :], ident).then_inc(ot_done, 1)

            def step(c, first=False):
                scores(c, 0)
                scores(c, 1)
                if not first:
                    weigh(c - 1, 0)
                    weigh(c - 1, 1)
                flip(c, 0)
                if not first:
                    flip_out(2 * c - 2, 0, ob)
                flip(c, 1)
                if not first:
                    flip_out(2 * c - 1, 1, ob)

            pe.wait_ge(evicted, B_OUT0)
            pe.wait_ge(aux_read, AX_R1)
            step(0, True)
            step(1)
            step(2)
            with pe.Fori(3, NCH) as c:
                step(c)
            for p in range(2):
                weigh(NCH - 1, p)
            for p in range(2):
                flip_out(2 * NCH - 2 + p, p, ob)

            pe.wait_ge(cache_in, 32)
            pe.wait_ge(kc_done, 1)
            pe.wait_ge(q_staged, NCH + 1)

            def s_scores(b, s, n):
                pe.wait_ge(p_done, n - 1)
                for v in range(2):
                    h_ = slice(HD * v, HD * v + HD)
                    r = mm(psum[h_, s, 0:SK], qss[h_, b, :], kc[h_, b, :],
                           start=True, stop=True)
                r.then_inc(s_done, 1)

            def s_flip(b, s, n):
                pe.wait_ge(p_done, n + 1)
                pe.wait_ge(pt_done, n - 1)
                tr(psum[:, 2 + 2 * s, 0:P], pr[:, s, 0:P], ident)
                tr(psum[0:TB, 2 + 2 * s, P:2 * P], pr[:, s, P:SK], ident).then_inc(t_done, 1)

            def s_weigh(b, s, n):
                pe.wait_ge(pt_done, n + 1)
                pe.wait_ge(mixed, n - 1)
                for v in range(2):
                    h_ = slice(HD * v, HD * v + HD)
                    mm(psum[h_, 6 + s, 0:HD], pT[:, s, h_], vc[:, b, h_], start=True, stop=False)
                    r = mm(psum[h_, 6 + s, 0:HD], pT[0:TB, s, P + HD * v:P + HD * v + HD], v16[0:TB, b, h_],
                           start=False, stop=True)
                r.then_inc(pv_done, 1)

            for b in range(NB + 1):
                n, s = 2 * NCH + b, b % 2
                if b < NB:
                    s_scores(b, s, n)
                if b > 0:
                    s_weigh(b - 1, 1 - s, n - 1)
                if b < NB:
                    s_flip(b, s, n)
                if b > 0:
                    flip_out(n - 1, 1 - s, obs)

            pe.wait_ge(mixed, 2 * NCH + NB)
            pe.wait_ge(ln_lo, NT)
            with pe.Fori(0, 4) as i:
                for s in range(2):
                    unit(s, 2 * i + (U_OUT0 + s + 1), s, 2 * i + (B_OUT0 + s - 1))
            token_sums(AX_R1, 1)
            ff(U_FF0, B_FF0, KT)

            token_sums(AX_R2, 2)
            unit(0, U_GATE + 1, B_GATE, B_GATE - 1, split_ready(2 * KT))
            pe.wait_ge(gates_act, 4)
            for g in range(3):
                aux(AX_GT + g, [(P, P * i, P * i + P, rows[:, P * (4 * g + i):P * (4 * g + i + 1)])
                                for i in range(min(4, NLC + 1 - 4 * g))])
            pe.wait_ge(gate_rows, GATE_ROWS)
            aux(AX_WC, [(0, MH * 16, (ones[0:MH, :], wd[0:MH, :], True, True))])
            pe.wait_ge(aux_read, AX_R3)

            with pe.Fori(0, MH) as h:
                for j in range(8):
                    u, b = U_HEAD + j, B_HEAD + j
                    if j == 0:
                        pe.wait_ge(mix_done, 9 * h + ONE)
                        pe.wait_ge(csu_done, 8 * h + ONE)
                    unit(u % 2, 8 * h + (u + 1), b, 8 * h + (b - 1))
                for c in range(NLC + 1):
                    if c >= 2:
                        pe.wait_ge(vcp, 9 * h + (c - 1))
                    for j in range(2):
                        r = tr(psum[:, 6 + c % 2, P * j:P * j + P], mv[:, j, LC * c:LC * (c + 1)], ident)
                    r.then_inc(vtr, 1)
                pe.wait_ge(evicted, 8 * h + (B_HEAD + 8))
                pe.wait_ge(vcp, 9 * h + 9)
                pe.wait_ge(qsilu, 4 * h + 4)
                pe.wait_ge(par_in, 16 * h + 16)

                def scores(c):
                    s = c % 2
                    if c >= 2:
                        pe.wait_ge(st_done, 9 * h + (c - 1))
                    q = slice(LC * c, LC * (c + 1))
                    mm(psum[:, s, 0:P], head_par[0:MH, H_SEL:H_SEL + P], mneg[0:MH, q], start=True, stop=False)
                    mm(psum[:, s, 0:P], ident, mats[:, K_CAUS if c < NLC else K_BLK, :], start=False, stop=True)
                    for k in range(2):
                        r = mm(psum[:, s, P:2 * P], mk[:, k, q], mq[:, k, q], start=k == 0, stop=k == 1)
                    r.then_inc(es_done, 1)
                    if c >= 1:
                        pe.wait_ge(kw_done, 8 * h + c)
                    for k in range(2):
                        r = tr(psum[:, 6, P * k:P * k + P], mk[:, k, q], ident)
                    r.then_inc(ktr, 1)

                def intra(c):
                    pe.wait_ge(st_done, 9 * h + (c + 1))
                    if c >= 1:
                        pe.wait_ge(num_done, 9 * h + c)
                    return mm(psum[:, 2, 0:MA], sT[:, c % 2, :], vaug[:, c, :], start=True, stop=True)

                def hidden_back(c):
                    pe.wait_ge(hn_done, 9 * h + (c + 1))
                    if c >= 1:
                        pe.wait_ge(mix_done, 9 * h + (c + ONE))
                    for k in range(2):
                        r = tr(psum[:, 7, P * k:P * k + P], hn[:, c % 2, P * k:P * k + P], ident)
                    r.then_inc(ht_done, 1)

                scores(0)
                for c in range(NLC):
                    q = slice(LC * c, LC * (c + 1))
                    scores(c + 1)
                    intra(c)
                    pe.wait_ge(cu_done, 9 * h + (c + 1))
                    for k in range(2):
                        r = mm(psum[:, 3, 0:MA], mq[:, k, q], cst[:, k, :], start=k == 0, stop=k == 1)
                    r.then_inc(ab_done, 1)
                    pe.wait_ge(kw_done, 8 * h + (c + 1))
                    for k in range(2):
                        r = mm(psum[:, 4 + k, 0:MA], kw[:, c % 2, P * k:P * k + P], vaug[:, c, :],
                               start=True, stop=True)
                    r.then_inc(c_done, 1)
                    if c >= 1:
                        hidden_back(c - 1)
                intra(NLC)
                pe.wait_ge(qx_done, h + 1)
                pe.wait_ge(cu_done, 9 * h + 9)
                for b in range(NB):
                    s = b % NCS
                    pe.wait_ge(cs_in[s], 16 * CS_USES[s] * h + 16 * (b // NCS + 1))
                    for k in range(2):
                        r = mm(psum[:, 3, 0:MA], qx[:, k, b, :], csl[:, s, MA * k:MA * (k + 1)],
                               start=b == 0 and k == 0, stop=b == NB - 1 and k == 1)
                    if b == NB - 1:
                        r.then_inc(ab_done, 1)
                    pe.wait_ge(kwm_done, 8 * h + (b + 1))
                    if b >= 1:
                        pe.wait_ge(csu_done, 8 * h + (b + ONE))
                    for k in range(2):
                        r = mm(psum[:, 4 + k, 0:MA], kw[:, b % 2, P * k:P * k + P], vaug[:, NLC, :],
                               start=True, stop=True)
                    r.then_inc(csc_done, 1)
                    if b == 0:
                        hidden_back(NLC - 1)
                hidden_back(NLC)

            pe.wait_ge(mix_done, 9 * MH + ONE)
            pe.wait_ge(csu_done, 8 * MH + ONE)
            for j in range(8):
                u, b = U_OUT1 + j, B_OUT1 + j
                unit(u % 2, u + 1, b, b - 1, split_ready(3 * KT) if j == 0 else None)
            token_sums(AX_R3, 3)
            ff(U_FF1, B_FF1, 4 * KT)
            token_sums(AX_R4, 4)

        @block.vector
        def _(dve):
            V = nc.vector
            for counted in [h_done, mix_done, csu_done, mix_out, cp_out] + cs_out + qh_out:
                dve.sem_inc(counted, ONE)

            def rest(m, k, n, src=None, g=None):
                dve.wait_ge(hi_done, n)
                src = x[:, k, :] if src is None else src
                V.scalar_tensor_tensor(out=a_lo[:, k, :], in0=src, scalar=1.0 if m is None else gain(m, k),
                                       in1=a_hi[:, k, :].bitcast(F32), op0=ALU.mult, op1=ALU.subtract)\
                    .then_inc(lo_done, 1)

            def add_squares(m, k):
                n = KT * m + k
                dve.wait_ge(sq_done, n + 1)
                q = (sq, hid)[k % 2]
                if k == 0:
                    V.tensor_copy(ssq[:, :], q).then_inc(ssq_done, 1)
                else:
                    dve.wait_ge(ssq_done, n)
                    V.tensor_tensor(ssq[:, :], ssq[:, :], q, ALU.add).then_inc(ssq_done, 1)

            def token_scale(n, m):
                for i in range(NT):
                    dve.wait_ge(aux_done, n + i + 1)
                    V.tensor_scalar(rbc[:, tok(i)], psum[:, 6 + (n + i) % 2, 0:TN], 1.0 / D, EPS, ALU.mult, ALU.add)\
                        .then_inc(aux_read, 1)
                dve.wait_ge(aux_read, n + NT)
                V.reciprocal(rbc[:, :], rbc[:, :]).then_inc(rsum_done, 1)
                dve.wait_ge(rbc_done, m + 1)

            def project(b, dst):
                dve.wait_ge(block_done, b + 1)
                V.tensor_tensor(by3(dst), out3(b), by3(rbc[:, :]), ALU.mult).then_inc(evicted, 1)

            def residual(b, count, k, x_ready=None):
                dve.wait_ge(block_done, count)
                if x_ready is not None:
                    dve.wait_ge(x_in[k], x_ready)
                V.tensor_tensor(by3(x[:, k, :]), out3(b), by3(x[:, k, :]), ALU.add).then_inc(evicted, 1)

            def ff(b0, m, last):
                hb = FK * FC * (b0 > B_GATE)

                def up(c, j):
                    dve.wait_ge(block_done, 12 * c + (b0 + j + 1))
                    dve.wait_ge(h_done, FK * c + (hb + j + ONE))
                    V.scalar_tensor_tensor(out=by3(hid), in0=out3(b0 + j), scalar=0.0, in1=by3(rbc[:, :]),
                                           op0=ALU.max, op1=ALU.mult).then_inc(evicted, 1)
                    dve.wait_ge(hsq_done, FK * c + (hb + j + 1))
                    V.tensor_tensor(h_lo[:, j, :], hid, h_hi[:, j, :].bitcast(F32), ALU.subtract).then_inc(h_done, 1)

                with dve.Fori(0, FC - 1) as c:
                    for j in range(FK):
                        up(c, j)
                    for k in range(KT):
                        residual(b0 + FK + k, 12 * c + (b0 + FK + k + 1), k)
                for j in range(FK):
                    up(FC - 1, j)
                for k in range(KT):
                    residual(b0 + FK + k, 12 * (FC - 1) + (b0 + FK + k + 1), k)
                    if not last:
                        rest(m, k, (m if m < 3 else m + 1) * KT + k + 1)
                    add_squares(m, k)

            dve.wait_ge(cols_in, 16)
            dve.wait_ge(mats_in, 16)
            for k in range(KT):
                rest(0, k, k + 1)
                add_squares(0, k)
            V.memset(ext[:, 1:CT + 1, 0:HIST], 0.0).then_inc(pads, 1)
            token_scale(AX_R0, 0)

            def glu(j):
                project(2 * j, za)
                project(2 * j + 1, zs)
                dve.wait_ge(sig_done, j + 1)
                e = ext[:, j + 1, :]
                V.tensor_tensor(e[:, HIST:HIST + TP], za[:, 0:TP], zs[:, 0:TP], ALU.mult)
                V.tensor_tensor(sample(e[:, HIST + TP:EXT], HIST, HIST + TB), sample(za[:, TP:T], 0, TB),
                                sample(zs[:, TP:T], 0, TB), ALU.mult).then_inc(ext_done, 1)

            def conv(j, first, last):
                src, dst = ext[:, j + 1, :], ext[:, j, :]
                sdst = sample(dst[:, TP:T], 0, TB)
                ssrc = src[:, HIST + TP:EXT].rearrange("p (b w) -> p b w", w=HIST + TB)
                n = 2 * CW * j
                if first == 0:
                    w = cols[:, C_CW + CW * j:C_CW + CW * j + 1]
                    cb = cols[:, C_CB + j:C_CB + j + 1]
                    dve.wait_ge(ext_done, j + 1)
                    dve.wait_ge(pads, 1)
                    dve.wait_ge(hist_in, 16 * CT)
                    if j > 0:
                        dve.wait_ge(conv_done, n)
                        dve.wait_ge(conv_out[j - 1], 32)
                    V.tensor_scalar(dst[:, 0:TP], src[:, 0:TP], w, cb, ALU.mult, ALU.add).then_inc(conv_done, 1)
                    V.tensor_scalar(sdst, ssrc[:, :, 0:TB], w, cb, ALU.mult, ALU.add).then_inc(conv_done, 1)
                    first = 1
                with dve.Fori(first, last) as r:
                    w = cols[:, bass.ds(r + (C_CW + CW * j), 1)]
                    dve.wait_ge(conv_done, 2 * r + (n - 1))
                    V.scalar_tensor_tensor(out=dst[:, 0:TP], in0=src[:, bass.ds(r, TP)], scalar=w,
                                           in1=dst[:, 0:TP], op0=ALU.mult, op1=ALU.add).then_inc(conv_done, 1)
                    dve.wait_ge(conv_done, 2 * r + n)
                    V.scalar_tensor_tensor(out=sdst, in0=ssrc[:, :, bass.ds(r, TB)], scalar=w,
                                           in1=sdst, op0=ALU.mult, op1=ALU.add).then_inc(conv_done, 1)

            def rope(n, dst, tile):
                for i in range(NT):
                    dve.wait_ge(aux_done, n + i + 1)
                    V.tensor_tensor(za[:, tok(i)], psum[:, 6 + (n + i) % 2, 0:TN], sin[:, tok(i)], ALU.mult)\
                        .then_inc(aux_read, 1)
                    V.tensor_tensor(dst[:, tok(i)], dst[:, tok(i)], cos[:, tok(i)], ALU.mult).then_inc(rope_done, 1)
                    dve.wait_ge(aux_read, n + i + 1)
                    dve.wait_ge(rope_done, 2 * (NT * tile + i) + 1)
                    V.tensor_tensor(dst[:, tok(i)], dst[:, tok(i)], za[:, tok(i)], ALU.add).then_inc(rope_done, 1)

            glu(0)
            conv(0, 0, 12)
            glu(1)
            conv(0, 12, 26)
            glu(2)
            conv(0, 26, CW)
            conv(1, 0, 9)
            glu(3)
            conv(1, 9, 16)
            project(8, kT)
            conv(1, 16, 23)
            project(9, vT)
            conv(1, 23, 30)
            project(10, qT[:, 0, :])
            dve.wait_ge(cs_tab_in, 32)
            rope(AX_KROPE, kT, 0)
            for g in range(6):
                dve.wait_ge(aux_done, AX_V + g + 1)
                n, dst = (CH, v64[0:CH, 4 * g:4 * g + 4, :]) if g < 4 else (TB, v16[0:TB, 4 * g - 16:4 * g - 12, :])
                V.tensor_copy(dst, psum[0:n, 6 + g % 2, :].rearrange("p (a b) -> p a b", a=4)).then_inc(aux_read, 1)
            dve.wait_ge(cache_in, 32)
            dve.wait_ge(rope_done, 2 * NT)
            V.tensor_copy(kc[:, :, WIN:SK], sample(kT[:, TP:T], 0, TB)).then_inc(kc_done, 1)
            project(11, qT[:, 1, :])
            rope(AX_QROPE, qT[:, 0, :], 1)
            conv(1, 30, CW)
            conv(2, 0, 4)
            project(12, qT[:, 2, :])
            rope(AX_QROPE + NT, qT[:, 1, :], 2)
            conv(2, 4, 9)
            project(13, qT[:, 3, :])
            rope(AX_QROPE + 2 * NT, qT[:, 2, :], 3)
            rope(AX_QROPE + 3 * NT, qT[:, 3, :], 4)
            conv(2, 9, CW)
            conv(3, 0, CW)

            rows_v = zs[:, :]
            dve.wait_ge(conv_done, 2 * CT * CW)
            for i in range(NT):
                dve.wait_ge(aux_done, AX_LN + i + 1)
                for j in range(CT):
                    r = V.scalar_tensor_tensor(out=ext[:, j, tok(i)], in0=psum[:, 6 + (AX_LN + i) % 2, 0:TN],
                                               scalar=-1.0 / (CT * P), in1=ext[:, j, tok(i)],
                                               op0=ALU.mult, op1=ALU.add)
                r.then_inc(aux_read, 1)
            for i in range(NT):
                n = AX_LN + NT + i
                dve.wait_ge(aux_done, n + 1)
                V.tensor_scalar(rows_v[:, tok(i)], psum[:, 6 + n % 2, 0:TN], 1.0 / (CT * P), EPS, ALU.mult, ALU.add)\
                    .then_inc(aux_read, 1)
                dve.wait_ge(aux_read, n + 1)
                V.reciprocal(rows_v[:, tok(i)], rows_v[:, tok(i)]).then_inc(ln_v, 1)
            for i in range(NT):
                dve.wait_ge(ln_rstd, i + 1)
                V.tensor_tensor(ext[:, 0:CT, tok(i)], ext[:, 0:CT, tok(i)],
                                rows_v[:, tok(i)].unsqueeze(1).to_broadcast([P, CT, TN]), ALU.mult)\
                    .then_inc(ln_scaled, 1)
            for i in range(NT):
                dve.wait_ge(ln_hi, i + 1)
                V.tensor_tensor(a_lo[:, CT:2 * CT, tok(i)], ext[:, 0:CT, tok(i)],
                                a_hi[:, CT:2 * CT, tok(i)].bitcast(F32), ALU.subtract).then_inc(ln_lo, 1)

            def stage(c):
                if not (isinstance(c, int) and c == 0):
                    dve.wait_ge(s_done, 2 * c)
                for v in range(2):
                    h_ = slice(HD * v, HD * v + HD)
                    r = V.tensor_scalar(qs[h_, v, :, :], qT[h_, :, bass.ds(CH * c, CH)], 1.0, None, ALU.mult)
                r.then_inc(q_staged, 1)

            def maxima(n, p, src, width, col):
                dve.wait_ge(s_done, n + 1)
                if not (isinstance(n, int) and n < 2):
                    dve.wait_ge(p_done, n - 1)
                V.tensor_reduce(st[:, p, 0:width], src, AX, ALU.max).then_inc(stat_done, 1)
                dve.wait_ge(stat_done, 2 * n + (NSINK + 1))
                V.scalar_tensor_tensor(out=st[:, p, 2:2 + width], in0=st[:, p, 0:width], scalar=-ATT_SCALE,
                                       in1=nsink[:, col:col + width], op0=ALU.mult, op1=ALU.min)\
                    .then_inc(stat_done, 1)
                dve.wait_ge(stat_done, 2 * n + (NSINK + 2))
                V.tensor_tensor(st[:, p, 4:4 + width], st[:, p, 2:2 + width],
                                cols[:, C_SINK + col:C_SINK + col + width], ALU.add).then_inc(m_done, 1)

            def denominators(n, p, width):
                dve.wait_ge(pv_done, n + 1)
                dve.wait_ge(p_done, n + 1)
                V.tensor_tensor(st[:, p, 8:8 + width], st[:, p, 6:6 + width], st[:, p, 10:10 + width], ALU.add)\
                    .then_inc(den_done, 1)
                dve.wait_ge(den_done, 2 * n + 1)
                V.reciprocal(st[:, p, 12:12 + width], st[:, p, 8:8 + width]).then_inc(den_done, 1)
                dve.wait_ge(den_done, 2 * n + 2)
                if not (isinstance(n, int) and n < 2):
                    dve.wait_ge(ot_done, n - 1)

            def output(n, p):
                denominators(n, p, 2)
                V.tensor_tensor(ob[:, p, :].rearrange("p (v d) -> p v d", v=2),
                                psum[:, 6 + p, 0:P].rearrange("p (v d) -> p v d", v=2),
                                st[:, p, 12:14].unsqueeze(2).to_broadcast([P, 2, HD]), ALU.mult).then_inc(o_done, 1)

            def mixed_in(c, p):
                n = 2 * c + p
                dve.wait_ge(ot_done, n + 1)
                src = psum[:, 6 + p, P:2 * P].rearrange("p (j q) -> p j q", j=2)
                at = bass.ds(CH * c, CH)
                V.tensor_scalar(a_hi[:, 2 * p:2 * p + 2, at], src, 1.0, None, ALU.mult).then_inc(ahi_done, 1)
                dve.wait_ge(ahi_done, n + 1)
                V.tensor_tensor(a_lo[:, 2 * p:2 * p + 2, at], src, a_hi[:, 2 * p:2 * p + 2, at].bitcast(F32),
                                ALU.subtract).then_inc(mixed, 1)

            def chunk_width(c):
                return CH * (c + 1) if isinstance(c, int) and c < 2 else 3 * CH

            def astep(c, first=False, more=True):
                w = chunk_width(c)
                for p in range(2):
                    maxima(2 * c + p, p, psum[:, p, 0:384].rearrange("p (v k) -> p v k", v=2)[:, :, 0:w], 2, 2 * p)
                if more:
                    stage(c + 1)
                if not first:
                    for p in range(2):
                        output(2 * c - 2 + p, p)
                    for p in range(2):
                        mixed_in(c - 1, p)

            V.memset(qs[:, :, :, :], 0.0).then_inc(stat_done, 1)
            V.memset(obs[:, :, :], 0.0)
            V.tensor_scalar(nsink, cols[:, C_SINK:C_SINK + 5], -1.0, None, ALU.mult).then_inc(stat_done, 1)
            dve.wait_ge(stat_done, NSINK)
            stage(0)
            astep(0, True)
            astep(1)
            astep(2)
            with dve.Fori(3, NCH - 1) as c:
                astep(c)
            astep(NCH - 1, more=False)
            for p in range(2):
                output(2 * NCH - 2 + p, p)
            for p in range(2):
                mixed_in(NCH - 1, p)

            dve.wait_ge(s_done, 2 * NCH)
            V.tensor_copy(qss.rearrange("p b (j t) -> p b j t", j=4),
                          qT[:, :, TP:T].rearrange("p j (b t) -> p b j t", t=TB)).then_inc(q_staged, 1)

            def s_output(b, s, n):
                denominators(n, s, 1)
                for v in range(2):
                    h_ = slice(HD * v, HD * v + HD)
                    r = V.tensor_scalar(obs[h_, s, h_], psum[h_, 6 + s, 0:HD], st[h_, s, 12:13], None, ALU.mult)
                r.then_inc(o_done, 1)

            def s_mixed(b, s, n):
                dve.wait_ge(ot_done, n + 1)
                at = slice(TP + TB * b, TP + TB * (b + 1))

                def src(h_):
                    return psum[h_, 6 + s, P + h_.start:P + h_.stop].rearrange("p (j q) -> p j q", j=4)
                halves = [slice(HD * v, HD * v + HD) for v in range(2)]
                for h_ in halves:
                    r = V.tensor_scalar(a_hi[h_, 0:4, at], src(h_), 1.0, None, ALU.mult)
                r.then_inc(ahi_done, 1)
                dve.wait_ge(ahi_done, n + 1)
                for h_ in halves:
                    r = V.tensor_tensor(a_lo[h_, 0:4, at], src(h_), a_hi[h_, 0:4, at].bitcast(F32), ALU.subtract)
                r.then_inc(mixed, 1)

            for b in range(NB + 1):
                n, s = 2 * NCH + b, b % 2
                if b < NB:
                    maxima(n, s, psum[:, s, 0:SK].unsqueeze(1), 1, 4)
                if b > 0:
                    s_output(b - 1, 1 - s, n - 1)
                    s_mixed(b - 1, 1 - s, n - 1)

            for k in range(KT):
                residual(B_OUT0 + k, B_OUT0 + k + 1, k, 32)
                add_squares(1, k)
            for k in range(KT):
                rest(1, k, KT + k + 1)
            token_scale(AX_R1, 1)
            ff(B_FF0, 2, False)

            token_scale(AX_R2, 2)
            rowc = [0]

            def row(ins):
                rowc[0] += 1
                ins.then_inc(gate_rows, 1)
                dve.wait_ge(gate_rows, rowc[0])

            R4 = slice(0, MH)
            row(V.memset(gp[R4, :], 1.0))
            row(V.memset(gp[R4, 0:TP:LC], 0.0))
            row(V.memset(gp[R4, TP:T:TB], 0.0))
            V.memset(gd[R4, :], 0.0)
            V.memset(rows[:, :], 0.0)
            dve.wait_ge(block_done, B_GATE + 1)
            gsrc = out3(B_GATE)
            V.tensor_tensor(by3(gz)[0:64], gsrc[0:64], by3(rbc[:, :])[0:64], ALU.mult).then_inc(evicted, 1)
            dve.wait_ge(evicted, B_GATE + 1)
            row(V.tensor_scalar(gt[0:64, :], gz[0:64, :], cols[0:64, C_GB:C_GB + 1], None, ALU.add))
            row(V.tensor_scalar(gm[32:36, :], gt[32:36, :], 0.0, None, ALU.min))
            dve.wait_ge(gates_act, 1)
            row(V.tensor_tensor(glf[R4, :], gm[32:36, :], gz[32:36, :], ALU.subtract))
            row(V.tensor_tensor_scan(gb[R4, :], gp[R4, :], glf[R4, :], 0.0, ALU.mult, ALU.add))
            row(V.tensor_tensor(gg[R4, :], gt[R4, :], gb[R4, :], ALU.subtract))
            row(V.tensor_copy(gz[R4, :], gg[R4, :]))
            m0 = cols[R4, C_M0:C_M0 + NB]
            row(V.tensor_tensor(gz[R4, TP:T:TB], gg[R4, TP:T:TB], m0, ALU.max))
            row(V.tensor_copy(gd[R4, LC:TP:LC], gb[R4, LC - 1:TP - 1:LC]))
            row(V.memset(gd[R4, TP:T:TB], NEG))
            row(V.tensor_tensor_scan(gm[R4, :], gd[R4, :], gz[R4, :], 0.0, ALU.add, ALU.max))
            V.tensor_tensor(mend[R4, 0:8], gb[R4, LC - 1:TP:LC], gm[R4, LC - 1:TP:LC], ALU.add)
            row(V.tensor_tensor(mend[R4, 8:16], gb[R4, TP + TB - 1:T:TB], gm[R4, TP + TB - 1:T:TB], ALU.add))
            row(V.memset(gp[R4, 0:LC], 0.0))
            row(V.tensor_copy(gp[R4, LC:TP].rearrange("p (c t) -> p c t", t=LC),
                              mend[R4, 0:7].unsqueeze(2).to_broadcast([MH, NLC - 1, LC])))
            row(V.tensor_copy(gp[R4, TP:T].rearrange("p (c t) -> p c t", t=TB),
                              m0.unsqueeze(2).to_broadcast([MH, NB, TB])))
            row(V.tensor_copy(gd[R4, 0:TP].rearrange("p (c t) -> p c t", t=LC),
                              gm[R4, LC - 1:TP:LC].unsqueeze(2).to_broadcast([MH, NLC, LC])))
            row(V.tensor_copy(gd[R4, TP:T].rearrange("p (c t) -> p c t", t=TB),
                              gm[R4, TP + TB - 1:T:TB].unsqueeze(2).to_broadcast([MH, NB, TB])))
            V.tensor_scalar(mneg[R4, :], gm[R4, :], -1.0, None, ALU.mult)
            V.tensor_tensor(rows[0:4, :], gp[R4, :], gm[R4, :], ALU.subtract)
            V.tensor_tensor(rows[32:36, :], gg[R4, :], gd[R4, :], ALU.subtract)
            V.tensor_copy(rows[64:68, :], gg[R4, :])
            V.scalar_tensor_tensor(out=rows[96:100, :], in0=gb[R4, :], scalar=-1.0, in1=gm[R4, :],
                                   op0=ALU.mult, op1=ALU.subtract)
            V.tensor_tensor(wc16[R4, 0:8], gp[R4, 0:TP:LC], gd[R4, 0:TP:LC], ALU.subtract)
            row(V.tensor_tensor(wc16[R4, 8:16], gp[R4, TP:T:TB], gd[R4, TP:T:TB], ALU.subtract))
            assert rowc[0] == GATE_TO_EXP
            dve.wait_ge(gates_act, 4)
            row(V.tensor_tensor(wd[R4, :].rearrange("p (h i) -> p h i", h=MH), wc16[R4, :].unsqueeze(1).to_broadcast([MH, MH, 16]),
                                cols[R4, C_MH:C_MH + MH * 16].rearrange("p (h i) -> p h i", h=MH), ALU.mult))
            assert rowc[0] == GATE_ROWS
            for g in range(3):
                dve.wait_ge(aux_done, AX_GT + g + 1)
                k = min(4, NLC + 1 - 4 * g)
                V.tensor_copy(rtc[:, 4 * g:4 * g + k, :, :],
                              psum[:, 6 + (AX_GT + g) % 2, 0:P * k].rearrange("p (c q r) -> p c q r", c=k, q=4)[:, :, :, 0:MH])\
                    .then_inc(aux_read, 1)
            dve.wait_ge(aux_done, AX_WC + 1)
            V.tensor_copy(wcb[:, :, :], psum[:, 6 + AX_WC % 2, 0:MH * 16].rearrange("p (h i) -> p h i", h=MH))\
                .then_inc(aux_read, 1)
            dve.wait_ge(aux_read, AX_WC + 1)
            row(V.tensor_scalar(rtc[:, :, Q_WS, :], rtc[:, :, Q_WS, :], MD ** -0.5, None, ALU.mult))

            V.memset(qext[:, :, 0:QH], 0.0)
            V.memset(vaug[:, :, MD:MA], 1.0)
            row(V.memset(qx[:, :, :, :], 0.0))
            dve.wait_ge(spilled, 16 * KT)
            with dve.Fori(0, MH) as h:
                V.tensor_scalar(rth[:, :, :], rtc[:, :, :, bass.ds(h, 1)].rearrange("p c q o -> p c (q o)"),
                                1.0, None, ALU.mult)
                V.tensor_scalar(wch[:, :], wcb[:, bass.ds(h, 1), :].rearrange("p o i -> p (o i)"),
                                1.0, None, ALU.mult).then_inc(head_set, 1)
                dve.wait_ge(head_set, 2 * h + 1)
                V.tensor_scalar(ws8[:, :], cols[:, C_BSEL:C_BSEL + NB], rth[:, NLC, Q_WS:Q_WS + 1], None, ALU.mult)\
                    .then_inc(head_set, 1)
                dve.wait_ge(cp_out, 16 * h + ONE)
                V.memset(cst[:, :, :], 0.0).then_inc(cu_done, 1)

                def leave(j, dst):
                    dve.wait_ge(block_done, 8 * h + (B_HEAD + j + 1))
                    V.tensor_tensor(by3(dst), out3(B_HEAD + j), by3(rbc[:, :]), ALU.mult).then_inc(evicted, 1)

                def qk_ext(j):
                    i, s = j - 2, j % 2
                    e, z = qext[:, s, :], out3(B_HEAD + j)
                    dve.wait_ge(block_done, 8 * h + (B_HEAD + j + 1))
                    dve.wait_ge(qh_in[i], 16 * h + 16)
                    dve.wait_ge(qh_out[(i + 2) % 4], 32 * h + (32 * (i >= 2) + ONE))
                    V.tensor_tensor(e[:, QH:QH + 2 * TN].rearrange("p (a b) -> p a b", a=2), z[:, 0:2, :],
                                    by3(rbc[:, :])[:, 0:2, :], ALU.mult)
                    V.tensor_tensor(e[:, QH + 2 * TN:QH + TP], z[:, 2, 0:TP - 2 * TN], rbc[:, 2 * TN:TP], ALU.mult)
                    V.tensor_tensor(sample(e[:, QH + TP:QEXT], QH, QH + TB), sample(z[:, 2, TP - 2 * TN:TN], 0, TB),
                                    sample(rbc[:, TP:T], 0, TB), ALU.mult).then_inc(evicted, 1)
                    dve.wait_ge(evicted, 8 * h + (B_HEAD + j + 1))
                    if i == 0:
                        dve.wait_ge(par_in, 16 * h + 16)
                    dst = mk[:, i, :] if i < 2 else mq[:, i - 2, :]
                    es_ = e[:, QH + TP:QEXT].rearrange("p (b w) -> p b w", w=QH + TB)
                    for r in range(QW):
                        w = head_par[:, H_W + QW * i + r:H_W + QW * i + r + 1]
                        for part, (o, a) in enumerate((
                                (dst[:, 0:TP], e[:, r:r + TP]),
                                (sample(dst[:, TP:T], 0, TB), es_[:, :, r:r + TB]))):
                            if r == 0:
                                V.tensor_scalar(o, a, w, head_par[:, H_B + i:H_B + i + 1], ALU.mult, ALU.add)\
                                    .then_inc(qconv, 1)
                            else:
                                dve.wait_ge(qconv, 32 * h + (8 * i + 2 * r + part - 1))
                                V.scalar_tensor_tensor(out=o, in0=a, scalar=w, in1=o, op0=ALU.mult, op1=ALU.add)\
                                    .then_inc(qconv, 1)

                leave(0, mv[:, 0, :])
                leave(1, mv[:, 1, :])
                for j in range(2, 6):
                    qk_ext(j)
                leave(6, mo[:, 0, :])
                leave(7, mo[:, 1, :])
                dve.wait_ge(qsilu, 4 * h + 4)
                for b in range(NB):
                    r = V.tensor_copy(qx[:, :, b, TB * b:TB * (b + 1)], mq[:, :, TP + TB * b:TP + TB * (b + 1)])
                r.then_inc(qx_done, 1)
                dve.wait_ge(osig, 2 * h + 2)
                dve.wait_ge(mix_out, 16 * h + ONE)

                def gated(c):
                    s = c % 2
                    dve.wait_ge(e_done, 9 * h + (c + 1))
                    V.scalar_tensor_tensor(out=sT[:, s, :], in0=psum[:, s, P:2 * P], scalar=MD ** -0.5,
                                           in1=eM[:, s, :], op0=ALU.mult, op1=ALU.mult).then_inc(st_done, 1)

                def numerator(c):
                    s = c % 2
                    dve.wait_ge(tb_done, 9 * h + (c + 1))
                    V.tensor_tensor(num[:, s, 0:MA], psum[:, 2, 0:MA], tB[:, s, 0:MA], ALU.add).then_inc(num_done, 1)
                    dve.wait_ge(num_done, 9 * h + (c + 1))
                    den = num[:, s, MD:MA]
                    V.scalar_tensor_tensor(out=sm[:, s, 0:1], in0=den, scalar=-1.0, in1=den, op0=ALU.mult,
                                           op1=ALU.max).then_inc(dn_done, 1)
                    dve.wait_ge(dn_done, 27 * h + (3 * c + 1))
                    V.tensor_scalar(sm[:, s, 1:2], sm[:, s, 0:1], rth[:, c, Q_EM:Q_EM + 1], None, ALU.max)\
                        .then_inc(dn_done, 1)
                    dve.wait_ge(dn_done, 27 * h + (3 * c + 2))
                    V.reciprocal(sm[:, s, 2:3], sm[:, s, 1:2]).then_inc(dn_done, 1)

                def normed(c):
                    s = c % 2
                    dve.wait_ge(sc_done, 9 * h + (c + 1))
                    V.tensor_scalar(hn[:, s, :], num[:, s, 0:MD], sm[:, s, 6:7], 16.0, ALU.mult, ALU.mult)\
                        .then_inc(hn_done, 1)

                def gate_out(c):
                    q = slice(LC * c, LC * (c + 1))
                    dve.wait_ge(ht_done, 9 * h + (c + 1))
                    for k in range(2):
                        r = V.scalar_tensor_tensor(out=mix[:, k, q], in0=psum[:, 7, P * k:P * k + P],
                                                   scalar=head_par[:, H_G + k:H_G + k + 1], in1=mo[:, k, q],
                                                   op0=ALU.mult, op1=ALU.mult)
                    r.then_inc(mix_done, 1)

                gated(0)
                for c in range(NLC):
                    numerator(c)
                    dve.wait_ge(c_done, 8 * h + (c + 1))
                    V.scalar_tensor_tensor(out=cst[:, :, :], in0=cst[:, :, :], scalar=wch[:, c:c + 1],
                                           in1=psum[:, 4:6, 0:MA], op0=ALU.mult, op1=ALU.add).then_inc(cu_done, 1)
                    gated(c + 1)
                    if c >= 1:
                        gate_out(c - 1)
                    normed(c)
                for b in range(NB):
                    s = b % NCS
                    dve.wait_ge(csc_done, 8 * h + (b + 1))
                    m = csl[:, s, :].rearrange("p (k e) -> p k e", k=2)
                    V.scalar_tensor_tensor(out=m, in0=m, scalar=wch[:, 8 + b:9 + b], in1=psum[:, 4:6, 0:MA],
                                           op0=ALU.mult, op1=ALU.add).then_inc(csu_done, 1)
                    if b == 0:
                        gate_out(NLC - 1)
                numerator(NLC)
                normed(NLC)
                gate_out(NLC)

            for k in range(KT):
                rest(None, k, 3 * KT + k + 1, src=mixed_h[:, k, :])
            for k in range(KT):
                residual(B_OUT1 + k, B_OUT1 + k + 1, k, 48)
                add_squares(3, k)
            for k in range(KT):
                rest(3, k, 4 * KT + k + 1)
            token_scale(AX_R3, 3)
            ff(B_FF1, 4, True)

            token_scale(AX_R4, 4)
            for k in range(KT):
                V.scalar_tensor_tensor(out=x[:, k, :], in0=x[:, k, :], scalar=gain(4, k), in1=rbc[:, :],
                                       op0=ALU.mult, op1=ALU.mult).then_inc(y_done, 1)

        @block.scalar
        def _(act):
            A = nc.scalar.activation
            dma = act.dma_start

            def high_part(m, k, src=None):
                src = x[:, k, :] if src is None else src
                A(a_hi[:, k, :], src, ACT.Copy, scale=1.0 if m is None else gain(m, k)).then_inc(hi_done, 1)

            def square(m, k):
                n = KT * m + k
                if n >= 2:
                    act.wait_ge(ssq_done, n - 1)
                A((sq, hid)[k % 2], x[:, k, :], ACT.Square).then_inc(sq_done, 1)

            def root(m):
                act.wait_ge(rsum_done, m + 1)
                A(rbc[:, :], rbc[:, :], ACT.Sqrt).then_inc(rbc_done, 1)

            def ff(b0, m, last):
                hb = FK * FC * (b0 > B_GATE)

                def up(c, j):
                    act.wait_ge(evicted, 12 * c + (b0 + j + 1))
                    A(h_hi[:, j, :], hid, ACT.Square)
                    A(hid, hid, ACT.Square).then_inc(hsq_done, 1)

                with act.Fori(0, FC) as c:
                    for j in range(FK):
                        up(c, j)
                for k in range(KT):
                    act.wait_ge(evicted, 12 * (FC - 1) + (b0 + FK + k + 1))
                    if not last:
                        high_part(m, k)
                    square(m, k)
                    if not last:
                        dma(t["x_spill"][k], x[:, k, :]).then_inc(spilled, 16)

            dma(cols[:, :], t["cols"]).then_inc(cols_in, 16)
            dma(mats[:, :, :], t["mats"]).then_inc(mats_in, 16)
            for k in range(KT):
                dma(x[:, k, :], t["x"][k]).then_inc(x_in[k], 16)
            dma(kc[:, :, 0:WIN], t["kcache"]).then_inc(cache_in, 16)
            dma(vc[:, :, :], t["vcache"]).then_inc(cache_in, 16)

            act.wait_ge(cols_in, 16)
            for k in range(KT):
                act.wait_ge(x_in[k], 16)
                high_part(0, k)
                square(0, k)
            act.wait_ge(lo_done, KT)
            act.wait_ge(sq_done, KT)
            for j in range(CT):
                dma(ext[:, j + 1, HIST + TP:EXT].rearrange("p (b w) -> p b w", w=HIST + TB)[:, :, 0:HIST],
                    t["conv_hist"][j]).then_inc(hist_in, 16)
            root(0)
            act.wait_ge(rbc_done, 1)
            dma(cos, t["cos"]).then_inc(cs_tab_in, 16)
            dma(sin, t["sin"]).then_inc(cs_tab_in, 16)

            for j in range(CT):
                act.wait_ge(evicted, 2 * j + 2)
                A(zs, zs, ACT.Sigmoid).then_inc(sig_done, 1)
                act.wait_ge(ext_done, j + 1)
                e = ext[:, j + 1, :]
                dma(t["conv_p"][j], e[:, TP:TP + HIST]).then_inc(conv_out[j], 16)
                act.wait_ge(hist_in, 16 * CT)
                dma(t["conv_s"][j], e[:, HIST + TP:EXT].rearrange("p (b w) -> p b w", w=HIST + TB)[:, :, TB:])\
                    .then_inc(conv_out[j], 16)
            act.wait_ge(evicted, 10)
            dma(t["v_p"], vT[:, TP - WIN:TP]).then_inc(kv_out, 16)
            dma(t["v_s"], vT[:, TP:T]).then_inc(kv_out, 16)
            act.wait_ge(cache_in, 32)
            dma(t["v_old"], vc[TB:WIN, :, :]).then_inc(kv_out, 16)
            act.wait_ge(kc_done, 1)
            dma(t["k_p"], kT[:, TP - WIN:TP]).then_inc(kv_out, 16)
            dma(t["k_s"], kc[:, :, TB:SK]).then_inc(kv_out, 16)

            for i in range(NT):
                act.wait_ge(aux_read, AX_LN + i + 1)
                if i > 0:
                    act.wait_ge(aux_done, AX_LN + NT + i)
                A(lnsq[:, :, :], ext[:, 0:CT, tok(i)], ACT.Square).then_inc(ln_sq, 1)
            for i in range(NT):
                act.wait_ge(ln_v, i + 1)
                A(zs[:, tok(i)], zs[:, tok(i)], ACT.Sqrt).then_inc(ln_rstd, 1)
            for i in range(NT):
                act.wait_ge(ln_scaled, i + 1)
                for j in range(CT):
                    A(ext[:, j, tok(i)], ext[:, j, tok(i)], ACT.Silu, bias=cols[:, C_LB + j:C_LB + j + 1],
                      scale=cols[:, C_LG + j:C_LG + j + 1]).then_inc(ln_y, 1)
                act.wait_ge(ln_y, CT * (i + 1))
                A(a_hi[:, CT:2 * CT, tok(i)], ext[:, 0:CT, tok(i)], ACT.Copy).then_inc(ln_hi, 1)
            act.wait_ge(ln_lo, NT)
            act.wait_ge(kv_out, 16 * 5)
            for j in range(CT):
                act.wait_ge(conv_out[j], 32)
            for k in range(KT):
                dma(x[:, k, :], t["x"][k]).then_inc(x_in[k], 16)

            def probs(n, p, parts, width):
                act.wait_ge(m_done, n + 1)
                if not (isinstance(n, int) and n < 2):
                    act.wait_ge(t_done, n - 1)
                    act.wait_ge(den_done, 2 * n - 2)
                for v, (dst, src) in enumerate(parts):
                    A(dst, src, ACT.Exp, bias=st[:, p, 2 + v:3 + v], scale=ATT_SCALE, accum_out=st[:, p, 6 + v:7 + v])
                A(st[:, p, 10:10 + width], st[:, p, 4:4 + width], ACT.Exp).then_inc(p_done, 1)

            def copy_flipped(n, p, pieces):
                act.wait_ge(t_done, n + 1)
                if not (isinstance(n, int) and n < 2):
                    act.wait_ge(pv_done, n - 1)
                for dst, src in pieces:
                    r = A(dst, src, ACT.Copy)
                r.then_inc(pt_done, 1)

            def astep(c):
                nb = c + 1 if isinstance(c, int) and c < 2 else 3
                for p in range(2):
                    probs(2 * c + p, p, [(pr[:, p, 192 * v:192 * v + CH * nb], psum[:, p, 192 * v:192 * v + CH * nb])
                                         for v in range(2)], 2)
                for p in range(2):
                    both = psum[0:CH, 2 + 2 * p:4 + 2 * p, :].rearrange("p a b -> p (a b)")
                    if nb == 3:
                        pieces = [(pT[0:CH, p, 0:6 * P], both[:, 0:6 * P])]
                    else:
                        pieces = [(pT[0:CH, p, 3 * P * v:3 * P * v + nb * P], both[:, 3 * P * v:3 * P * v + nb * P])
                                  for v in range(2)]
                    copy_flipped(2 * c + p, p, pieces)

            for c in range(3):
                astep(c)
            with act.Fori(3, NCH) as c:
                astep(c)
            for b in range(NB):
                n, s = 2 * NCH + b, b % 2
                probs(n, s, [(pr[:, s, 0:SK], psum[:, s, 0:SK])], 1)
                copy_flipped(n, s, [(pT[:, s, 0:P], psum[:, 2 + 2 * s, 0:P]),
                                    (pT[0:TB, s, P:2 * P], psum[0:TB, 2 + 2 * s, P:2 * P])])

            for k in range(KT):
                act.wait_ge(evicted, B_OUT0 + k + 1)
                square(1, k)
            for k in range(KT):
                high_part(1, k)
            root(1)
            ff(B_FF0, 2, False)

            root(2)
            act.wait_ge(gate_rows, 5)
            A(gz[32:36, :], gt[32:36, :], ACT.Abs).then_inc(gact_own, 1)
            act.wait_ge(gact_own, 1)
            A(gz[32:36, :], gz[32:36, :], ACT.Exp, scale=-1.0).then_inc(gact_own, 1)
            act.wait_ge(gact_own, 2)
            A(gz[32:36, :], gz[32:36, :], ACT.Ln, bias=1.0).then_inc(gates_act, 1)
            act.wait_ge(gate_rows, GATE_TO_EXP)
            for q in (0, 32, 96):
                r = A(rows[q:q + MH, :], rows[q:q + MH, :], ACT.Exp)
                if q:
                    r.then_inc(gates_act, 1)
            A(wc16[0:MH, :], wc16[0:MH, :], ACT.Exp).then_inc(gates_act, 1)
            dma(t["m_out"], mend[0:MH, :]).then_inc(g_out, 16)
            act.wait_ge(gate_rows, GATE_ROWS + 2)

            with act.Fori(0, MH) as h:
                act.wait_ge(mix_done, 9 * h + ONE)
                dma(head_par[:, :], t["head_par"][h]).then_inc(par_in, 16)

                def history(i):
                    e = qext[:, i % 2, QH + TP:QEXT].rearrange("p (b w) -> p b w", w=QH + TB)
                    dma(e[:, :, 0:QH], t["qk_hist"][h, i]).then_inc(qh_in[i], 16)

                def sample_in(b):
                    s = b % NCS
                    if b < NCS:
                        act.wait_ge(cs_out[s], 16 * CS_USES[s] * h + ONE)
                    else:
                        act.wait_ge(cs_out[s], 16 * CS_USES[s] * h + (16 * (b // NCS) + ONE))
                    dma(csl[:, s, :], t["mem_in"][h, b]).then_inc(cs_in[s], 16)

                for i in (2, 3):
                    act.wait_ge(qh_out[i], 32 * h + ONE)
                history(0)
                history(1)
                for b in range(NCS):
                    sample_in(b)
                for i in range(4):
                    j = i + 2
                    act.wait_ge(evicted, 8 * h + (B_HEAD + j + 1))
                    act.wait_ge(qh_in[i], 16 * h + 16)
                    e = qext[:, i % 2, :]
                    dma(t["qk_p"][h, i], e[:, TP:TP + QH]).then_inc(qh_out[i], 16)
                    dma(t["qk_s"][h, i], e[:, QH + TP:QEXT].rearrange("p (b w) -> p b w", w=QH + TB)[:, :, TB:])\
                        .then_inc(qh_out[i], 16)
                    act.wait_ge(qconv, 32 * h + 8 * (i + 1))
                    dst = mk[:, i, :] if i < 2 else mq[:, i - 2, :]
                    A(dst, dst, ACT.Silu).then_inc(qsilu, 1)
                    if i < 2:
                        act.wait_ge(qh_out[i], 32 * h + (32 + ONE))
                        history(i + 2)
                for k in range(2):
                    act.wait_ge(evicted, 8 * h + (B_HEAD + 7 + k))
                    A(mo[:, k, :], mo[:, k, :], ACT.Sigmoid).then_inc(osig, 1)
                for c in range(NLC + 1):
                    act.wait_ge(vtr, 9 * h + (c + 1))
                    A(vaug[:, c, 0:MD], psum[:, 6 + c % 2, 0:MD], ACT.Copy).then_inc(vcp, 1)
                act.wait_ge(head_set, 2 * h + 2)

                def decay(c):
                    s = c % 2
                    act.wait_ge(es_done, 9 * h + (c + 1))
                    A(eM[:, s, :], psum[:, s, 0:P], ACT.Exp, bias=rth[:, c, Q_G:Q_G + 1]).then_inc(e_done, 1)

                def keys(c):
                    s = c % 2
                    act.wait_ge(ktr, 9 * h + (c + 1))
                    if c >= 2:
                        act.wait_ge(c_done, 8 * h + (c - 1))
                    A(kw[:, s, :], psum[:, 6, 0:MD], ACT.Copy, scale=rth[:, c, Q_WS:Q_WS + 1]).then_inc(kw_done, 1)

                def inter(c):
                    s = c % 2
                    act.wait_ge(ab_done, 9 * h + (c + 1))
                    A(tB[:, s, 0:MA], psum[:, 3, 0:MA], ACT.Copy, scale=rth[:, c, Q_INT:Q_INT + 1])\
                        .then_inc(tb_done, 1)

                def sumsq(c):
                    s = c % 2
                    act.wait_ge(dn_done, 27 * h + (3 * c + 3))
                    A(junk, num[:, s, 0:MD], ACT.Square, scale=sm[:, s, 2:3], accum_out=sm[:, s, 3:4])\
                        .then_inc(ss_done, 1)

                def masked_keys(b):
                    if b < 2:
                        act.wait_ge(ktr, 9 * h + 9)
                        act.wait_ge(c_done, 8 * h + (7 + b))
                    else:
                        act.wait_ge(csc_done, 8 * h + (b - 1))
                    A(kw[:, b % 2, :], psum[:, 6, 0:MD], ACT.Copy, scale=ws8[:, b:b + 1]).then_inc(kwm_done, 1)

                def sample_out(b):
                    s = b % NCS
                    act.wait_ge(csu_done, 8 * h + (b + 1 + ONE))
                    dma(t["mem_s"][h, b], csl[:, s, :]).then_inc(cs_out[s], 16)

                decay(0)
                keys(0)
                for c in range(NLC):
                    inter(c)
                    decay(c + 1)
                    sumsq(c)
                    if c + 1 < NLC:
                        keys(c + 1)
                act.wait_ge(cu_done, 9 * h + 9)
                dma(t["mem_p"][h], cst[:, :, :]).then_inc(cp_out, 16)
                masked_keys(0)
                masked_keys(1)
                for b in range(NB):
                    sample_out(b)
                    if b + 2 < NB:
                        masked_keys(b + 2)
                    if b + NCS < NB:
                        sample_in(b + NCS)
                inter(NLC)
                sumsq(NLC)
                act.wait_ge(mix_done, 9 * h + (9 + ONE))
                dma(t["mix_spill"][h], mix[:, :, :]).then_inc(mix_out, 16)

            act.wait_ge(mix_out, 16 * MH + ONE)
            act.wait_ge(cp_out, 16 * MH + ONE)
            for s in range(NCS):
                act.wait_ge(cs_out[s], 16 * CS_USES[s] * MH + ONE)
            for i in range(4):
                act.wait_ge(qh_out[i], 32 * MH + ONE)
            for h in range(MH):
                dma(mixed_h[:, 2 * h:2 * h + 2, :], t["mix_spill"][h]).then_inc(mix_back[h], 16)
            for k in range(KT):
                dma(x[:, k, :], t["x_spill"][k]).then_inc(x_in[k], 16)
            for k in range(KT):
                act.wait_ge(mix_back[k // 2], 16)
                high_part(None, k, mixed_h[:, k, :])
            for k in range(KT):
                act.wait_ge(evicted, B_OUT1 + k + 1)
                square(3, k)
            for k in range(KT):
                high_part(3, k)
            root(3)
            ff(B_FF1, 4, True)

            root(4)
            for k in range(KT):
                act.wait_ge(y_done, k + 1)
                dma(t["y"][k], x[:, k, :]).then_inc(y_out, 16)
            act.wait_ge(y_out, 16 * KT)
            act.wait_ge(g_out, 16)


F = "float32"
_SHAPES_IN = ["x", "wall", "cols", "mats", "cos", "sin", "kcache", "vcache", "conv_hist", "head_par", "qk_hist",
              "mem_in"]
_OUTS = {
    "y": (KT, P, T), "conv_p": (CT, P, HIST), "conv_s": (CT, P, NB, HIST), "v_p": (P, WIN), "v_s": (P, NB * TB),
    "v_old": (WIN - TB, NB, P), "k_p": (P, WIN), "k_s": (P, NB, WIN), "qk_p": (MH, 4, P, QH),
    "qk_s": (MH, 4, P, NB, QH), "mem_p": (MH, P, 2, MA), "mem_s": (MH, NB, P, 2 * MA), "m_out": (MH, 16),
    "x_spill": (KT, P, T), "mix_spill": (MH, P, 2, T),
}


def _lay_out(i):
    import numpy as np

    def by_k(w):
        n = w.shape[1] // P
        return w.reshape(KT, P, n, P).transpose(2, 1, 0, 3).reshape(n, P, KT * P)

    def channels(v):
        return np.asarray(v).reshape(-1, P).T

    a = {}
    x = np.concatenate([i["x_prompt"][0], i["x_sample"].reshape(NB * TB, D)])
    a["x"] = x.T.reshape(KT, P, T)
    w = i["w_in_even"][0]
    half = CT * P
    glu = w[:, 768:].reshape(D, 2, CT, P).transpose(0, 2, 1, 3).reshape(D, 2 * half)
    q = w[:, :512].reshape(D, 2, 4, HD).transpose(0, 2, 1, 3).reshape(D, 512)
    wo = i["w_out_even"][0]
    wo = np.concatenate([wo[:512].reshape(2, 4, HD, D).transpose(1, 0, 2, 3).reshape(512, D), wo[512:]])
    units = [by_k(glu), by_k(w[:, 512:768]), by_k(q), by_k(wo)]

    def ffn(layer):
        w1 = by_k(i["w_ff1"][layer]).reshape(FC, FK, P, KT * P)
        w2 = i["w_ff2"][layer].reshape(FC, FK, P, 4, 2, P).transpose(0, 3, 2, 4, 1, 5).reshape(FC, 4, P, KT * P)
        return np.concatenate([w1, w2], axis=1).reshape(FC * 8, P, KT * P)
    units.append(ffn(0))
    w = i["w_in_odd"][0]
    gates = np.zeros((D, P), w.dtype)
    gates[:, 0:MH] = w[:, 4 * D:4 * D + MH]
    gates[:, 32:32 + MH] = w[:, 4 * D + MH:]
    heads = w[:, :4 * D].reshape(D, 4, MH, MD)[:, [2, 1, 0, 3]].transpose(0, 2, 1, 3).reshape(D, 4 * D)
    units += [by_k(gates), by_k(heads), by_k(i["w_out_odd"][0]), ffn(1)]
    a["wall"] = np.concatenate(units)
    c = np.zeros((P, NCOL), np.float32)
    for n, g in enumerate([i["norm_mix_g"][0], i["norm_ffn_g"][0], i["norm_mix_g"][1], i["norm_ffn_g"][1],
                           i["norm_out_g"]]):
        c[:, C_G + KT * n:C_G + KT * (n + 1)] = channels(g)
    c[:, C_CW:C_CB] = i["conv_w"][0].reshape(CW, CT, P).transpose(2, 1, 0).reshape(P, CT * CW)
    c[:, C_CB:C_CB + CT] = channels(i["conv_b"][0])
    c[:, C_LG:C_LG + CT] = channels(i["conv_ln_g"][0])
    c[:, C_LB:C_LB + CT] = channels(i["conv_ln_b"][0])
    sink = i["attn_sink"][0]
    for p in range(2):
        for v in range(2):
            c[:, C_SINK + 2 * p + v] = np.repeat(sink[4 * v + 2 * p:4 * v + 2 * p + 2], CH)
    c[:, C_SINKS] = np.repeat(sink, TB)
    c[0:MH, C_GB] = i["gate_b_i"][0]
    c[32:32 + MH, C_GB] = i["gate_b_f"][0]
    c[:, C_BSEL:C_BSEL + NB] = np.repeat(np.eye(NB, dtype=np.float32), TB, axis=0)
    c[0:MH, C_M0:C_M0 + NB] = i["state_mlstm_m"][0].T
    c[:, C_POW] = MD * EPS
    c[:, C_POW + 1] = -0.5
    c[0:MH, C_MH:C_MH + MH * 16] = np.repeat(np.eye(MH, dtype=np.float32), 16, axis=1)
    a["cols"] = c
    m = np.zeros((P, NK, P), np.float32)
    m[:, K_ID] = np.eye(P)
    m[:, K_ONE] = 1
    for base in (0, HD):
        for r in range(8):
            m[base + 8 + r, K_PERM, base + r] = -1
            m[base + r, K_PERM, base + 8 + r] = 1
    at = np.arange(P)
    causal = at[:, None] <= at[None, :]
    m[:, K_CAUS] = np.where(causal, 0, NEG)
    m[:, K_BLK] = np.where(causal & (at[:, None] // TB == at[None, :] // TB), 0, NEG)
    a["mats"] = m
    pos = np.concatenate([np.arange(TP), np.tile(1024 + np.arange(TB), NB)]).astype(np.float32)
    inv = np.float32(500000.0) ** (-np.arange(8, dtype=np.float32) / np.float32(8))
    ang = inv[:, None] * pos[None, :]
    cos, sin = np.ones((P, T), np.float32), np.zeros((P, T), np.float32)
    for base in (0, 8, HD, HD + 8):
        cos[base:base + 8] = np.cos(ang)
        sin[base:base + 8] = np.sin(ang)
    a["cos"], a["sin"] = cos, sin
    a["kcache"] = i["cache_swa_k"][0].transpose(2, 3, 0, 1).reshape(P, NB, WIN)
    a["vcache"] = i["cache_swa_v"][0].transpose(1, 0, 2, 3).reshape(WIN, NB, P)
    a["conv_hist"] = i["state_conv"][0].reshape(NB, HIST, CT, P).transpose(2, 3, 0, 1)

    def by_head(v):
        v = np.asarray(v).reshape(v.shape[:-1] + (2, MH, 2, P))
        v = np.flip(v, -4)
        n = v.ndim
        v = np.moveaxis(v, (n - 3, n - 4, n - 2, n - 1), (0, 1, 2, 3))
        return v.reshape((MH, 4, P) + v.shape[4:])
    a["qk_hist"] = by_head(i["state_qk_conv"][0])
    hp = np.zeros((MH, P, NH), np.float32)
    hp[:, :, H_W:H_W + 16] = by_head(i["qk_conv_w"][0]).transpose(0, 2, 1, 3).reshape(MH, P, 16)
    hp[:, :, H_B:H_B + 4] = by_head(i["qk_conv_b"][0]).transpose(0, 2, 1)
    hp[:, :, H_G:H_G + 2] = i["mlstm_norm_g"][0].reshape(MH, 2, P).transpose(0, 2, 1)
    for h in range(MH):
        hp[h, h, H_SEL:] = 1
    a["head_par"] = hp
    mem = np.concatenate([i["state_mlstm_C"][0].transpose(0, 1, 3, 2), i["state_mlstm_n"][0][..., None]], axis=-1)
    a["mem_in"] = mem.reshape(NB, MH, 2, P, MA).transpose(1, 0, 3, 2, 4).reshape(MH, NB, P, 2 * MA)
    return {k: np.ascontiguousarray(v) for k, v in a.items()}


def _put_back(r):
    import numpy as np

    y = r["y"].reshape(D, T).T
    out = [y[:TP][None], y[TP:].reshape(NB, TB, D)]

    def heads(v):
        return v.T.reshape(1, 1, -1, 2, HD)
    kp, vp = heads(r["k_p"]), heads(r["v_p"])
    cp = r["conv_p"].transpose(2, 0, 1).reshape(1, 1, HIST, CT * P)

    def from_heads(v):
        v = v.reshape((MH, 2, 2, P) + v.shape[3:])
        n = v.ndim
        v = np.moveaxis(v, (0, 1, 2, 3), (n - 3, n - 4, n - 2, n - 1))
        v = np.flip(v, -4)
        return v.reshape(v.shape[:-4] + (2 * D,))
    qp = from_heads(r["qk_p"]).reshape(1, 1, QH, 2 * D)
    qs = from_heads(r["qk_s"]).reshape(1, NB, QH, 2 * D)
    mp = r["mem_p"].transpose(0, 2, 1, 3).reshape(1, 1, MH, MD, MA)
    ms = r["mem_s"].reshape(MH, NB, P, 2, MA).transpose(1, 0, 3, 2, 4).reshape(1, NB, MH, MD, MA)
    m = r["m_out"]
    ks = r["k_s"].reshape(2, HD, NB, WIN).transpose(2, 3, 0, 1)[None]
    vs = np.concatenate([r["v_old"].transpose(1, 0, 2), r["v_s"].reshape(P, NB, TB).transpose(1, 2, 0)], axis=1)
    vs = vs.reshape(1, NB, WIN, 2, HD)
    cs = r["conv_s"].transpose(2, 3, 0, 1).reshape(1, NB, HIST, CT * P)
    out += [kp, vp, cp, qp, mp[..., :MD].swapaxes(-1, -2), mp[..., MD], m[:, 7].reshape(1, 1, MH),
            ks, vs, cs, qs, ms[..., :MD].swapaxes(-1, -2), ms[..., MD], m[:, 8:].T.reshape(1, NB, MH)]
    return tuple(np.ascontiguousarray(o) for o in out)


def kernel(**inputs):
    import numpy as np
    import concourse.bacc as bacc
    from concourse.bass_utils import run_bass_kernel_spmd

    arrays = _lay_out({k: np.asarray(v) for k, v in inputs.items()})
    nc = bacc.Bacc("TRN2", target_bir_lowering=False, num_devices=1)
    t = {}
    for name, a in arrays.items():
        t[name] = nc.dram_tensor("in_" + name, a.shape, F32, kind="ExternalInput").ap()
    for name, shape in _OUTS.items():
        t[name] = nc.dram_tensor("out_" + name, shape, F32, kind="ExternalOutput").ap()
    build(nc, t)
    r = run_bass_kernel_spmd(nc, [{"in_" + k: v for k, v in arrays.items()}], core_ids=[0])
    return _put_back({name: r.results[0]["out_" + name] for name in _OUTS})
```

```python
import concourse.bass as bass
from concourse import mybir
from contextlib import ExitStack

F32 = mybir.dt.float32
F32R = mybir.dt.float32r
ALU = mybir.AluOpType
ACT = mybir.ActivationFunctionType
AX = mybir.AxisListType.X

P = 128
D = 1024
KT = D // P
TP = 1024
NB, TB = 8, 16
T = TP + NB * TB
NT = 3
TN = T // NT
EPS = 1e-6
NEG = -1e30

CH = 64
NCH = TP // CH
HD = 64
WIN = 128
SK = WIN + TB
ATT_SCALE = HD ** -0.5
CW = 31
HIST = CW - 1
CT = 4
EXT = HIST + TP + NB * (HIST + TB)
MH = 4
MD = 256
MA = MD + 1
LC = 128
NLC = TP // LC
QW = 4
QH = QW - 1
QEXT = QH + TP + NB * (QH + TB)
FC = 8
FK = 4

U_IN0, U_OUT0, U_FF0 = 0, 14, 22
U_GATE = U_FF0 + FC * 8
U_HEAD = U_GATE + 1
U_OUT1 = U_HEAD + MH * 8
U_FF1 = U_OUT1 + 8
N_UNITS = U_FF1 + FC * 8
B_IN0, B_OUT0, B_FF0 = 0, 14, 22
B_GATE = B_FF0 + FC * 12
B_HEAD = B_GATE + 1
B_OUT1 = B_HEAD + MH * 8
B_FF1 = B_OUT1 + 8
B_END = B_FF1 + FC * 12
FF_BLOCKS = [1, 2, 3, 4, 6, 8, 10, 12]

C_G = 0
C_CW = C_G + 5 * KT
C_CB = C_CW + CT * CW
C_LG = C_CB + CT
C_LB = C_LG + CT
C_SINK = C_LB + CT
C_SINKS = C_SINK + 4
C_GB = C_SINKS + 1
C_BSEL = C_GB + 1
C_M0 = C_BSEL + NB
C_POW = C_M0 + NB
C_MH = C_POW + 2
NCOL = C_MH + MH * 16
K_ID, K_ONE, K_PERM, K_CAUS, K_BLK = range(5)
NK = 5
H_W, H_B, H_G, H_SEL = 0, 16, 20, 22
NH = H_SEL + P
NCS = 4
CS_USES = NB // NCS
SEQ = list(range(NLC - 1)) + [NLC, NLC - 1]
STREAMS = [[b] for b in range(NLC - 2)] + [[NLC - 2, NLC - 1], [], []]
PIECE_BANK, STREAM_BANK = 6, 7
PIECES = 6
LAST_O = 2
RELOADED = [[], [0, 1], [2], [3], [4], [5]]
HT = 288
ONE = 1
NSINK = 2
GATE_TO_EXP, GATE_ROWS = 20, 21


LOW = 6 * EXT + T
HIGH = (NLC + 1) * MA + 2 * QEXT + 2 * NB * P + 2 * MA + NCS * 2 * MA


def build(nc, t):
    es = ExitStack()
    with es:
        def sb(name, shape, dt=F32):
            return es.enter_context(nc.sbuf_tensor(name, shape, dt))

        def sem(name):
            return es.enter_context(nc.semaphore(name))

        cols = sb("cols", [P, NCOL])
        mats = sb("mats", [P, NK, P])
        head_par = sb("head_par", [P, NH])
        w_raw = sb("w_raw", [P, 2, D])
        w_hi = sb("w_hi", [P, 2, D], F32R)
        w_lo = sb("w_lo", [P, 2, D], F32R)
        a_hi = sb("a_hi", [P, KT, T], F32R)
        with nc.sbuf_tensor("a_lo", [P, KT, T], F32R) as a_lo:
            pass
        back = sb("back", [P, KT, T])
        low = sb("low", [P, LOW])
        rbc = sb("rbc", [P, T])
        mid = sb("mid", [P, 6784])
        with nc.sbuf_tensor("h_hi", [P, FK, T], F32R) as h_hi, nc.sbuf_tensor("h_lo", [P, FK, T], F32R) as h_lo:
            pass
        high = sb("high", [P, HIGH])
        psum = es.enter_context(nc.psum_tensor("psum", [P, 8, 512], F32))

        ident = mats[:, K_ID, :]
        ones = mats[:, K_ONE, :]
        x = low[:, 0:KT * T].rearrange("p (k t) -> p k t", k=KT)

        def carve(buf):
            at = [0]

            def take(*shape):
                n = 1
                for s in shape:
                    n *= s
                v = buf[:, at[0]:at[0] + n]
                at[0] += n
                if len(shape) == 2:
                    v = v.rearrange("p (a b) -> p a b", a=shape[0])
                if len(shape) == 3:
                    v = v.rearrange("p (a b c) -> p a b c", a=shape[0], b=shape[1])
                return v
            return take

        take = carve(mid)
        ssq = take(T)
        sq = take(T)
        hid = take(T)
        take = carve(low)
        ext = take(CT + 1, EXT)
        vT = take(T)
        take = carve(high)
        qT = take(4, T)
        kT = take(T)
        v64 = take(NCH, P)
        kc = take(NB, SK)
        take = carve(mid)
        cos, sin, za, zs = take(T), take(T), take(T), take(T)
        vc = take(NB, P)
        v16 = take(NB, P)
        take = carve(mid)
        qs = take(2, 4, CH)
        qss = carve(mid)(NB, 4 * TB)
        pr = take(2, 2 * 192)
        pT = take(2, 6 * P)
        ob = take(2, P)
        obs = take(2, P)
        nsink = take(5)
        st = take(2, 16)
        lnsq = carve(mid)(CT, TN)
        take = carve(low)
        mq, mk, mo, mv = take(2, T), take(2, T), take(2, T), take(2, T)
        ks = take(MD)
        take = carve(high)
        vaug = take(NLC + 1, MA)
        qext = take(2, QEXT)
        qx = take(2, NB, P)
        cst = take(2, MA)
        csl = take(NCS, 2 * MA)
        high_end = sb("kwm", [P, 2, MD])
        take = carve(high)
        gz, gt, glf, gb, gg, gd, gm, gp = [take(T) for _ in range(8)]
        take = carve(mid)
        mix = take(2, T)
        mneg = take(T)
        rows = mix[:, 0, :]
        eM = take(2, P)
        sT = take(2, P)
        tB = take(2, MA + 1)
        num = take(2, MA + 1)
        kw = take(2, MD)
        hn = take(2, MD)
        kwm = high_end
        rtc = take(NLC + 1, 4, MH)
        rth = take(NLC + 1, 4)
        wc16 = take(16)
        wcb = take(MH, 16)
        wch = take(16)
        mend = take(16)
        ws8 = take(NB)
        sm = take(2, 8)
        wd = take(MH * 16)
        junk = take(MD)
        Q_INT, Q_WS, Q_G, Q_EM = range(4)

        cols_in, mats_in, cs_tab_in, cache_in, hist_in = [sem(n) for n in (
            "cols_in", "mats_in", "cos_sin_in", "cache_in", "hist_in")]
        x_in = [sem(f"x_in{k}") for k in range(KT)]
        w_in = [sem(f"w_in{s}") for s in range(2)]
        w_taken, w_high, w_split = sem("w_taken"), sem("w_high"), sem("w_split")
        block_done, evicted = sem("block_done"), sem("evicted")
        sq_done, ssq_copy, ssq_done = sem("sq_done"), sem("ssq_copy"), sem("ssq_done")
        aux_done, aux_read, rsum_done, rbc_done = [sem(n) for n in ("aux_done", "aux_read", "rsum_done", "rbc_done")]
        hi_done, lo_done, hsq_done, h_done = [sem(n) for n in ("hi_done", "lo_done", "hsq_done", "h_done")]
        pads, sig_done, ext_done, conv_done, rope_done, v_in_place, kc_done, kv_out = [sem(n) for n in (
            "pads", "sig_done", "ext_done", "conv_done", "rope_done", "v_in_place", "kc_done", "kv_out")]
        conv_out = [sem(f"conv_state_out{j}") for j in range(CT)]
        ln_centred, ln_sq, ln_v, ln_rstd, ln_scaled, ln_y, ln_hi, ln_lo = [sem("ln_" + n) for n in (
            "centred", "sq", "var", "rstd", "scaled", "y", "hi", "lo")]
        q_staged, s_done, stat_done, m_done, p_done, t_done, pt_done, pe_step, pv_done, den_done, o_done, ot_done, \
            ahi_done, mixed = [sem("att_" + n) for n in (
                "staged", "scores", "stat", "max", "probs", "tr", "tr_copied", "step", "pv", "den", "out", "out_tr",
                "hi", "mixed")]
        spilled, gates_act, gate_rows, g_out = sem("spilled"), sem("gates_act"), sem("gate_rows"), sem("gate_out")
        par_in, head_set, qconv, qsilu, osig, vtr, vcp = [sem("m_" + n) for n in (
            "par_in", "head_set", "conv", "silu", "ogate", "vtr", "vcopied")]
        qh_in = [sem(f"m_hist_in{i}") for i in range(4)]
        qh_out = [sem(f"m_hist_out{i}") for i in range(4)]
        es_done, e_done, st_done, intra_done, kw_done, ab_done, tb_done, num_done, c_done, cu_done, dn_done, ss_done, \
            sc_own, sc_done, hn_done, ht_done, mix_done = [sem("m_" + n) for n in (
                "scores", "decay", "gated", "intra", "kw", "numer", "inter_scaled", "num", "delta", "state", "den",
                "ss", "pow", "scale", "hn", "hT", "mix")]
        cs_in = [sem(f"m_cs_in{s}") for s in range(NCS)]
        cs_out = [sem(f"m_cs_out{s}") for s in range(NCS)]
        qx_done, kwm_done, csc_done, csu_done, cp_out, mix_out, mix_in = [sem("m_" + n) for n in (
            "qx", "kwm", "sample_delta", "sample_state", "prompt_out", "mix_out", "mix_in")]
        gact_own = sem("gates_act_own")
        piece_done, piece_out = sem("piece_done"), sem("piece_out")
        mix_back = [sem(f"mix_back{h}") for h in range(MH)]
        y_done, y_out = sem("y_done"), sem("y_out")

        block = es.enter_context(nc.Block())

        AX_R0, AX_KROPE, AX_V, AX_QROPE = 0, 3, 6, 12
        AX_LN = AX_QROPE + 4 * NT
        AX_R1 = AX_LN + 2 * NT
        AX_R2 = AX_R1 + NT
        AX_GT = AX_R2 + NT
        AX_WC = AX_GT + 3
        AX_R3 = AX_WC + 1
        AX_R4 = AX_R3 + NT

        def out3(b):
            s = 3 * (b % 2)
            return psum[:, s:s + 3, 0:TN]

        def by3(v):
            return v.rearrange("p (a b) -> p a b", a=NT)

        def gain(m, k):
            return cols[:, C_G + KT * m + k:C_G + KT * m + k + 1]

        def tok(i):
            return slice(i * TN, (i + 1) * TN)

        def sample(v, pre, width):
            return v.rearrange("p (b w) -> p b w", w=width)[:, :, pre:pre + TB]

        @block.sync
        def _(sp):
            def load(u, s, split):
                if split is not None:
                    sp.wait_ge(w_split, split)
                sp.dma_start(w_raw[:, s, :], t["wall"][u]).then_inc(w_in[s], 16)

            load(0, 0, None)
            load(1, 1, None)
            with sp.Fori(1, N_UNITS // 2) as i:
                for s in range(2):
                    load(2 * i + s, s, 2 * i + (s - 1))
            load(N_UNITS - 1, 0, N_UNITS - 2)

        @block.gpsimd
        def _(pool):
            def split(s, loads, units, used):
                pool.wait_ge(w_in[s], loads * 16)
                if used is not None:
                    pool.wait_ge(block_done, used)
                pool.sem_inc(w_taken, 1)
                nc.gpsimd.tensor_scalar(w_hi[:, s, :], w_raw[:, s, :], 1.0, 1.0, ALU.mult, ALU.mult)\
                    .then_inc(w_high, 1)
                pool.wait_ge(w_high, units)
                nc.gpsimd.tensor_tensor(w_lo[:, s, :], w_raw[:, s, :], w_hi[:, s, :].bitcast(F32), ALU.subtract)\
                    .then_inc(w_split, 1)

            def single(u, used):
                split(u % 2, u // 2 + 1, u + 1, used)

            def ff(u0, b0):
                before = [-1, 0] + FF_BLOCKS[:6]
                with pool.Fori(0, FC) as c:
                    for j in range(8):
                        u = u0 + j
                        split(u % 2, 4 * c + (u // 2 + 1), 8 * c + (u + 1), 12 * c + (b0 + before[j]))

            single(0, None)
            single(1, None)
            with pool.Fori(1, U_FF0 // 2) as i:
                for s in range(2):
                    split(s, i + 1, 2 * i + (s + 1), 2 * i + (s - 1))
            ff(U_FF0, B_FF0)
            single(U_GATE, B_GATE - 2)
            single(U_HEAD, B_GATE)
            single(U_HEAD + 1, B_GATE + 1)
            pool.wait_ge(cols_in, 16)
            for j in (2, 3):
                single(U_HEAD + j, B_HEAD + j - 1)

            def head(h, last):
                def head_unit(j):
                    u = U_HEAD + j
                    split(u % 2, 4 * h + (u // 2 + 1), 8 * h + (u + 1), 8 * h + (B_HEAD + j - 1))

                for j in range(4, 8):
                    head_unit(j)
                for p in range(NLC + 1):
                    s = p % 2
                    pool.wait_ge(ss_done, 9 * h + (p + 1))
                    nc.gpsimd.tensor_tensor(sm[:, s, 4:5], sm[:, s, 3:4], cols[:, C_POW:C_POW + 1], ALU.add)\
                        .then_inc(sc_own, 1)
                    pool.wait_ge(sc_own, 18 * h + (2 * p + 1))
                    nc.gpsimd.tensor_tensor(sm[:, s, 5:6], sm[:, s, 4:5], cols[:, C_POW + 1:C_POW + 2], ALU.pow)\
                        .then_inc(sc_own, 1)
                    pool.wait_ge(sc_own, 18 * h + (2 * p + 2))
                    nc.gpsimd.tensor_tensor(sm[:, s, 6:7], sm[:, s, 5:6], sm[:, s, 2:3], ALU.mult)\
                        .then_inc(sc_done, 1)
                    if p in (1, 2):
                        head_unit(p + 7)
                    if p in (7, 8) and not last:
                        head_unit(p + 3)

            with pool.Fori(0, MH - 1) as h:
                head(h, False)
            head(MH - 1, True)
            with pool.Fori(0, 3) as i:
                for s in range(2):
                    u = U_OUT1 + 2 + s
                    split(u % 2, i + (u // 2 + 1), 2 * i + (u + 1), 2 * i + (B_OUT1 + s + 1))
            ff(U_FF1, B_FF1)

        @block.tensor
        def _(pe):
            mm = nc.tensor.matmul
            tr = nc.tensor.transpose

            def passes(s, k, kk, b, hi, lo, first, last):
                z = 3 * (b % 2)
                n = 0
                for w, a in ((w_hi, hi), (w_hi, lo), (w_lo, hi)):
                    for i in range(NT):
                        r = mm(psum[:, z + i, 0:TN], w[:, s, k * P:(k + 1) * P], a[:, kk, tok(i)],
                               start=first and n == 0, stop=last and n == 2)
                    n += 1
                return r

            def unit(s, units, b, free, ready=None):
                pe.wait_ge(w_split, units)
                if free is not None:
                    pe.wait_ge(evicted, free)
                for k in range(KT):
                    if ready is not None:
                        ready(k)
                    r = passes(s, k, k, b, a_hi, a_lo, k == 0, k == KT - 1)
                r.then_inc(block_done, 1)

            def aux(n, cells, done=True):
                if n >= 2:
                    pe.wait_ge(aux_read, n - 1)
                bank = 6 + n % 2
                for c in cells:
                    if len(c) == 3:
                        lo_, hi_, (a, b_, st_, sp_) = c
                        r = mm(psum[:, bank, lo_:hi_], a, b_, start=st_, stop=sp_)
                    else:
                        rows_, lo_, hi_, a = c
                        r = tr(psum[0:rows_, bank, lo_:hi_], a, ident)
                r.then_inc(aux_done, 1)

            def token_sums(n, m):
                pe.wait_ge(ssq_done, KT * (m + 1))
                for i in range(NT):
                    aux(n + i, [(0, TN, (ones, ssq[:, tok(i)], True, True))])

            def split_ready(base):
                def ready(k):
                    pe.wait_ge(lo_done, base + k + 1)
                return ready

            def ff(u0, b0, base):
                with pe.Fori(0, FC) as c:
                    for j in range(FK):
                        u, b = u0 + j, b0 + j
                        unit(u % 2, 8 * c + (u + 1), b, 12 * c + (b - 1), split_ready(base) if j == 0 else None)
                    for j in range(4):
                        u = u0 + FK + j
                        pe.wait_ge(w_split, 8 * c + (u + 1))
                        for o in range(2):
                            b = b0 + FK + 2 * j + o
                            pe.wait_ge(evicted, 12 * c + (b - 1))
                            for k in range(FK):
                                if j == 0 and o == 0:
                                    pe.wait_ge(h_done, FK * c + (FK * FC * (b0 > B_GATE) + k + 1 + ONE))
                                r = passes(u % 2, FK * o + k, k, b, h_hi, h_lo, k == 0, k == FK - 1)
                            r.then_inc(block_done, 1)

            pe.wait_ge(mats_in, 16)
            unit(0, 1, 0, None, split_ready(0))
            token_sums(AX_R0, 0)
            unit(1, 2, 1, None)
            with pe.Fori(1, 5) as i:
                for s in range(2):
                    unit(s, 2 * i + (s + 1), s, 2 * i + (s - 1))

            def rope(n, b, src):
                pe.wait_ge(evicted, b + 1)
                for i in range(NT):
                    aux(n + i, [(0, TN, (mats[:, K_PERM, :], src[:, tok(i)], True, True))])

            unit(0, 11, 10, 9)
            rope(AX_KROPE, 8, kT)
            pe.wait_ge(evicted, 10)
            for g in range(4):
                aux(AX_V + g, [(CH, P * i, P * i + P, vT[:, CH * (4 * g + i):CH * (4 * g + i + 1)]) for i in range(4)])
            for g in range(2):
                aux(AX_V + 4 + g, [(TB, P * i, P * i + P, vT[:, TP + TB * (4 * g + i):TP + TB * (4 * g + i + 1)])
                                   for i in range(4)])
            for j in range(1, 4):
                unit((10 + j) % 2, 11 + j, 10 + j, 9 + j)
                rope(AX_QROPE + NT * (j - 1), 9 + j, qT[:, j - 1, :])
            rope(AX_QROPE + NT * 3, 13, qT[:, 3, :])

            pe.wait_ge(conv_done, CT * 2 * CW)
            for i in range(NT):
                aux(AX_LN + i, [(0, TN, (ones, ext[:, j, tok(i)], j == 0, j == CT - 1)) for j in range(CT)])
            for i in range(NT):
                pe.wait_ge(ln_sq, i + 1)
                aux(AX_LN + NT + i, [(0, TN, (ones, lnsq[:, j, :], j == 0, j == CT - 1)) for j in range(CT)])

            def blocks_of(c):
                return c + 1 if isinstance(c, int) and c < 2 else 3

            def scores(c, p):
                if p == 0:
                    pe.wait_ge(q_staged, c + 1)
                if not (isinstance(c, int) and c == 0):
                    pe.wait_ge(p_done, 2 * c + p - 1)
                nb = blocks_of(c)
                for v in range(2):
                    r = mm(psum[:, p, 192 * v:192 * v + CH * nb], qs[:, v, 2 * p:2 * p + 2, :],
                           kT[:, bass.ds(CH * c - CH * (nb - 1), CH * nb)], start=True, stop=True)
                r.then_inc(s_done, 1)

            def flip(c, p):
                pe.wait_ge(p_done, 2 * c + p + 1)
                if not (isinstance(c, int) and c == 0):
                    pe.wait_ge(pt_done, 2 * c + p - 1)
                pe.sem_inc(pe_step, 1)
                nb = blocks_of(c)
                for v in range(2):
                    for i in range(nb):
                        e = 3 * v + i
                        r = tr(psum[0:CH, 2 + 2 * p + e // 4, P * (e % 4):P * (e % 4) + P],
                               pr[:, p, 192 * v + CH * i:192 * v + CH * (i + 1)], ident)
                r.then_inc(t_done, 1)

            def weigh(c, p):
                pe.wait_ge(pt_done, 2 * c + p + 1)
                if not (isinstance(c, int) and c == 0):
                    pe.wait_ge(mixed, 2 * c + p - 1)
                pe.sem_inc(pe_step, 1)
                nb = blocks_of(c)
                for v in range(2):
                    for i in range(nb):
                        e = 3 * v + i
                        r = mm(psum[:, 6 + p, HD * v:HD * v + HD], pT[0:CH, p, P * e:P * e + P],
                               v64[0:CH, c - (nb - 1) + i, HD * v:HD * v + HD], start=i == 0, stop=i == nb - 1)
                r.then_inc(pv_done, 1)

            def flip_out(n, p, src):
                pe.wait_ge(o_done, n + 1)
                tr(psum[:, 6 + p, P:2 * P], src[:, p, :], ident).then_inc(ot_done, 1)

            def step(c, first=False):
                scores(c, 0)
                scores(c, 1)
                if not first:
                    weigh(c - 1, 0)
                    weigh(c - 1, 1)
                flip(c, 0)
                if not first:
                    flip_out(2 * c - 2, 0, ob)
                flip(c, 1)
                if not first:
                    flip_out(2 * c - 1, 1, ob)

            pe.wait_ge(evicted, B_OUT0)
            pe.wait_ge(aux_read, AX_R1)
            step(0, True)
            step(1)
            step(2)
            with pe.Fori(3, NCH) as c:
                step(c)
            for p in range(2):
                weigh(NCH - 1, p)
            for p in range(2):
                flip_out(2 * NCH - 2 + p, p, ob)

            pe.wait_ge(cache_in, 32)
            pe.wait_ge(kc_done, 1)
            pe.wait_ge(q_staged, NCH + 1)

            def s_scores(b, s, n):
                pe.wait_ge(p_done, n - 1)
                for v in range(2):
                    h_ = slice(HD * v, HD * v + HD)
                    r = mm(psum[h_, s, 0:SK], qss[h_, b, :], kc[h_, b, :],
                           start=True, stop=True)
                r.then_inc(s_done, 1)

            def s_flip(b, s, n):
                pe.wait_ge(p_done, n + 1)
                pe.wait_ge(pt_done, n - 1)
                tr(psum[:, 2 + 2 * s, 0:P], pr[:, s, 0:P], ident)
                tr(psum[0:TB, 2 + 2 * s, P:2 * P], pr[:, s, P:SK], ident).then_inc(t_done, 1)

            def s_weigh(b, s, n):
                pe.wait_ge(pt_done, n + 1)
                pe.wait_ge(mixed, n - 1)
                for v in range(2):
                    h_ = slice(HD * v, HD * v + HD)
                    mm(psum[h_, 6 + s, 0:HD], pT[:, s, h_], vc[:, b, h_], start=True, stop=False)
                    r = mm(psum[h_, 6 + s, 0:HD], pT[0:TB, s, P + HD * v:P + HD * v + HD], v16[0:TB, b, h_],
                           start=False, stop=True)
                r.then_inc(pv_done, 1)

            for b in range(NB + 1):
                n, s = 2 * NCH + b, b % 2
                if b < NB:
                    s_scores(b, s, n)
                if b > 0:
                    s_weigh(b - 1, 1 - s, n - 1)
                if b < NB:
                    s_flip(b, s, n)
                if b > 0:
                    flip_out(n - 1, 1 - s, obs)

            pe.wait_ge(mixed, 2 * NCH + NB)
            pe.wait_ge(ln_lo, NT)
            with pe.Fori(0, 4) as i:
                for s in range(2):
                    unit(s, 2 * i + (U_OUT0 + s + 1), s, 2 * i + (B_OUT0 + s - 1))
            token_sums(AX_R1, 1)
            ff(U_FF0, B_FF0, KT)

            token_sums(AX_R2, 2)
            unit(0, U_GATE + 1, B_GATE, B_GATE - 1, split_ready(2 * KT))
            for j in range(2):
                unit((U_HEAD + j) % 2, U_HEAD + j + 1, B_HEAD + j, B_HEAD + j - 1)
            pe.wait_ge(gates_act, 4)
            for g in range(3):
                aux(AX_GT + g, [(P, P * i, P * i + P, rows[:, P * (4 * g + i):P * (4 * g + i + 1)])
                                for i in range(min(4, NLC + 1 - 4 * g))])
            pe.wait_ge(gate_rows, GATE_ROWS)
            aux(AX_WC, [(0, MH * 16, (ones[0:MH, :], wd[0:MH, :], True, True))])
            pe.wait_ge(aux_read, AX_R3)

            def head(h, last):
                def turn(n, src):
                    if n >= 2:
                        pe.wait_ge(vcp, 10 * h + (n - 1))
                    for j in range(2):
                        r = tr(psum[:, 6 + n % 2, P * j:P * j + P], src(j), ident)
                    r.then_inc(vtr, 1)

                pe.wait_ge(mix_done, 9 * h + ONE)
                pe.wait_ge(csu_done, 8 * h + ONE)
                for j in range(2, 6):
                    b = B_HEAD + j
                    unit((U_HEAD + j) % 2, 8 * h + (U_HEAD + j + 1), b, 8 * h + (b - 1))
                    if j == 2:
                        pe.wait_ge(evicted, 8 * h + (B_HEAD + 2))
                    for n in range(2 * j - 4, 2 * j - 2 + (j == 5)):
                        turn(n, lambda i: mv[:, i, LC * n:LC * (n + 1)])
                pe.wait_ge(qsilu, 4 * h + 2)
                turn(NLC + 1, lambda i: mk[:, i, TP:T])
                b = B_HEAD + 6
                unit((U_HEAD + 6) % 2, 8 * h + (U_HEAD + 7), b, 8 * h + (b - 1))
                pe.wait_ge(vcp, 10 * h + 10)
                pe.wait_ge(qsilu, 4 * h + 4)
                pe.wait_ge(par_in, 16 * h + 16)

                def piece(m):
                    if last and m > 2:
                        return
                    i, j = (m, 7) if m < 3 else ((m - 3) // 2, 8 + (m - 3) % 2)
                    s = (U_HEAD + j) % 2
                    if i == 0:
                        pe.wait_ge(w_split, 8 * h + (U_HEAD + j + 1))
                    if m in (3, 8):
                        pe.wait_ge(evicted, 8 * h + (B_HEAD + (8 if m == 3 else 9)))
                    elif m > 0:
                        pe.wait_ge(piece_out, PIECES * h + (m - (m > 3)))
                    for k in range(KT):
                        for q, (w, a) in enumerate(((w_hi, a_hi), (w_hi, a_lo), (w_lo, a_hi))):
                            r = mm(psum[:, PIECE_BANK, 0:TN], w[:, s, k * P:(k + 1) * P], a[:, k, tok(i)],
                                   start=k == 0 and q == 0, stop=k == KT - 1 and q == 2)
                    r.then_inc(piece_done if i < 2 else block_done, 1)

                def scores(p):
                    c, s = SEQ[p], p % 2
                    if p >= 2:
                        pe.wait_ge(st_done, 9 * h + (p - 1))
                        pe.wait_ge(kw_done, 8 * h + (p - 1 if p < NLC else NLC - 1))
                    q = slice(LC * c, LC * (c + 1))
                    mm(psum[:, s, 0:P], head_par[0:MH, H_SEL:H_SEL + P], mneg[0:MH, q], start=True, stop=False)
                    mm(psum[:, s, 0:P], ident, mats[:, K_CAUS if c < NLC else K_BLK, :], start=False, stop=True)
                    for k in range(2):
                        r = mm(psum[:, s, P:2 * P], mk[:, k, q], mq[:, k, q], start=k == 0, stop=k == 1)
                    if c < NLC:
                        for k in range(2):
                            r = tr(psum[:, s, 2 * P + P * k:3 * P + P * k], mk[:, k, q], ident)
                    r.then_inc(es_done, 1)

                def intra(p):
                    pe.wait_ge(st_done, 9 * h + (p + 1))
                    if p >= 1:
                        pe.wait_ge(num_done, 9 * h + p)
                    if p >= 2:
                        pe.wait_ge(mix_done, 9 * h + (p - 1 + ONE))
                    mm(psum[:, 2, 0:MA], sT[:, p % 2, :], vaug[:, SEQ[p], :], start=True, stop=True)\
                        .then_inc(intra_done, 1)

                def stream(b, c, first):
                    s = b % NCS
                    pe.wait_ge(cs_in[s], 16 * CS_USES * h + 16 * (b // NCS + 1))
                    for k in range(2):
                        r = mm(psum[:, STREAM_BANK, 0:MA], qx[:, k, b, :], csl[:, s, MA * k:MA * (k + 1)],
                               start=b == 0 and k == 0, stop=b == NB - 1 and k == 1)
                    if b == NB - 1:
                        r.then_inc(ab_done, 1)
                    pe.wait_ge(kwm_done, 8 * h + (b + 1))
                    if first:
                        pe.wait_ge(cu_done, 9 * h + (c + 2))
                    else:
                        pe.wait_ge(csu_done, 8 * h + (b + ONE))
                    for k in range(2):
                        r = mm(psum[:, 4 + k, 0:MA], kwm[:, b % 2, P * k:P * k + P], vaug[:, NLC, :],
                               start=True, stop=True)
                    r.then_inc(csc_done, 1)

                def hidden_back(p):
                    pe.wait_ge(hn_done, 9 * h + (p + 1))
                    if p >= 1:
                        pe.wait_ge(mix_done, 9 * h + (p + ONE))
                    pe.wait_ge(num_done, 9 * h + min(p + 2, NLC + 1))
                    pe.wait_ge(tb_done, 9 * h + min(p + 2, NLC + 1))
                    for k in range(2):
                        r = tr(psum[:, 2 + k, HT:HT + P], hn[:, p % 2, P * k:P * k + P], ident)
                    r.then_inc(ht_done, 1)

                scores(0)
                pe.wait_ge(qx_done, h + 1)
                pe.wait_ge(evicted, 8 * h + (B_HEAD + 7))
                for p in range(NLC + 1):
                    c = SEQ[p]
                    q = slice(LC * c, LC * (c + 1))
                    if p < NLC:
                        scores(p + 1)
                        piece(p)
                    intra(p)
                    if c < NLC:
                        pe.wait_ge(cu_done, 9 * h + (c + 1))
                        if p >= 1:
                            pe.wait_ge(tb_done, 9 * h + p)
                        for k in range(2):
                            r = mm(psum[:, 3, 0:MA], mq[:, k, q], cst[:, k, :], start=k == 0, stop=k == 1)
                        r.then_inc(ab_done, 1)
                        pe.wait_ge(kw_done, 8 * h + (c + 1))
                        if c >= 1:
                            pe.wait_ge(csu_done, 8 * h + (min(c + (c == NLC - 1), NB) + ONE))
                        for k in range(2):
                            r = mm(psum[:, 4 + k, 0:MA], kw[:, c % 2, P * k:P * k + P], vaug[:, c, :],
                                   start=True, stop=True)
                        r.then_inc(c_done, 1)
                    for b in STREAMS[p]:
                        stream(b, c, b == STREAMS[p][0])
                    if p >= 1:
                        hidden_back(p - 1)
                piece(NLC)
                hidden_back(NLC)

            with pe.Fori(0, MH - 1) as h:
                head(h, False)
            head(MH - 1, True)

            pe.wait_ge(mix_done, 9 * MH + ONE)
            pe.wait_ge(csu_done, 8 * MH + ONE)
            for j in range(8):
                u, b = U_OUT1 + j, B_OUT1 + j
                unit(u % 2, u + 1, b, b - 1, split_ready(3 * KT) if j == 0 else None)
            token_sums(AX_R3, 3)
            ff(U_FF1, B_FF1, 4 * KT)
            token_sums(AX_R4, 4)

        @block.vector
        def _(dve):
            V = nc.vector
            for counted in [h_done, mix_done, csu_done, mix_out, cp_out] + cs_out + qh_out:
                dve.sem_inc(counted, ONE)

            def rest(m, k, n, src=None, g=None):
                dve.wait_ge(hi_done, n)
                src = x[:, k, :] if src is None else src
                V.scalar_tensor_tensor(out=a_lo[:, k, :], in0=src, scalar=1.0 if m is None else gain(m, k),
                                       in1=a_hi[:, k, :].bitcast(F32), op0=ALU.mult, op1=ALU.subtract)\
                    .then_inc(lo_done, 1)

            def add_squares(m, k):
                n = KT * m + k
                dve.wait_ge(sq_done, n + 1)
                q = (sq, hid)[k % 2]
                if k == 0:
                    V.tensor_copy(ssq[:, :], q).then_inc(ssq_done, 1)
                else:
                    dve.wait_ge(ssq_done, n)
                    V.tensor_tensor(ssq[:, :], ssq[:, :], q, ALU.add).then_inc(ssq_done, 1)

            def token_scale(n, m):
                for i in range(NT):
                    dve.wait_ge(aux_done, n + i + 1)
                    V.tensor_scalar(rbc[:, tok(i)], psum[:, 6 + (n + i) % 2, 0:TN], 1.0 / D, EPS, ALU.mult, ALU.add)\
                        .then_inc(aux_read, 1)
                dve.wait_ge(aux_read, n + NT)
                V.reciprocal(rbc[:, :], rbc[:, :]).then_inc(rsum_done, 1)
                dve.wait_ge(rbc_done, m + 1)

            def project(b, dst):
                dve.wait_ge(block_done, b + 1)
                V.tensor_tensor(by3(dst), out3(b), by3(rbc[:, :]), ALU.mult).then_inc(evicted, 1)

            def residual(b, count, k, x_ready=None):
                dve.wait_ge(block_done, count)
                if x_ready is not None:
                    dve.wait_ge(x_in[k], x_ready)
                V.tensor_tensor(by3(x[:, k, :]), out3(b), by3(x[:, k, :]), ALU.add).then_inc(evicted, 1)

            def ff(b0, m, last):
                hb = FK * FC * (b0 > B_GATE)

                def up(c, j):
                    dve.wait_ge(block_done, 12 * c + (b0 + j + 1))
                    dve.wait_ge(h_done, FK * c + (hb + j + ONE))
                    V.scalar_tensor_tensor(out=by3(hid), in0=out3(b0 + j), scalar=0.0, in1=by3(rbc[:, :]),
                                           op0=ALU.max, op1=ALU.mult).then_inc(evicted, 1)
                    dve.wait_ge(hsq_done, FK * c + (hb + j + 1))
                    V.tensor_tensor(h_lo[:, j, :], hid, h_hi[:, j, :].bitcast(F32), ALU.subtract).then_inc(h_done, 1)

                with dve.Fori(0, FC - 1) as c:
                    for j in range(FK):
                        up(c, j)
                    for k in range(KT):
                        residual(b0 + FK + k, 12 * c + (b0 + FK + k + 1), k)
                for j in range(FK):
                    up(FC - 1, j)
                for k in range(KT):
                    residual(b0 + FK + k, 12 * (FC - 1) + (b0 + FK + k + 1), k)
                    if not last:
                        rest(m, k, (m if m < 3 else m + 1) * KT + k + 1)
                    add_squares(m, k)

            dve.wait_ge(cols_in, 16)
            dve.wait_ge(mats_in, 16)
            for k in range(KT):
                rest(0, k, k + 1)
                add_squares(0, k)
            V.memset(ext[:, 1:CT + 1, 0:HIST], 0.0).then_inc(pads, 1)
            token_scale(AX_R0, 0)

            def glu(j):
                project(2 * j, za)
                project(2 * j + 1, zs)
                dve.wait_ge(sig_done, j + 1)
                e = ext[:, j + 1, :]
                V.tensor_tensor(e[:, HIST:HIST + TP], za[:, 0:TP], zs[:, 0:TP], ALU.mult)
                V.tensor_tensor(sample(e[:, HIST + TP:EXT], HIST, HIST + TB), sample(za[:, TP:T], 0, TB),
                                sample(zs[:, TP:T], 0, TB), ALU.mult).then_inc(ext_done, 1)

            def conv(j, first, last):
                src, dst = ext[:, j + 1, :], ext[:, j, :]
                sdst = sample(dst[:, TP:T], 0, TB)
                ssrc = src[:, HIST + TP:EXT].rearrange("p (b w) -> p b w", w=HIST + TB)
                n = 2 * CW * j
                if first == 0:
                    w = cols[:, C_CW + CW * j:C_CW + CW * j + 1]
                    cb = cols[:, C_CB + j:C_CB + j + 1]
                    dve.wait_ge(ext_done, j + 1)
                    dve.wait_ge(pads, 1)
                    dve.wait_ge(hist_in, 16 * CT)
                    if j > 0:
                        dve.wait_ge(conv_done, n)
                        dve.wait_ge(conv_out[j - 1], 32)
                    V.tensor_scalar(dst[:, 0:TP], src[:, 0:TP], w, cb, ALU.mult, ALU.add).then_inc(conv_done, 1)
                    V.tensor_scalar(sdst, ssrc[:, :, 0:TB], w, cb, ALU.mult, ALU.add).then_inc(conv_done, 1)
                    first = 1
                with dve.Fori(first, last) as r:
                    w = cols[:, bass.ds(r + (C_CW + CW * j), 1)]
                    dve.wait_ge(conv_done, 2 * r + (n - 1))
                    V.scalar_tensor_tensor(out=dst[:, 0:TP], in0=src[:, bass.ds(r, TP)], scalar=w,
                                           in1=dst[:, 0:TP], op0=ALU.mult, op1=ALU.add).then_inc(conv_done, 1)
                    dve.wait_ge(conv_done, 2 * r + n)
                    V.scalar_tensor_tensor(out=sdst, in0=ssrc[:, :, bass.ds(r, TB)], scalar=w,
                                           in1=sdst, op0=ALU.mult, op1=ALU.add).then_inc(conv_done, 1)

            def rope(n, dst, tile):
                for i in range(NT):
                    dve.wait_ge(aux_done, n + i + 1)
                    V.tensor_tensor(za[:, tok(i)], psum[:, 6 + (n + i) % 2, 0:TN], sin[:, tok(i)], ALU.mult)\
                        .then_inc(aux_read, 1)
                    V.tensor_tensor(dst[:, tok(i)], dst[:, tok(i)], cos[:, tok(i)], ALU.mult).then_inc(rope_done, 1)
                    dve.wait_ge(aux_read, n + i + 1)
                    dve.wait_ge(rope_done, 2 * (NT * tile + i) + 1)
                    V.tensor_tensor(dst[:, tok(i)], dst[:, tok(i)], za[:, tok(i)], ALU.add).then_inc(rope_done, 1)

            glu(0)
            conv(0, 0, 12)
            glu(1)
            conv(0, 12, 26)
            glu(2)
            conv(0, 26, CW)
            conv(1, 0, 9)
            glu(3)
            conv(1, 9, 16)
            project(8, kT)
            conv(1, 16, 23)
            project(9, vT)
            conv(1, 23, 30)
            project(10, qT[:, 0, :])
            dve.wait_ge(cs_tab_in, 32)
            rope(AX_KROPE, kT, 0)
            for g in range(6):
                dve.wait_ge(aux_done, AX_V + g + 1)
                n, dst = (CH, v64[0:CH, 4 * g:4 * g + 4, :]) if g < 4 else (TB, v16[0:TB, 4 * g - 16:4 * g - 12, :])
                V.tensor_copy(dst, psum[0:n, 6 + g % 2, :].rearrange("p (a b) -> p a b", a=4)).then_inc(aux_read, 1)
            dve.wait_ge(cache_in, 32)
            dve.wait_ge(rope_done, 2 * NT)
            V.tensor_copy(kc[:, :, WIN:SK], sample(kT[:, TP:T], 0, TB)).then_inc(kc_done, 1)
            project(11, qT[:, 1, :])
            rope(AX_QROPE, qT[:, 0, :], 1)
            conv(1, 30, CW)
            conv(2, 0, 4)
            project(12, qT[:, 2, :])
            rope(AX_QROPE + NT, qT[:, 1, :], 2)
            conv(2, 4, 9)
            project(13, qT[:, 3, :])
            rope(AX_QROPE + 2 * NT, qT[:, 2, :], 3)
            rope(AX_QROPE + 3 * NT, qT[:, 3, :], 4)
            conv(2, 9, CW)
            conv(3, 0, CW)

            rows_v = zs[:, :]
            dve.wait_ge(conv_done, 2 * CT * CW)
            for i in range(NT):
                dve.wait_ge(aux_done, AX_LN + i + 1)
                for j in range(CT):
                    r = V.scalar_tensor_tensor(out=ext[:, j, tok(i)], in0=psum[:, 6 + (AX_LN + i) % 2, 0:TN],
                                               scalar=-1.0 / (CT * P), in1=ext[:, j, tok(i)],
                                               op0=ALU.mult, op1=ALU.add)
                r.then_inc(aux_read, 1)
            for i in range(NT):
                n = AX_LN + NT + i
                dve.wait_ge(aux_done, n + 1)
                V.tensor_scalar(rows_v[:, tok(i)], psum[:, 6 + n % 2, 0:TN], 1.0 / (CT * P), EPS, ALU.mult, ALU.add)\
                    .then_inc(aux_read, 1)
                dve.wait_ge(aux_read, n + 1)
                V.reciprocal(rows_v[:, tok(i)], rows_v[:, tok(i)]).then_inc(ln_v, 1)
            for i in range(NT):
                dve.wait_ge(ln_rstd, i + 1)
                V.tensor_tensor(ext[:, 0:CT, tok(i)], ext[:, 0:CT, tok(i)],
                                rows_v[:, tok(i)].unsqueeze(1).to_broadcast([P, CT, TN]), ALU.mult)\
                    .then_inc(ln_scaled, 1)
            for i in range(NT):
                dve.wait_ge(ln_hi, i + 1)
                V.tensor_tensor(a_lo[:, CT:2 * CT, tok(i)], ext[:, 0:CT, tok(i)],
                                a_hi[:, CT:2 * CT, tok(i)].bitcast(F32), ALU.subtract).then_inc(ln_lo, 1)

            def stage(c):
                if not (isinstance(c, int) and c == 0):
                    dve.wait_ge(s_done, 2 * c)
                for v in range(2):
                    h_ = slice(HD * v, HD * v + HD)
                    r = V.tensor_scalar(qs[h_, v, :, :], qT[h_, :, bass.ds(CH * c, CH)], 1.0, None, ALU.mult)
                r.then_inc(q_staged, 1)

            def maxima(n, p, src, width, col):
                dve.wait_ge(s_done, n + 1)
                if not (isinstance(n, int) and n < 2):
                    dve.wait_ge(p_done, n - 1)
                V.tensor_reduce(st[:, p, 0:width], src, AX, ALU.max).then_inc(stat_done, 1)
                dve.wait_ge(stat_done, 2 * n + (NSINK + 1))
                V.scalar_tensor_tensor(out=st[:, p, 2:2 + width], in0=st[:, p, 0:width], scalar=-ATT_SCALE,
                                       in1=nsink[:, col:col + width], op0=ALU.mult, op1=ALU.min)\
                    .then_inc(stat_done, 1)
                dve.wait_ge(stat_done, 2 * n + (NSINK + 2))
                V.tensor_tensor(st[:, p, 4:4 + width], st[:, p, 2:2 + width],
                                cols[:, C_SINK + col:C_SINK + col + width], ALU.add).then_inc(m_done, 1)

            def denominators(n, p, width):
                dve.wait_ge(pv_done, n + 1)
                dve.wait_ge(p_done, n + 1)
                V.tensor_tensor(st[:, p, 8:8 + width], st[:, p, 6:6 + width], st[:, p, 10:10 + width], ALU.add)\
                    .then_inc(den_done, 1)
                dve.wait_ge(den_done, 2 * n + 1)
                V.reciprocal(st[:, p, 12:12 + width], st[:, p, 8:8 + width]).then_inc(den_done, 1)
                dve.wait_ge(den_done, 2 * n + 2)
                if not (isinstance(n, int) and n < 2):
                    dve.wait_ge(ot_done, n - 1)

            def output(n, p):
                denominators(n, p, 2)
                V.tensor_tensor(ob[:, p, :].rearrange("p (v d) -> p v d", v=2),
                                psum[:, 6 + p, 0:P].rearrange("p (v d) -> p v d", v=2),
                                st[:, p, 12:14].unsqueeze(2).to_broadcast([P, 2, HD]), ALU.mult).then_inc(o_done, 1)

            def mixed_in(c, p):
                n = 2 * c + p
                dve.wait_ge(ot_done, n + 1)
                src = psum[:, 6 + p, P:2 * P].rearrange("p (j q) -> p j q", j=2)
                at = bass.ds(CH * c, CH)
                V.tensor_scalar(a_hi[:, 2 * p:2 * p + 2, at], src, 1.0, None, ALU.mult).then_inc(ahi_done, 1)
                dve.wait_ge(ahi_done, n + 1)
                V.tensor_tensor(a_lo[:, 2 * p:2 * p + 2, at], src, a_hi[:, 2 * p:2 * p + 2, at].bitcast(F32),
                                ALU.subtract).then_inc(mixed, 1)

            def chunk_width(c):
                return CH * (c + 1) if isinstance(c, int) and c < 2 else 3 * CH

            def astep(c, first=False, more=True):
                w = chunk_width(c)
                for p in range(2):
                    maxima(2 * c + p, p, psum[:, p, 0:384].rearrange("p (v k) -> p v k", v=2)[:, :, 0:w], 2, 2 * p)
                if more:
                    stage(c + 1)
                if not first:
                    for p in range(2):
                        output(2 * c - 2 + p, p)
                    for p in range(2):
                        mixed_in(c - 1, p)

            V.memset(qs[:, :, :, :], 0.0).then_inc(stat_done, 1)
            V.memset(obs[:, :, :], 0.0)
            V.tensor_scalar(nsink, cols[:, C_SINK:C_SINK + 5], -1.0, None, ALU.mult).then_inc(stat_done, 1)
            dve.wait_ge(stat_done, NSINK)
            stage(0)
            astep(0, True)
            astep(1)
            astep(2)
            with dve.Fori(3, NCH - 1) as c:
                astep(c)
            astep(NCH - 1, more=False)
            for p in range(2):
                output(2 * NCH - 2 + p, p)
            for p in range(2):
                mixed_in(NCH - 1, p)

            dve.wait_ge(s_done, 2 * NCH)
            V.tensor_copy(qss.rearrange("p b (j t) -> p b j t", j=4),
                          qT[:, :, TP:T].rearrange("p j (b t) -> p b j t", t=TB)).then_inc(q_staged, 1)

            def s_output(b, s, n):
                denominators(n, s, 1)
                for v in range(2):
                    h_ = slice(HD * v, HD * v + HD)
                    r = V.tensor_scalar(obs[h_, s, h_], psum[h_, 6 + s, 0:HD], st[h_, s, 12:13], None, ALU.mult)
                r.then_inc(o_done, 1)

            def s_mixed(b, s, n):
                dve.wait_ge(ot_done, n + 1)
                at = slice(TP + TB * b, TP + TB * (b + 1))

                def src(h_):
                    return psum[h_, 6 + s, P + h_.start:P + h_.stop].rearrange("p (j q) -> p j q", j=4)
                halves = [slice(HD * v, HD * v + HD) for v in range(2)]
                for h_ in halves:
                    r = V.tensor_scalar(a_hi[h_, 0:4, at], src(h_), 1.0, None, ALU.mult)
                r.then_inc(ahi_done, 1)
                dve.wait_ge(ahi_done, n + 1)
                for h_ in halves:
                    r = V.tensor_tensor(a_lo[h_, 0:4, at], src(h_), a_hi[h_, 0:4, at].bitcast(F32), ALU.subtract)
                r.then_inc(mixed, 1)

            for b in range(NB + 1):
                n, s = 2 * NCH + b, b % 2
                if b < NB:
                    maxima(n, s, psum[:, s, 0:SK].unsqueeze(1), 1, 4)
                if b > 0:
                    s_output(b - 1, 1 - s, n - 1)
                    s_mixed(b - 1, 1 - s, n - 1)

            for k in range(KT):
                residual(B_OUT0 + k, B_OUT0 + k + 1, k, 32)
                add_squares(1, k)
            for k in range(KT):
                rest(1, k, KT + k + 1)
            token_scale(AX_R1, 1)
            ff(B_FF0, 2, False)

            token_scale(AX_R2, 2)
            rowc = [0]

            def row(ins):
                rowc[0] += 1
                ins.then_inc(gate_rows, 1)
                dve.wait_ge(gate_rows, rowc[0])

            def first_values(j):
                dve.wait_ge(spilled, 16 * KT)
                project(B_HEAD + j, mv[:, j, :])

            R4 = slice(0, MH)
            row(V.memset(gp[R4, :], 1.0))
            row(V.memset(gp[R4, 0:TP:LC], 0.0))
            row(V.memset(gp[R4, TP:T:TB], 0.0))
            V.memset(gd[R4, :], 0.0)
            V.memset(rows[:, :], 0.0)
            dve.wait_ge(block_done, B_GATE + 1)
            gsrc = out3(B_GATE)
            V.tensor_tensor(by3(gz)[0:64], gsrc[0:64], by3(rbc[:, :])[0:64], ALU.mult).then_inc(evicted, 1)
            dve.wait_ge(evicted, B_GATE + 1)
            row(V.tensor_scalar(gt[0:64, :], gz[0:64, :], cols[0:64, C_GB:C_GB + 1], None, ALU.add))
            row(V.tensor_scalar(gm[32:36, :], gt[32:36, :], 0.0, None, ALU.min))
            dve.wait_ge(gates_act, 1)
            row(V.tensor_tensor(glf[R4, :], gm[32:36, :], gz[32:36, :], ALU.subtract))
            first_values(0)
            row(V.tensor_tensor_scan(gb[R4, :], gp[R4, :], glf[R4, :], 0.0, ALU.mult, ALU.add))
            row(V.tensor_tensor(gg[R4, :], gt[R4, :], gb[R4, :], ALU.subtract))
            row(V.tensor_copy(gz[R4, :], gg[R4, :]))
            m0 = cols[R4, C_M0:C_M0 + NB]
            row(V.tensor_tensor(gz[R4, TP:T:TB], gg[R4, TP:T:TB], m0, ALU.max))
            row(V.tensor_copy(gd[R4, LC:TP:LC], gb[R4, LC - 1:TP - 1:LC]))
            row(V.memset(gd[R4, TP:T:TB], NEG))
            row(V.tensor_tensor_scan(gm[R4, :], gd[R4, :], gz[R4, :], 0.0, ALU.add, ALU.max))
            V.tensor_tensor(mend[R4, 0:8], gb[R4, LC - 1:TP:LC], gm[R4, LC - 1:TP:LC], ALU.add)
            row(V.tensor_tensor(mend[R4, 8:16], gb[R4, TP + TB - 1:T:TB], gm[R4, TP + TB - 1:T:TB], ALU.add))
            first_values(1)
            row(V.memset(gp[R4, 0:LC], 0.0))
            row(V.tensor_copy(gp[R4, LC:TP].rearrange("p (c t) -> p c t", t=LC),
                              mend[R4, 0:7].unsqueeze(2).to_broadcast([MH, NLC - 1, LC])))
            row(V.tensor_copy(gp[R4, TP:T].rearrange("p (c t) -> p c t", t=TB),
                              m0.unsqueeze(2).to_broadcast([MH, NB, TB])))
            row(V.tensor_copy(gd[R4, 0:TP].rearrange("p (c t) -> p c t", t=LC),
                              gm[R4, LC - 1:TP:LC].unsqueeze(2).to_broadcast([MH, NLC, LC])))
            row(V.tensor_copy(gd[R4, TP:T].rearrange("p (c t) -> p c t", t=TB),
                              gm[R4, TP + TB - 1:T:TB].unsqueeze(2).to_broadcast([MH, NB, TB])))
            V.tensor_scalar(mneg[R4, :], gm[R4, :], -1.0, None, ALU.mult)
            V.tensor_tensor(rows[0:4, :], gp[R4, :], gm[R4, :], ALU.subtract)
            V.tensor_tensor(rows[32:36, :], gg[R4, :], gd[R4, :], ALU.subtract)
            V.tensor_copy(rows[64:68, :], gg[R4, :])
            V.scalar_tensor_tensor(out=rows[96:100, :], in0=gb[R4, :], scalar=-1.0, in1=gm[R4, :],
                                   op0=ALU.mult, op1=ALU.subtract)
            V.tensor_tensor(wc16[R4, 0:8], gp[R4, 0:TP:LC], gd[R4, 0:TP:LC], ALU.subtract)
            row(V.tensor_tensor(wc16[R4, 8:16], gp[R4, TP:T:TB], gd[R4, TP:T:TB], ALU.subtract))
            assert rowc[0] == GATE_TO_EXP
            dve.wait_ge(gates_act, 4)
            row(V.tensor_tensor(wd[R4, :].rearrange("p (h i) -> p h i", h=MH), wc16[R4, :].unsqueeze(1).to_broadcast([MH, MH, 16]),
                                cols[R4, C_MH:C_MH + MH * 16].rearrange("p (h i) -> p h i", h=MH), ALU.mult))
            assert rowc[0] == GATE_ROWS
            for g in range(3):
                dve.wait_ge(aux_done, AX_GT + g + 1)
                k = min(4, NLC + 1 - 4 * g)
                V.tensor_copy(rtc[:, 4 * g:4 * g + k, :, :],
                              psum[:, 6 + (AX_GT + g) % 2, 0:P * k].rearrange("p (c q r) -> p c q r", c=k, q=4)[:, :, :, 0:MH])\
                    .then_inc(aux_read, 1)
            dve.wait_ge(aux_done, AX_WC + 1)
            V.tensor_copy(wcb[:, :, :], psum[:, 6 + AX_WC % 2, 0:MH * 16].rearrange("p (h i) -> p h i", h=MH))\
                .then_inc(aux_read, 1)
            dve.wait_ge(aux_read, AX_WC + 1)
            row(V.tensor_scalar(rtc[:, :, Q_WS, :], rtc[:, :, Q_WS, :], MD ** -0.5, None, ALU.mult))

            V.memset(qext[:, :, 0:QH], 0.0)
            V.memset(vaug[:, :, MD:MA], 1.0)
            row(V.memset(qx[:, :, :, :], 0.0))

            def head(h, last):
                dve.wait_ge(mix_done, 9 * h + ONE)
                V.tensor_scalar(rth[:, :, :], rtc[:, :, :, bass.ds(h, 1)].rearrange("p c q o -> p c (q o)"),
                                1.0, None, ALU.mult)
                V.tensor_scalar(wch[:, :], wcb[:, bass.ds(h, 1), :].rearrange("p o i -> p (o i)"),
                                1.0, None, ALU.mult).then_inc(head_set, 1)
                dve.wait_ge(head_set, 2 * h + 1)
                V.tensor_scalar(ws8[:, :], cols[:, C_BSEL:C_BSEL + NB], rth[:, NLC, Q_WS:Q_WS + 1], None, ALU.mult)\
                    .then_inc(head_set, 1)
                dve.wait_ge(cp_out, 16 * h + ONE)
                V.memset(cst[:, :, :], 0.0).then_inc(cu_done, 1)

                def qk_ext(j):
                    i, s = j - 2, j % 2
                    e, z = qext[:, s, :], out3(B_HEAD + j)
                    dve.wait_ge(block_done, 8 * h + (B_HEAD + j + 1))
                    dve.wait_ge(qh_in[i], 16 * h + 16)
                    dve.wait_ge(qh_out[(i + 2) % 4], 32 * h + (32 * (i >= 2) + ONE))
                    V.tensor_tensor(e[:, QH:QH + 2 * TN].rearrange("p (a b) -> p a b", a=2), z[:, 0:2, :],
                                    by3(rbc[:, :])[:, 0:2, :], ALU.mult)
                    V.tensor_tensor(e[:, QH + 2 * TN:QH + TP], z[:, 2, 0:TP - 2 * TN], rbc[:, 2 * TN:TP], ALU.mult)
                    V.tensor_tensor(sample(e[:, QH + TP:QEXT], QH, QH + TB), sample(z[:, 2, TP - 2 * TN:TN], 0, TB),
                                    sample(rbc[:, TP:T], 0, TB), ALU.mult).then_inc(evicted, 1)
                    dve.wait_ge(evicted, 8 * h + (B_HEAD + j + 1))
                    if i == 0:
                        dve.wait_ge(par_in, 16 * h + 16)
                    dst = mk[:, i, :] if i < 2 else mq[:, i - 2, :]
                    es_ = e[:, QH + TP:QEXT].rearrange("p (b w) -> p b w", w=QH + TB)
                    for r in range(QW):
                        w = head_par[:, H_W + QW * i + r:H_W + QW * i + r + 1]
                        for part, (o, a) in enumerate((
                                (dst[:, 0:TP], e[:, r:r + TP]),
                                (sample(dst[:, TP:T], 0, TB), es_[:, :, r:r + TB]))):
                            if r == 0:
                                V.tensor_scalar(o, a, w, head_par[:, H_B + i:H_B + i + 1], ALU.mult, ALU.add)\
                                    .then_inc(qconv, 1)
                            else:
                                dve.wait_ge(qconv, 32 * h + (8 * i + 2 * r + part - 1))
                                V.scalar_tensor_tensor(out=o, in0=a, scalar=w, in1=o, op0=ALU.mult, op1=ALU.add)\
                                    .then_inc(qconv, 1)

                for j in range(2, 6):
                    qk_ext(j)
                dve.wait_ge(qsilu, 4 * h + 4)
                for b in range(NB):
                    r = V.tensor_copy(qx[:, :, b, TB * b:TB * (b + 1)], mq[:, :, TP + TB * b:TP + TB * (b + 1)])
                r.then_inc(qx_done, 1)
                dve.wait_ge(block_done, 8 * h + (B_HEAD + 7))
                V.tensor_tensor(by3(mo[:, 0, :]), out3(B_HEAD + 6), by3(rbc[:, :]), ALU.mult).then_inc(evicted, 1)
                dve.wait_ge(mix_out, 16 * h + ONE)

                def piece(m):
                    if last and m > 2:
                        return
                    i, j = (m, 7) if m < 3 else ((m - 3) // 2, 8 + (m - 3) % 2)
                    if i < 2:
                        dve.wait_ge(piece_done, PIECES * h + (m + 1 - (m > 2)))
                    else:
                        dve.wait_ge(block_done, 8 * h + (B_HEAD + j + 1))
                    if m == 3:
                        dve.wait_ge(vcp, 10 * h + 9)
                    dst = mo[:, 1, tok(i)] if j == 7 else mv[:, j - 8, tok(i)]
                    V.tensor_tensor(dst, psum[:, PIECE_BANK, 0:TN], rbc[:, tok(i)], ALU.mult)\
                        .then_inc(piece_out if i < 2 else evicted, 1)

                def gated(p):
                    s = p % 2
                    dve.wait_ge(e_done, 9 * h + (p + 1))
                    if SEQ[p] < NLC:
                        dve.wait_ge(kw_done, 8 * h + (SEQ[p] + 1))
                    V.scalar_tensor_tensor(out=sT[:, s, :], in0=psum[:, s, P:2 * P], scalar=MD ** -0.5,
                                           in1=eM[:, s, :], op0=ALU.mult, op1=ALU.mult).then_inc(st_done, 1)

                def numerator(p):
                    s = p % 2
                    dve.wait_ge(intra_done, 9 * h + (p + 1))
                    dve.wait_ge(tb_done, 9 * h + (p + 1))
                    V.tensor_tensor(num[:, s, 0:MA], psum[:, 2, 0:MA], tB[:, s, 0:MA], ALU.add).then_inc(num_done, 1)
                    dve.wait_ge(num_done, 9 * h + (p + 1))
                    den = num[:, s, MD:MA]
                    V.scalar_tensor_tensor(out=sm[:, s, 0:1], in0=den, scalar=-1.0, in1=den, op0=ALU.mult,
                                           op1=ALU.max).then_inc(dn_done, 1)
                    dve.wait_ge(dn_done, 27 * h + (3 * p + 1))
                    V.tensor_scalar(sm[:, s, 1:2], sm[:, s, 0:1], rth[:, SEQ[p], Q_EM:Q_EM + 1], None, ALU.max)\
                        .then_inc(dn_done, 1)
                    dve.wait_ge(dn_done, 27 * h + (3 * p + 2))
                    V.reciprocal(sm[:, s, 2:3], sm[:, s, 1:2]).then_inc(dn_done, 1)

                def normed(p):
                    s = p % 2
                    dve.wait_ge(sc_done, 9 * h + (p + 1))
                    V.tensor_scalar(hn[:, s, :], num[:, s, 0:MD], sm[:, s, 6:7], 16.0, ALU.mult, ALU.mult)\
                        .then_inc(hn_done, 1)

                def gate_out(p):
                    c = SEQ[p]
                    q = slice(LC * c, LC * (c + 1))
                    dve.wait_ge(ht_done, 9 * h + (p + 1))
                    dve.wait_ge(osig, 4 * h + (LC * c // TN + 2))
                    for k in range(2):
                        r = V.scalar_tensor_tensor(out=mix[:, k, q], in0=psum[:, 2 + k, HT:HT + P],
                                                   scalar=head_par[:, H_G + k:H_G + k + 1], in1=mo[:, k, q],
                                                   op0=ALU.mult, op1=ALU.mult)
                    r.then_inc(mix_done, 1)

                def updated(b):
                    s = b % NCS
                    dve.wait_ge(csc_done, 8 * h + (b + 1))
                    m = csl[:, s, :].rearrange("p (k e) -> p k e", k=2)
                    V.scalar_tensor_tensor(out=m, in0=m, scalar=wch[:, 8 + b:9 + b], in1=psum[:, 4:6, 0:MA],
                                           op0=ALU.mult, op1=ALU.add).then_inc(csu_done, 1)

                gated(0)
                for p in range(NLC + 1):
                    c = SEQ[p]
                    if p < NLC:
                        gated(p + 1)
                        piece(p)
                    if c < NLC:
                        dve.wait_ge(c_done, 8 * h + (c + 1))
                        V.scalar_tensor_tensor(out=cst[:, :, :], in0=cst[:, :, :], scalar=wch[:, c:c + 1],
                                               in1=psum[:, 4:6, 0:MA], op0=ALU.mult, op1=ALU.add).then_inc(cu_done, 1)
                    numerator(p)
                    for b in STREAMS[p]:
                        updated(b)
                    if last and p > LAST_O:
                        for k in RELOADED[p - LAST_O - 1]:
                            rest(None, k, 3 * KT + k + 1, src=back[:, k, :])
                    if p >= 1:
                        gate_out(p - 1)
                    normed(p)
                piece(NLC)
                gate_out(NLC)

            with dve.Fori(0, MH - 1) as h:
                head(h, False)
            head(MH - 1, True)

            for k in range(2):
                rest(None, KT - 2 + k, 4 * KT - 1 + k, src=mix[:, k, :])
            for k in range(KT):
                residual(B_OUT1 + k, B_OUT1 + k + 1, k, 48)
                add_squares(3, k)
            for k in range(KT):
                rest(3, k, 4 * KT + k + 1)
            token_scale(AX_R3, 3)
            ff(B_FF1, 4, True)

            token_scale(AX_R4, 4)
            for k in range(KT):
                V.scalar_tensor_tensor(out=x[:, k, :], in0=x[:, k, :], scalar=gain(4, k), in1=rbc[:, :],
                                       op0=ALU.mult, op1=ALU.mult).then_inc(y_done, 1)

        @block.scalar
        def _(act):
            A = nc.scalar.activation
            dma = act.dma_start

            def high_part(m, k, src=None):
                src = x[:, k, :] if src is None else src
                A(a_hi[:, k, :], src, ACT.Copy, scale=1.0 if m is None else gain(m, k)).then_inc(hi_done, 1)

            def square(m, k):
                n = KT * m + k
                if n >= 2:
                    act.wait_ge(ssq_done, n - 1)
                A((sq, hid)[k % 2], x[:, k, :], ACT.Square).then_inc(sq_done, 1)

            def root(m):
                act.wait_ge(rsum_done, m + 1)
                A(rbc[:, :], rbc[:, :], ACT.Sqrt).then_inc(rbc_done, 1)

            def ff(b0, m, last):
                hb = FK * FC * (b0 > B_GATE)

                def up(c, j):
                    act.wait_ge(evicted, 12 * c + (b0 + j + 1))
                    A(h_hi[:, j, :], hid, ACT.Square)
                    A(hid, hid, ACT.Square).then_inc(hsq_done, 1)

                with act.Fori(0, FC) as c:
                    for j in range(FK):
                        up(c, j)
                for k in range(KT):
                    act.wait_ge(evicted, 12 * (FC - 1) + (b0 + FK + k + 1))
                    if not last:
                        high_part(m, k)
                    square(m, k)
                    if not last:
                        dma(t["x_spill"][k], x[:, k, :]).then_inc(spilled, 16)

            dma(cols[:, :], t["cols"]).then_inc(cols_in, 16)
            dma(mats[:, :, :], t["mats"]).then_inc(mats_in, 16)
            for k in range(KT):
                dma(x[:, k, :], t["x"][k]).then_inc(x_in[k], 16)
            dma(kc[:, :, 0:WIN], t["kcache"]).then_inc(cache_in, 16)
            dma(vc[:, :, :], t["vcache"]).then_inc(cache_in, 16)

            act.wait_ge(cols_in, 16)
            for k in range(KT):
                act.wait_ge(x_in[k], 16)
                high_part(0, k)
                square(0, k)
            act.wait_ge(lo_done, KT)
            act.wait_ge(sq_done, KT)
            for j in range(CT):
                dma(ext[:, j + 1, HIST + TP:EXT].rearrange("p (b w) -> p b w", w=HIST + TB)[:, :, 0:HIST],
                    t["conv_hist"][j]).then_inc(hist_in, 16)
            root(0)
            act.wait_ge(rbc_done, 1)
            dma(cos, t["cos"]).then_inc(cs_tab_in, 16)
            dma(sin, t["sin"]).then_inc(cs_tab_in, 16)

            for j in range(CT):
                act.wait_ge(evicted, 2 * j + 2)
                A(zs, zs, ACT.Sigmoid).then_inc(sig_done, 1)
                act.wait_ge(ext_done, j + 1)
                e = ext[:, j + 1, :]
                dma(t["conv_p"][j], e[:, TP:TP + HIST]).then_inc(conv_out[j], 16)
                act.wait_ge(hist_in, 16 * CT)
                dma(t["conv_s"][j], e[:, HIST + TP:EXT].rearrange("p (b w) -> p b w", w=HIST + TB)[:, :, TB:])\
                    .then_inc(conv_out[j], 16)
            act.wait_ge(evicted, 10)
            dma(t["v_p"], vT[:, TP - WIN:TP]).then_inc(kv_out, 16)
            dma(t["v_s"], vT[:, TP:T]).then_inc(kv_out, 16)
            act.wait_ge(cache_in, 32)
            dma(t["v_old"], vc[TB:WIN, :, :]).then_inc(kv_out, 16)
            act.wait_ge(kc_done, 1)
            dma(t["k_p"], kT[:, TP - WIN:TP]).then_inc(kv_out, 16)
            dma(t["k_s"], kc[:, :, TB:SK]).then_inc(kv_out, 16)

            for i in range(NT):
                act.wait_ge(aux_read, AX_LN + i + 1)
                if i > 0:
                    act.wait_ge(aux_done, AX_LN + NT + i)
                A(lnsq[:, :, :], ext[:, 0:CT, tok(i)], ACT.Square).then_inc(ln_sq, 1)
            for i in range(NT):
                act.wait_ge(ln_v, i + 1)
                A(zs[:, tok(i)], zs[:, tok(i)], ACT.Sqrt).then_inc(ln_rstd, 1)
            for i in range(NT):
                act.wait_ge(ln_scaled, i + 1)
                for j in range(CT):
                    A(ext[:, j, tok(i)], ext[:, j, tok(i)], ACT.Silu, bias=cols[:, C_LB + j:C_LB + j + 1],
                      scale=cols[:, C_LG + j:C_LG + j + 1]).then_inc(ln_y, 1)
                act.wait_ge(ln_y, CT * (i + 1))
                A(a_hi[:, CT:2 * CT, tok(i)], ext[:, 0:CT, tok(i)], ACT.Copy).then_inc(ln_hi, 1)
            act.wait_ge(ln_lo, NT)
            act.wait_ge(kv_out, 16 * 5)
            for j in range(CT):
                act.wait_ge(conv_out[j], 32)
            for k in range(KT):
                dma(x[:, k, :], t["x"][k]).then_inc(x_in[k], 16)

            def probs(n, p, parts, width):
                act.wait_ge(m_done, n + 1)
                if not (isinstance(n, int) and n < 2):
                    act.wait_ge(t_done, n - 1)
                    act.wait_ge(den_done, 2 * n - 2)
                for v, (dst, src) in enumerate(parts):
                    A(dst, src, ACT.Exp, bias=st[:, p, 2 + v:3 + v], scale=ATT_SCALE, accum_out=st[:, p, 6 + v:7 + v])
                A(st[:, p, 10:10 + width], st[:, p, 4:4 + width], ACT.Exp).then_inc(p_done, 1)

            def copy_flipped(n, p, pieces):
                act.wait_ge(t_done, n + 1)
                if not (isinstance(n, int) and n < 2):
                    act.wait_ge(pv_done, n - 1)
                for dst, src in pieces:
                    r = A(dst, src, ACT.Copy)
                r.then_inc(pt_done, 1)

            def astep(c):
                nb = c + 1 if isinstance(c, int) and c < 2 else 3
                for p in range(2):
                    probs(2 * c + p, p, [(pr[:, p, 192 * v:192 * v + CH * nb], psum[:, p, 192 * v:192 * v + CH * nb])
                                         for v in range(2)], 2)
                for p in range(2):
                    both = psum[0:CH, 2 + 2 * p:4 + 2 * p, :].rearrange("p a b -> p (a b)")
                    if nb == 3:
                        pieces = [(pT[0:CH, p, 0:6 * P], both[:, 0:6 * P])]
                    else:
                        pieces = [(pT[0:CH, p, 3 * P * v:3 * P * v + nb * P], both[:, 3 * P * v:3 * P * v + nb * P])
                                  for v in range(2)]
                    copy_flipped(2 * c + p, p, pieces)

            for c in range(3):
                astep(c)
            with act.Fori(3, NCH) as c:
                astep(c)
            for b in range(NB):
                n, s = 2 * NCH + b, b % 2
                probs(n, s, [(pr[:, s, 0:SK], psum[:, s, 0:SK])], 1)
                copy_flipped(n, s, [(pT[:, s, 0:P], psum[:, 2 + 2 * s, 0:P]),
                                    (pT[0:TB, s, P:2 * P], psum[0:TB, 2 + 2 * s, P:2 * P])])

            for k in range(KT):
                act.wait_ge(evicted, B_OUT0 + k + 1)
                square(1, k)
            for k in range(KT):
                high_part(1, k)
            root(1)
            ff(B_FF0, 2, False)

            root(2)
            act.wait_ge(gate_rows, 5)
            A(gz[32:36, :], gt[32:36, :], ACT.Abs).then_inc(gact_own, 1)
            act.wait_ge(gact_own, 1)
            A(gz[32:36, :], gz[32:36, :], ACT.Exp, scale=-1.0).then_inc(gact_own, 1)
            act.wait_ge(gact_own, 2)
            A(gz[32:36, :], gz[32:36, :], ACT.Ln, bias=1.0).then_inc(gates_act, 1)
            act.wait_ge(gate_rows, GATE_TO_EXP)
            for q in (0, 32, 96):
                r = A(rows[q:q + MH, :], rows[q:q + MH, :], ACT.Exp)
                if q:
                    r.then_inc(gates_act, 1)
            A(wc16[0:MH, :], wc16[0:MH, :], ACT.Exp).then_inc(gates_act, 1)
            dma(t["m_out"], mend[0:MH, :]).then_inc(g_out, 16)
            act.wait_ge(gate_rows, GATE_ROWS + 2)

            def head(h, last):
                act.wait_ge(mix_done, 9 * h + ONE)
                dma(head_par[:, :], t["head_par"][h]).then_inc(par_in, 16)

                def history(i):
                    e = qext[:, i % 2, QH + TP:QEXT].rearrange("p (b w) -> p b w", w=QH + TB)
                    dma(e[:, :, 0:QH], t["qk_hist"][h, i]).then_inc(qh_in[i], 16)

                def sample_in(b):
                    s = b % NCS
                    act.wait_ge(cs_out[s], 16 * CS_USES * h + (16 * (b // NCS) + ONE))
                    dma(csl[:, s, :], t["mem_in"][h, b]).then_inc(cs_in[s], 16)

                for i in (2, 3):
                    act.wait_ge(qh_out[i], 32 * h + ONE)
                history(0)
                history(1)
                for b in range(NCS):
                    sample_in(b)
                def turned(n, dst):
                    act.wait_ge(vtr, 10 * h + (n + 1))
                    A(dst, psum[:, 6 + n % 2, 0:MD], ACT.Copy).then_inc(vcp, 1)

                for i in range(4):
                    j = i + 2
                    act.wait_ge(evicted, 8 * h + (B_HEAD + j + 1))
                    act.wait_ge(qh_in[i], 16 * h + 16)
                    e = qext[:, i % 2, :]
                    dma(t["qk_p"][h, i], e[:, TP:TP + QH]).then_inc(qh_out[i], 16)
                    dma(t["qk_s"][h, i], e[:, QH + TP:QEXT].rearrange("p (b w) -> p b w", w=QH + TB)[:, :, TB:])\
                        .then_inc(qh_out[i], 16)
                    for n in range(2 * i, 2 * i + 2 + (i == 3)):
                        turned(n, vaug[:, n, 0:MD])
                    if i == 3:
                        turned(NLC + 1, ks)
                    act.wait_ge(qconv, 32 * h + 8 * (i + 1))
                    dst = mk[:, i, :] if i < 2 else mq[:, i - 2, :]
                    A(dst, dst, ACT.Silu).then_inc(qsilu, 1)
                    if i < 2:
                        act.wait_ge(qh_out[i], 32 * h + (32 + ONE))
                        history(i + 2)
                act.wait_ge(evicted, 8 * h + (B_HEAD + 7))
                A(mo[:, 0, :], mo[:, 0, :], ACT.Sigmoid).then_inc(osig, 1)
                act.wait_ge(head_set, 2 * h + 2)

                def decay(p):
                    s = p % 2
                    act.wait_ge(es_done, 9 * h + (p + 1))
                    A(eM[:, s, :], psum[:, s, 0:P], ACT.Exp, bias=rth[:, SEQ[p], Q_G:Q_G + 1]).then_inc(e_done, 1)

                def keys(c):
                    s = c % 2
                    if c >= 2:
                        act.wait_ge(c_done, 8 * h + (c - 1))
                    z = (c if c < NLC - 1 else NLC) % 2
                    A(kw[:, s, :], psum[:, z, 2 * P:2 * P + MD], ACT.Copy, scale=rth[:, c, Q_WS:Q_WS + 1])\
                        .then_inc(kw_done, 1)

                def inter(p):
                    s, z = p % 2, 3 if SEQ[p] < NLC else STREAM_BANK
                    act.wait_ge(ab_done, 9 * h + (p + 1))
                    A(tB[:, s, 0:MA], psum[:, z, 0:MA], ACT.Copy, scale=rth[:, SEQ[p], Q_INT:Q_INT + 1])\
                        .then_inc(tb_done, 1)

                def sumsq(p):
                    s = p % 2
                    act.wait_ge(dn_done, 27 * h + (3 * p + 3))
                    A(junk, num[:, s, 0:MD], ACT.Square, scale=sm[:, s, 2:3], accum_out=sm[:, s, 3:4])\
                        .then_inc(ss_done, 1)

                def masked_keys(b):
                    if b >= 2:
                        act.wait_ge(csc_done, 8 * h + (b - 1))
                    A(kwm[:, b % 2, :], ks, ACT.Copy, scale=ws8[:, b:b + 1]).then_inc(kwm_done, 1)

                def sample_out(b):
                    s = b % NCS
                    act.wait_ge(csu_done, 8 * h + (b + 1 + ONE))
                    dma(t["mem_s"][h, b], csl[:, s, :]).then_inc(cs_out[s], 16)

                def ogate(m):
                    if m < 2:
                        act.wait_ge(piece_out, PIECES * h + (m + 1))
                    else:
                        act.wait_ge(evicted, 8 * h + (B_HEAD + 8))
                    A(mo[:, 1, tok(m)], mo[:, 1, tok(m)], ACT.Sigmoid).then_inc(osig, 1)

                decay(0)
                keys(0)
                masked_keys(0)
                for p in range(NLC + 1):
                    c = SEQ[p]
                    if p < NLC:
                        decay(p + 1)
                        if SEQ[p + 1] < NLC:
                            keys(SEQ[p + 1])
                    inter(p)
                    sumsq(p)
                    if p < 3:
                        ogate(p)
                    for b in (STREAMS[p + 1] if p < NLC else []):
                        masked_keys(b)
                    for b in (STREAMS[p - 1] if p else []):
                        sample_out(b)
                    if p >= 2:
                        for b in STREAMS[p - 2]:
                            if b + NCS < NB:
                                sample_in(b + NCS)
                    if last and p == LAST_O:
                        act.wait_ge(block_done, B_OUT1)
                        act.wait_ge(mix_out, 16 * (MH - 1) + ONE)
                        for g in range(MH - 1):
                            dma(back[:, 2 * g:2 * g + 2, :], t["mix_spill"][g]).then_inc(mix_back[g], 16)
                    if last and p > LAST_O:
                        for k in RELOADED[p - LAST_O - 1]:
                            act.wait_ge(mix_back[k // 2], 16)
                            high_part(None, k, back[:, k, :])
                act.wait_ge(cu_done, 9 * h + 9)
                dma(t["mem_p"][h], cst[:, :, :]).then_inc(cp_out, 16)
                act.wait_ge(mix_done, 9 * h + (9 + ONE))
                if not last:
                    dma(t["mix_spill"][h], mix[:, :, :]).then_inc(mix_out, 16)

            with act.Fori(0, MH - 1) as h:
                head(h, False)
            head(MH - 1, True)

            for k in range(2):
                high_part(None, KT - 2 + k, mix[:, k, :])
            for i in range(4):
                act.wait_ge(qh_out[i], 32 * MH + ONE)
            for k in range(KT):
                dma(x[:, k, :], t["x_spill"][k]).then_inc(x_in[k], 16)
            for s in range(NCS):
                act.wait_ge(cs_out[s], 16 * CS_USES * MH + ONE)
            act.wait_ge(cp_out, 16 * MH + ONE)
            for k in range(KT):
                act.wait_ge(evicted, B_OUT1 + k + 1)
                square(3, k)
            for k in range(KT):
                high_part(3, k)
            root(3)
            ff(B_FF1, 4, True)

            root(4)
            for k in range(KT):
                act.wait_ge(y_done, k + 1)
                dma(t["y"][k], x[:, k, :]).then_inc(y_out, 16)
            act.wait_ge(y_out, 16 * KT)
            act.wait_ge(g_out, 16)


F = "float32"
_SHAPES_IN = ["x", "wall", "cols", "mats", "cos", "sin", "kcache", "vcache", "conv_hist", "head_par", "qk_hist",
              "mem_in"]
_OUTS = {
    "y": (KT, P, T), "conv_p": (CT, P, HIST), "conv_s": (CT, P, NB, HIST), "v_p": (P, WIN), "v_s": (P, NB * TB),
    "v_old": (WIN - TB, NB, P), "k_p": (P, WIN), "k_s": (P, NB, WIN), "qk_p": (MH, 4, P, QH),
    "qk_s": (MH, 4, P, NB, QH), "mem_p": (MH, P, 2, MA), "mem_s": (MH, NB, P, 2 * MA), "m_out": (MH, 16),
    "x_spill": (KT, P, T), "mix_spill": (MH, P, 2, T),
}


def _lay_out(i):
    import numpy as np

    def by_k(w):
        n = w.shape[1] // P
        return w.reshape(KT, P, n, P).transpose(2, 1, 0, 3).reshape(n, P, KT * P)

    def channels(v):
        return np.asarray(v).reshape(-1, P).T

    a = {}
    x = np.concatenate([i["x_prompt"][0], i["x_sample"].reshape(NB * TB, D)])
    a["x"] = x.T.reshape(KT, P, T)
    w = i["w_in_even"][0]
    half = CT * P
    glu = w[:, 768:].reshape(D, 2, CT, P).transpose(0, 2, 1, 3).reshape(D, 2 * half)
    q = w[:, :512].reshape(D, 2, 4, HD).transpose(0, 2, 1, 3).reshape(D, 512)
    wo = i["w_out_even"][0]
    wo = np.concatenate([wo[:512].reshape(2, 4, HD, D).transpose(1, 0, 2, 3).reshape(512, D), wo[512:]])
    units = [by_k(glu), by_k(w[:, 512:768]), by_k(q), by_k(wo)]

    def ffn(layer):
        w1 = by_k(i["w_ff1"][layer]).reshape(FC, FK, P, KT * P)
        w2 = i["w_ff2"][layer].reshape(FC, FK, P, 4, 2, P).transpose(0, 3, 2, 4, 1, 5).reshape(FC, 4, P, KT * P)
        return np.concatenate([w1, w2], axis=1).reshape(FC * 8, P, KT * P)
    units.append(ffn(0))
    w = i["w_in_odd"][0]
    gates = np.zeros((D, P), w.dtype)
    gates[:, 0:MH] = w[:, 4 * D:4 * D + MH]
    gates[:, 32:32 + MH] = w[:, 4 * D + MH:]
    heads = w[:, :4 * D].reshape(D, 4, MH, MD)[:, [2, 1, 0, 3]].transpose(0, 2, 1, 3).reshape(D, 4 * D)
    units += [by_k(gates), by_k(heads), by_k(i["w_out_odd"][0]), ffn(1)]
    a["wall"] = np.concatenate(units)
    c = np.zeros((P, NCOL), np.float32)
    for n, g in enumerate([i["norm_mix_g"][0], i["norm_ffn_g"][0], i["norm_mix_g"][1], i["norm_ffn_g"][1],
                           i["norm_out_g"]]):
        c[:, C_G + KT * n:C_G + KT * (n + 1)] = channels(g)
    c[:, C_CW:C_CB] = i["conv_w"][0].reshape(CW, CT, P).transpose(2, 1, 0).reshape(P, CT * CW)
    c[:, C_CB:C_CB + CT] = channels(i["conv_b"][0])
    c[:, C_LG:C_LG + CT] = channels(i["conv_ln_g"][0])
    c[:, C_LB:C_LB + CT] = channels(i["conv_ln_b"][0])
    sink = i["attn_sink"][0]
    for p in range(2):
        for v in range(2):
            c[:, C_SINK + 2 * p + v] = np.repeat(sink[4 * v + 2 * p:4 * v + 2 * p + 2], CH)
    c[:, C_SINKS] = np.repeat(sink, TB)
    c[0:MH, C_GB] = i["gate_b_i"][0]
    c[32:32 + MH, C_GB] = i["gate_b_f"][0]
    c[:, C_BSEL:C_BSEL + NB] = np.repeat(np.eye(NB, dtype=np.float32), TB, axis=0)
    c[0:MH, C_M0:C_M0 + NB] = i["state_mlstm_m"][0].T
    c[:, C_POW] = MD * EPS
    c[:, C_POW + 1] = -0.5
    c[0:MH, C_MH:C_MH + MH * 16] = np.repeat(np.eye(MH, dtype=np.float32), 16, axis=1)
    a["cols"] = c
    m = np.zeros((P, NK, P), np.float32)
    m[:, K_ID] = np.eye(P)
    m[:, K_ONE] = 1
    for base in (0, HD):
        for r in range(8):
            m[base + 8 + r, K_PERM, base + r] = -1
            m[base + r, K_PERM, base + 8 + r] = 1
    at = np.arange(P)
    causal = at[:, None] <= at[None, :]
    m[:, K_CAUS] = np.where(causal, 0, NEG)
    m[:, K_BLK] = np.where(causal & (at[:, None] // TB == at[None, :] // TB), 0, NEG)
    a["mats"] = m
    pos = np.concatenate([np.arange(TP), np.tile(1024 + np.arange(TB), NB)]).astype(np.float32)
    inv = np.float32(500000.0) ** (-np.arange(8, dtype=np.float32) / np.float32(8))
    ang = inv[:, None] * pos[None, :]
    cos, sin = np.ones((P, T), np.float32), np.zeros((P, T), np.float32)
    for base in (0, 8, HD, HD + 8):
        cos[base:base + 8] = np.cos(ang)
        sin[base:base + 8] = np.sin(ang)
    a["cos"], a["sin"] = cos, sin
    a["kcache"] = i["cache_swa_k"][0].transpose(2, 3, 0, 1).reshape(P, NB, WIN)
    a["vcache"] = i["cache_swa_v"][0].transpose(1, 0, 2, 3).reshape(WIN, NB, P)
    a["conv_hist"] = i["state_conv"][0].reshape(NB, HIST, CT, P).transpose(2, 3, 0, 1)

    def by_head(v):
        v = np.asarray(v).reshape(v.shape[:-1] + (2, MH, 2, P))
        v = np.flip(v, -4)
        n = v.ndim
        v = np.moveaxis(v, (n - 3, n - 4, n - 2, n - 1), (0, 1, 2, 3))
        return v.reshape((MH, 4, P) + v.shape[4:])
    a["qk_hist"] = by_head(i["state_qk_conv"][0])
    hp = np.zeros((MH, P, NH), np.float32)
    hp[:, :, H_W:H_W + 16] = by_head(i["qk_conv_w"][0]).transpose(0, 2, 1, 3).reshape(MH, P, 16)
    hp[:, :, H_B:H_B + 4] = by_head(i["qk_conv_b"][0]).transpose(0, 2, 1)
    hp[:, :, H_G:H_G + 2] = i["mlstm_norm_g"][0].reshape(MH, 2, P).transpose(0, 2, 1)
    for h in range(MH):
        hp[h, h, H_SEL:] = 1
    a["head_par"] = hp
    mem = np.concatenate([i["state_mlstm_C"][0].transpose(0, 1, 3, 2), i["state_mlstm_n"][0][..., None]], axis=-1)
    a["mem_in"] = mem.reshape(NB, MH, 2, P, MA).transpose(1, 0, 3, 2, 4).reshape(MH, NB, P, 2 * MA)
    return {k: np.ascontiguousarray(v) for k, v in a.items()}


def _put_back(r):
    import numpy as np

    y = r["y"].reshape(D, T).T
    out = [y[:TP][None], y[TP:].reshape(NB, TB, D)]

    def heads(v):
        return v.T.reshape(1, 1, -1, 2, HD)
    kp, vp = heads(r["k_p"]), heads(r["v_p"])
    cp = r["conv_p"].transpose(2, 0, 1).reshape(1, 1, HIST, CT * P)

    def from_heads(v):
        v = v.reshape((MH, 2, 2, P) + v.shape[3:])
        n = v.ndim
        v = np.moveaxis(v, (0, 1, 2, 3), (n - 3, n - 4, n - 2, n - 1))
        v = np.flip(v, -4)
        return v.reshape(v.shape[:-4] + (2 * D,))
    qp = from_heads(r["qk_p"]).reshape(1, 1, QH, 2 * D)
    qs = from_heads(r["qk_s"]).reshape(1, NB, QH, 2 * D)
    mp = r["mem_p"].transpose(0, 2, 1, 3).reshape(1, 1, MH, MD, MA)
    ms = r["mem_s"].reshape(MH, NB, P, 2, MA).transpose(1, 0, 3, 2, 4).reshape(1, NB, MH, MD, MA)
    m = r["m_out"]
    ks = r["k_s"].reshape(2, HD, NB, WIN).transpose(2, 3, 0, 1)[None]
    vs = np.concatenate([r["v_old"].transpose(1, 0, 2), r["v_s"].reshape(P, NB, TB).transpose(1, 2, 0)], axis=1)
    vs = vs.reshape(1, NB, WIN, 2, HD)
    cs = r["conv_s"].transpose(2, 3, 0, 1).reshape(1, NB, HIST, CT * P)
    out += [kp, vp, cp, qp, mp[..., :MD].swapaxes(-1, -2), mp[..., MD], m[:, 7].reshape(1, 1, MH),
            ks, vs, cs, qs, ms[..., :MD].swapaxes(-1, -2), ms[..., MD], m[:, 8:].T.reshape(1, NB, MH)]
    return tuple(np.ascontiguousarray(o) for o in out)


def kernel(**inputs):
    import numpy as np
    import concourse.bacc as bacc
    from concourse.bass_utils import run_bass_kernel_spmd

    arrays = _lay_out({k: np.asarray(v) for k, v in inputs.items()})
    nc = bacc.Bacc("TRN2", target_bir_lowering=False, num_devices=1)
    t = {}
    for name, a in arrays.items():
        t[name] = nc.dram_tensor("in_" + name, a.shape, F32, kind="ExternalInput").ap()
    for name, shape in _OUTS.items():
        t[name] = nc.dram_tensor("out_" + name, shape, F32, kind="ExternalOutput").ap()
    build(nc, t)
    r = run_bass_kernel_spmd(nc, [{"in_" + k: v for k, v in arrays.items()}], core_ids=[0])
    return _put_back({name: r.results[0]["out_" + name] for name in _OUTS})
```

```python
import concourse.bass as bass
from concourse import mybir
from contextlib import ExitStack

F32 = mybir.dt.float32
F32R = mybir.dt.float32r
ALU = mybir.AluOpType
ACT = mybir.ActivationFunctionType
AX = mybir.AxisListType.X

P = 128
D = 1024
KT = D // P
TP = 1024
NB, TB = 8, 16
T = TP + NB * TB
NT = 3
TN = T // NT
EPS = 1e-6
NEG = -1e30

CH = 64
NCH = TP // CH
HD = 64
WIN = 128
SK = WIN + TB
ATT_SCALE = HD ** -0.5
CW = 31
HIST = CW - 1
CT = 4
SLOT_IN = [2, 4, 3, 5]
T3 = 20
DVE_TAPS = {0: 0, 2: CW, 3: 2 * CW}
POOL_TAPS = [(1, r) for r in range(CW)] + [(3, r) for r in range(T3, CW)]
POOL_STEPS = 2 + 4 * (len(POOL_TAPS) - 1)
EXT = HIST + TP + NB * (HIST + TB)
MH = 4
MD = 256
MA = MD + 1
LC = 128
NLC = TP // LC
QW = 4
QH = QW - 1
QEXT = QH + TP + NB * (QH + TB)
FC = 8
FK = 4
POOL_Y = 2

U_IN0, U_OUT0, U_FF0 = 0, 14, 22
U_GATE = U_FF0 + FC * 8
U_HEAD = U_GATE + 1
U_OUT1 = U_HEAD + MH * 8
U_FF1 = U_OUT1 + 8
N_UNITS = U_FF1 + FC * 8
B_IN0, B_OUT0, B_FF0 = 0, 14, 22
B_GATE = B_FF0 + FC * 12
B_HEAD = B_GATE + 1
B_OUT1 = B_HEAD + MH * 8
B_FF1 = B_OUT1 + 8
B_END = B_FF1 + FC * 12
FF_BLOCKS = [1, 2, 3, 4, 6, 8, 10, 12]

C_G = 0
C_CW = C_G + 5 * KT
C_CB = C_CW + CT * CW
C_LG = C_CB + CT
C_LB = C_LG + CT
C_SINK = C_LB + CT
C_SINKS = C_SINK + 4
C_GB = C_SINKS + 1
C_BSEL = C_GB + 1
C_M0 = C_BSEL + NB
C_POW = C_M0 + NB
C_MH = C_POW + 2
NCOL = C_MH + MH * 16
K_ID, K_ONE, K_PERM, K_CAUS, K_BLK = range(5)
NK = 5
H_W, H_B, H_G, H_SEL = 0, 16, 20, 22
NH = H_SEL + P
NCS = 4
CS_USES = NB // NCS
SEQ = list(range(NLC - 1)) + [NLC, NLC - 1]
STREAMS = [[b] for b in range(NLC - 2)] + [[NLC - 2, NLC - 1], [], []]
PIECE_BANK, STREAM_BANK = 6, 7
PIECES = 6
LAST_O = 2
HT = 288
ONE = 1
NSINK = 2
GATE_TO_EXP, GATE_ROWS = 20, 21


LOW = 6 * EXT + T
HIGH = (NLC + 1) * MA + 2 * QEXT + 2 * NB * P + 2 * MA + NCS * 2 * MA


def build(nc, t):
    es = ExitStack()
    with es:
        def sb(name, shape, dt=F32):
            return es.enter_context(nc.sbuf_tensor(name, shape, dt))

        def sem(name):
            return es.enter_context(nc.semaphore(name))

        cols = sb("cols", [P, NCOL])
        mats = sb("mats", [P, NK, P])
        head_par = sb("head_par", [P, NH])
        w_raw = sb("w_raw", [P, 2, D])
        w_hi = sb("w_hi", [P, 2, D], F32R)
        w_lo = sb("w_lo", [P, 2, D], F32R)
        a_hi = sb("a_hi", [P, KT, T], F32R)
        with nc.sbuf_tensor("a_lo", [P, KT, T], F32R) as a_lo:
            pass
        back = sb("back", [P, KT, T])
        low = sb("low", [P, LOW])
        rbc = sb("rbc", [P, T])
        mid = sb("mid", [P, 6784])
        with nc.sbuf_tensor("h_hi", [P, FK, T], F32R) as h_hi, nc.sbuf_tensor("h_lo", [P, FK, T], F32R) as h_lo:
            pass
        high = sb("high", [P, HIGH])
        psum = es.enter_context(nc.psum_tensor("psum", [P, 8, 512], F32))

        ident = mats[:, K_ID, :]
        ones = mats[:, K_ONE, :]
        x = low[:, 0:KT * T].rearrange("p (k t) -> p k t", k=KT)

        def carve(buf):
            at = [0]

            def take(*shape):
                n = 1
                for s in shape:
                    n *= s
                v = buf[:, at[0]:at[0] + n]
                at[0] += n
                if len(shape) == 2:
                    v = v.rearrange("p (a b) -> p a b", a=shape[0])
                if len(shape) == 3:
                    v = v.rearrange("p (a b c) -> p a b c", a=shape[0], b=shape[1])
                return v
            return take

        take = carve(mid)
        ssq = take(T)
        sq = take(T)
        hid = take(T)
        take = carve(low)
        ext = take(CT + 2, EXT)
        vT = take(T)
        take = carve(high)
        qT = take(4, T)
        kT = take(T)
        v128 = take(NCH, P)
        kc = take(NB, SK)
        take = carve(mid)
        cos, sin, za, zs = take(T), take(T), take(T), take(T)
        vc = take(NB, P)
        v16 = take(NB, P)
        take = carve(mid)
        qs = take(2, 4, CH)
        qss = take(NB, 4 * TB)
        pr = take(2, 2 * 192)
        pT = take(2, 4, P)
        ob = take(2, P)
        obs = take(2, P)
        nsink = take(5)
        st = take(2, 16)
        lnsq = low[:, 4 * EXT:4 * EXT + CT * TN].rearrange("p (a b) -> p a b", a=CT)
        take = carve(low)
        mq, mk, mo, mv = take(2, T), take(2, T), take(2, T), take(2, T)
        ks = take(MD)
        take = carve(high)
        vaug = take(NLC + 1, MA)
        qext = take(2, QEXT)
        qx = take(2, NB, P)
        cst = take(2, MA)
        csl = take(NCS, 2 * MA)
        kwm = sb("kwm", [P, 2, MD])
        take = carve(high)
        gz, gt, glf, gb, gg, gd, gm, gp = [take(T) for _ in range(8)]
        take = carve(mid)
        mix = take(2, T)
        mneg = take(T)
        rows = mix[:, 0, :]
        eM = take(2, P)
        sT = take(2, P)
        tB = take(2, MA + 1)
        num = take(2, MA + 1)
        kw = take(2, MD)
        hn = take(2, MD)
        rtc = take(NLC + 1, 4, MH)
        rth = take(NLC + 1, 4)
        wc16 = take(16)
        wcb = take(MH, 16)
        wch = take(16)
        mend = take(16)
        ws8 = take(NB)
        sm = take(2, 8)
        wd = take(MH * 16)
        junk = take(MD)
        Q_INT, Q_WS, Q_G, Q_EM = range(4)

        cols_in, mats_in, cs_tab_in, cache_in, hist_in = [sem(n) for n in (
            "cols_in", "mats_in", "cos_sin_in", "cache_in", "hist_in")]
        x_in = [sem(f"x_in{k}") for k in range(KT)]
        w_in = [sem(f"w_in{s}") for s in range(2)]
        split_step, w_high, w_split = sem("split_step"), sem("w_high"), sem("w_split")
        block_done, evicted = sem("block_done"), sem("evicted")
        sq_done, ssq_done = sem("sq_done"), sem("ssq_done")
        aux_done, aux_read, rsum_done, rbc_done = [sem(n) for n in ("aux_done", "aux_read", "rsum_done", "rbc_done")]
        hi_done, lo_done, hsq_done, h_done = [sem(n) for n in ("hi_done", "lo_done", "hsq_done", "h_done")]
        pads, sig_done, ext_done, conv_done, rope_done, kc_done, kv_out = [sem(n) for n in (
            "pads", "sig_done", "ext_done", "conv_done", "rope_done", "kc_done", "kv_out")]
        conv_out = [sem(f"conv_state_out{j}") for j in range(CT)]
        pool_conv, ln_sum, ln_read = sem("pool_conv"), sem("ln_sum"), sem("ln_read")
        ln_sq, ln_v, ln_rstd, ln_scaled, ln_y, ln_hi, ln_lo = [sem("ln_" + n) for n in (
            "sq", "var", "rstd", "scaled", "y", "hi", "lo")]
        q_staged, s_done, stat_done, m_done, p_done, t_done, pt_done, ptb_done, pe_step, pv_done, den_done, o_done, ot_done, \
            ahi_done, mixed = [sem("att_" + n) for n in (
                "staged", "scores", "stat", "max", "probs", "tr", "tr_copied", "tr_last_copied", "step", "pv", "den", "out", "out_tr",
                "hi", "mixed")]
        spilled, gates_act, gate_rows, g_out = sem("spilled"), sem("gates_act"), sem("gate_rows"), sem("gate_out")
        par_in, head_set, qconv, qsilu, osig, vtr, vcp = [sem("m_" + n) for n in (
            "par_in", "head_set", "conv", "silu", "ogate", "vtr", "vcopied")]
        qh_in = [sem(f"m_hist_in{i}") for i in range(4)]
        qh_out = [sem(f"m_hist_out{i}") for i in range(4)]
        es_done, e_done, st_done, intra_done, kw_done, ab_done, tb_done, num_done, c_done, cu_done, dn_done, ss_done, \
            sc_own, sc_done, hn_done, ht_done, mix_done = [sem("m_" + n) for n in (
                "scores", "decay", "gated", "intra", "kw", "numer", "inter_scaled", "num", "delta", "state", "den",
                "ss", "pow", "scale", "hn", "hT", "mix")]
        cs_in = [sem(f"m_cs_in{s}") for s in range(NCS)]
        cs_out = [sem(f"m_cs_out{s}") for s in range(NCS)]
        qx_done, kwm_done, csc_done, csu_done, cp_out, mix_out = [sem("m_" + n) for n in (
            "qx", "kwm", "sample_delta", "sample_state", "prompt_out", "mix_out")]
        gact_own = sem("gates_act_own")
        vc_in, v_old_out, act_step = sem("cached_values_in"), sem("v_old_out"), sem("act_step")
        piece_done, piece_out = sem("piece_done"), sem("piece_out")
        back_high, back_split = sem("back_high"), sem("back_split")
        mix_back = [sem(f"mix_back{h}") for h in range(MH)]
        y_done, y_pool, y_scaled, y_out = sem("y_done"), sem("y_pool"), sem("y_scaled"), sem("y_out")

        block = es.enter_context(nc.Block())

        AX_R0, AX_KROPE, AX_V, AX_QROPE = 0, 3, 6, 12
        AX_R1 = AX_QROPE + 4 * NT
        AX_R2 = AX_R1 + NT
        AX_GT = AX_R2 + NT
        AX_WC = AX_GT + 3
        AX_R3 = AX_WC + 1
        AX_R4 = AX_R3 + NT

        UNITS = 2 * NCH + NB

        def earlier(c, p, k):
            p_ = (p - k) % 2
            d = (p_ - p + k) // 2
            if isinstance(c, int) and not 0 <= 2 * (c - d) + p_ < UNITS:
                return None
            return (c - d if d else c), p_

        def first_two(n):
            return isinstance(n, int) and n < 2

        def is_sample(c):
            return isinstance(c, int) and c >= NCH

        def result_places(c, p):
            if is_sample(c):
                b = 2 * (c - NCH) + p
                at = slice(TP + TB * b, TP + TB * (b + 1))
                return [(h_, slice(0, 4), at, psum[h_, 6 + p, P + h_.start:P + h_.stop].rearrange(
                    "p (j q) -> p j q", j=4)) for h_ in (slice(0, HD), slice(HD, P))]
            return [(slice(0, P), slice(2 * p, 2 * p + 2), bass.ds(CH * c, CH),
                     psum[:, 6 + p, P:2 * P].rearrange("p (j q) -> p j q", j=2))]

        def attention_steps(engine, step):
            for n in range(6):
                step(n // 2, n % 2)
            with engine.Fori(3, NCH) as c:
                step(c, 0)
                step(c, 1)
            for n in range(2 * NCH, UNITS + 3):
                step(n // 2, n % 2)

        def out3(b):
            s = 3 * (b % 2)
            return psum[:, s:s + 3, 0:TN]

        def by3(v):
            return v.rearrange("p (a b) -> p a b", a=NT)

        def gain(m, k):
            return cols[:, C_G + KT * m + k:C_G + KT * m + k + 1]

        def tok(i):
            return slice(i * TN, (i + 1) * TN)

        def sample(v, pre, width):
            return v.rearrange("p (b w) -> p b w", w=width)[:, :, pre:pre + TB]

        @block.sync
        def _(sp):
            def load(u, s, split):
                if split is not None:
                    sp.wait_ge(w_split, split)
                sp.dma_start(w_raw[:, s, :], t["wall"][u]).then_inc(w_in[s], 16)

            load(0, 0, None)
            load(1, 1, None)
            with sp.Fori(1, N_UNITS // 2) as i:
                for s in range(2):
                    load(2 * i + s, s, 2 * i + (s - 1))
            load(N_UNITS - 1, 0, N_UNITS - 2)

        @block.gpsimd
        def _(pool):
            def split(s, loads, units, used):
                pool.wait_ge(w_in[s], loads * 16)
                if used is not None:
                    pool.wait_ge(block_done, used)
                pool.sem_inc(split_step, 1)
                nc.gpsimd.tensor_scalar(w_hi[:, s, :], w_raw[:, s, :], 1.0, 1.0, ALU.mult, ALU.mult)\
                    .then_inc(w_high, 1)
                pool.wait_ge(w_high, units)
                nc.gpsimd.tensor_tensor(w_lo[:, s, :], w_raw[:, s, :], w_hi[:, s, :].bitcast(F32), ALU.subtract)\
                    .then_inc(w_split, 1)

            def single(u, used):
                split(u % 2, u // 2 + 1, u + 1, used)

            def ff(u0, b0):
                before = [-1, 0] + FF_BLOCKS[:6]
                with pool.Fori(0, FC) as c:
                    for j in range(8):
                        u = u0 + j
                        split(u % 2, 4 * c + (u // 2 + 1), 8 * c + (u + 1), 12 * c + (b0 + before[j]))

            product_p = vc.rearrange("p b k -> p (b k)")
            product_s = kwm[:, 0, 0:NB * TB]

            def tap(n):
                j, r = POOL_TAPS[n]
                src, dst = ext[:, SLOT_IN[j], :], ext[:, j, :]
                sdst = sample(dst[:, TP:T], 0, TB)
                ssrc = src[:, HIST + TP:EXT].rearrange("p (b w) -> p b w", w=HIST + TB)[:, :, r:r + TB]
                w = cols[:, C_CW + CW * j + r:C_CW + CW * j + r + 1]
                if n == 0:
                    pool.wait_ge(cols_in, 16)
                    pool.wait_ge(pads, 1)
                    pool.wait_ge(hist_in, 16 * CT)
                    pool.wait_ge(ext_done, j + 1)
                    cb = cols[:, C_CB + j:C_CB + j + 1]
                    nc.gpsimd.tensor_scalar(dst[:, 0:TP], src[:, 0:TP], w, cb, ALU.mult, ALU.add)\
                        .then_inc(pool_conv, 1)
                    nc.gpsimd.tensor_scalar(sdst, ssrc, w, cb, ALU.mult, ALU.add).then_inc(pool_conv, 1)
                    return
                if n == CW:
                    pool.wait_ge(conv_done, 2 * (DVE_TAPS[3] + T3))
                m = 4 * n - 2
                parts = [(dst[:, 0:TP], src[:, r:r + TP], product_p),
                         (sdst, ssrc, sample(product_s, 0, TB))]
                for q, (_, a, z) in enumerate(parts):
                    pool.wait_ge(pool_conv, m + q - 1)
                    nc.gpsimd.tensor_scalar(z, a, w, 1.0, ALU.mult, ALU.mult).then_inc(pool_conv, 1)
                for q, (o, _, z) in enumerate(parts):
                    pool.wait_ge(pool_conv, m + q + 1)
                    nc.gpsimd.tensor_tensor(o, o, z, ALU.add).then_inc(pool_conv, 1)

            single(0, None)
            single(1, None)
            taps = iter(range(len(POOL_TAPS)))
            for u in range(2, U_OUT0):
                single(u, u - 1)
                for _ in range(2 if u >= 5 else 0):
                    tap(next(taps))
            for n in taps:
                tap(n)
            pool.wait_ge(pool_conv, POOL_STEPS)
            pool.dma_start(vc[:, :, :], t["vcache"]).then_inc(vc_in, 16)
            pool.wait_ge(vc_in, 16)
            pool.dma_start(t["v_old"], vc[TB:WIN, :, :]).then_inc(v_old_out, 16)
            pool.wait_ge(v_old_out, 16)
            with pool.Fori(U_OUT0 // 2, U_FF0 // 2) as i:
                for s in range(2):
                    split(s, i + 1, 2 * i + (s + 1), 2 * i + (s - 1))
            ff(U_FF0, B_FF0)
            single(U_GATE, B_GATE - 2)
            single(U_HEAD, B_GATE)
            single(U_HEAD + 1, B_GATE + 1)
            pool.wait_ge(cols_in, 16)
            for j in (2, 3):
                single(U_HEAD + j, B_HEAD + j - 1)

            def head(h, last):
                def head_unit(j):
                    u = U_HEAD + j
                    split(u % 2, 4 * h + (u // 2 + 1), 8 * h + (u + 1), 8 * h + (B_HEAD + j - 1))

                for j in range(4, 8):
                    head_unit(j)
                for p in range(NLC + 1):
                    s = p % 2
                    pool.wait_ge(ss_done, 9 * h + (p + 1))
                    nc.gpsimd.tensor_tensor(sm[:, s, 4:5], sm[:, s, 3:4], cols[:, C_POW:C_POW + 1], ALU.add)\
                        .then_inc(sc_own, 1)
                    pool.wait_ge(sc_own, 18 * h + (2 * p + 1))
                    nc.gpsimd.tensor_tensor(sm[:, s, 5:6], sm[:, s, 4:5], cols[:, C_POW + 1:C_POW + 2], ALU.pow)\
                        .then_inc(sc_own, 1)
                    pool.wait_ge(sc_own, 18 * h + (2 * p + 2))
                    nc.gpsimd.tensor_tensor(sm[:, s, 6:7], sm[:, s, 5:6], sm[:, s, 2:3], ALU.mult)\
                        .then_inc(sc_done, 1)
                    if last and p > LAST_O:
                        k = p - LAST_O - 1
                        pool.wait_ge(mix_back[k // 2], 16)
                        nc.gpsimd.tensor_scalar(a_hi[:, k, :], back[:, k, :], 1.0, 1.0, ALU.mult, ALU.mult)\
                            .then_inc(back_high, 1)
                        pool.wait_ge(back_high, k + 1)
                        nc.gpsimd.tensor_tensor(a_lo[:, k, :], back[:, k, :], a_hi[:, k, :].bitcast(F32),
                                                ALU.subtract).then_inc(back_split, 1)
                    if p in (1, 2):
                        head_unit(p + 7)
                    if p in (7, 8) and not last:
                        head_unit(p + 3)

            with pool.Fori(0, MH - 1) as h:
                head(h, False)
            head(MH - 1, True)
            with pool.Fori(0, 3) as i:
                for s in range(2):
                    u = U_OUT1 + 2 + s
                    split(u % 2, i + (u // 2 + 1), 2 * i + (u + 1), 2 * i + (B_OUT1 + s + 1))
            ff(U_FF1, B_FF1)
            pool.wait_ge(rbc_done, 5)
            for k in range(KT - POOL_Y, KT):
                nc.gpsimd.tensor_tensor(x[:, k, :], x[:, k, :], rbc[:, :], ALU.mult).then_inc(y_pool, 1)

        @block.tensor
        def _(pe):
            mm = nc.tensor.matmul
            tr = nc.tensor.transpose

            def passes(s, k, kk, b, hi, lo, first, last):
                z = 3 * (b % 2)
                n = 0
                for w, a in ((w_hi, hi), (w_hi, lo), (w_lo, hi)):
                    for i in range(NT):
                        r = mm(psum[:, z + i, 0:TN], w[:, s, k * P:(k + 1) * P], a[:, kk, tok(i)],
                               start=first and n == 0, stop=last and n == 2)
                    n += 1
                return r

            def unit(s, units, b, free, ready=None):
                pe.wait_ge(w_split, units)
                if free is not None:
                    pe.wait_ge(evicted, free)
                for k in range(KT):
                    if ready is not None:
                        ready(k)
                    r = passes(s, k, k, b, a_hi, a_lo, k == 0, k == KT - 1)
                r.then_inc(block_done, 1)

            def aux(n, cells, done=True):
                if n >= 2:
                    pe.wait_ge(aux_read, n - 1)
                bank = 6 + n % 2
                for c in cells:
                    if len(c) == 3:
                        lo_, hi_, (a, b_, st_, sp_) = c
                        r = mm(psum[:, bank, lo_:hi_], a, b_, start=st_, stop=sp_)
                    else:
                        rows_, lo_, hi_, a = c
                        r = tr(psum[0:rows_, bank, lo_:hi_], a, ident)
                r.then_inc(aux_done, 1)

            def token_sums(n, m):
                pe.wait_ge(ssq_done, KT * (m + 1))
                for i in range(NT):
                    aux(n + i, [(0, TN, (ones, ssq[:, tok(i)], True, True))])

            def split_ready(base, sums=None):
                def ready(k):
                    if sums and k == KT - 2:
                        token_sums(*sums)
                    pe.wait_ge(lo_done, base + k + 1)
                return ready

            def ff(u0, b0, base, sums):
                unit(u0 % 2, u0 + 1, b0, b0 - 1, split_ready(base, sums))

                def chunk(c):
                    for j in range(1, FK):
                        u, b = u0 + j, b0 + j
                        unit(u % 2, 8 * c + (u + 1), b, 12 * c + (b - 1))
                    for j in range(4):
                        u = u0 + FK + j
                        pe.wait_ge(w_split, 8 * c + (u + 1))
                        for o in range(2):
                            b = b0 + FK + 2 * j + o
                            pe.wait_ge(evicted, 12 * c + (b - 1))
                            for k in range(FK):
                                if j == 0 and o == 0:
                                    pe.wait_ge(h_done, FK * c + (FK * FC * (b0 > B_GATE) + k + 1 + ONE))
                                r = passes(u % 2, FK * o + k, k, b, h_hi, h_lo, k == 0, k == FK - 1)
                            r.then_inc(block_done, 1)

                with pe.Fori(0, FC - 1) as c:
                    chunk(c)
                    unit(u0 % 2, 8 * c + (u0 + 9), b0, 12 * c + (b0 + 11))
                chunk(FC - 1)

            pe.wait_ge(mats_in, 16)
            unit(0, 1, 0, None, split_ready(0))
            token_sums(AX_R0, 0)
            unit(1, 2, 1, None)
            with pe.Fori(1, 5) as i:
                for s in range(2):
                    unit(s, 2 * i + (s + 1), s, 2 * i + (s - 1))

            def rope(n, b, src):
                pe.wait_ge(evicted, b + 1)
                for i in range(NT):
                    aux(n + i, [(0, TN, (mats[:, K_PERM, :], src[:, tok(i)], True, True))])

            unit(0, 11, 10, 9)
            rope(AX_KROPE, 8, kT)
            pe.wait_ge(evicted, 10)
            for g in range(4):
                aux(AX_V + g, [(P, P * i, P * i + P, vT[:, CH * (4 * g + i):CH * (4 * g + i) + P]) for i in range(4)])
            for g in range(2):
                aux(AX_V + 4 + g, [(TB, P * i, P * i + P, vT[:, TP + TB * (4 * g + i):TP + TB * (4 * g + i + 1)])
                                   for i in range(4)])
            for j in range(1, 4):
                unit((10 + j) % 2, 11 + j, 10 + j, 9 + j)
                rope(AX_QROPE + NT * (j - 1), 9 + j, qT[:, j - 1, :])
            rope(AX_QROPE + NT * 3, 13, qT[:, 3, :])

            def key_blocks(c):
                if isinstance(c, int) and c < 2:
                    return [(0, CH * (c + 1), 0, 0)]
                return [(0, P, 0, c - 2), (1, CH, P, c)]

            def scores(c, p):
                n = 2 * c + p
                if not first_two(n):
                    pe.wait_ge(p_done, n - 1)
                if is_sample(c):
                    b = n - 2 * NCH
                    pe.wait_ge(cache_in, 16)
                    pe.wait_ge(vc_in, 16)
                    pe.wait_ge(kc_done, 1)
                    for v in range(2):
                        h_ = slice(HD * v, HD * v + HD)
                        r = mm(psum[h_, p, 0:SK], qss[h_, b, :], kc[h_, b, :], start=True, stop=True)
                else:
                    pe.wait_ge(q_staged, n + 2)
                    w = CH * (c + 1) if isinstance(c, int) and c < 2 else 3 * CH
                    for v in range(2):
                        r = mm(psum[:, p, 192 * v:192 * v + w], qs[:, v, 2 * p:2 * p + 2, :],
                               kT[:, bass.ds(CH * c - (w - CH), w)], start=True, stop=True)
                r.then_inc(s_done, 1)

            def flip(c, p):
                n = 2 * c + p
                pe.wait_ge(p_done, n + 1)
                if not first_two(n):
                    pe.wait_ge(pt_done, n - 1)
                if not (isinstance(n, int) and n < 6):
                    pe.wait_ge(ptb_done, min(n - 5, 2 * NCH - 4) if isinstance(n, int) else n - 5)
                pe.sem_inc(pe_step, 1)
                if is_sample(c):
                    tr(psum[:, 2 + 2 * p, 0:P], pr[:, p, 0:P], ident)
                    r = tr(psum[0:TB, 2 + 2 * p, P:2 * P], pr[:, p, P:SK], ident)
                else:
                    for v in range(2):
                        for g, w, k0, _ in key_blocks(c):
                            r = tr(psum[0:w, 2 + 2 * p + g, P * v:P * v + P], pr[:, p, 192 * v + k0:192 * v + k0 + w],
                                   ident)
                r.then_inc(t_done, 1)

            def weigh(c, p):
                n = 2 * c + p
                pe.wait_ge(pt_done, n + 1)
                if not (isinstance(c, int) and (c < 2 or c >= NCH)):
                    pe.wait_ge(ptb_done, n - 3)
                if not first_two(n):
                    pe.wait_ge(mixed, n - 1)
                pe.sem_inc(pe_step, 1)
                if is_sample(c):
                    b = n - 2 * NCH
                    for v in range(2):
                        h_ = slice(HD * v, HD * v + HD)
                        mm(psum[h_, 6 + p, 0:HD], pT[:, p, 0, h_], vc[:, b, h_], start=True, stop=False)
                        r = mm(psum[h_, 6 + p, 0:HD], pT[0:TB, p, 1, h_], v16[0:TB, b, h_], start=False, stop=True)
                else:
                    parts = key_blocks(c)
                    for v in range(2):
                        for g, w, _, tile in parts:
                            r = mm(psum[:, 6 + p, HD * v:HD * v + HD], pT[0:w, p, 2 * g + v, :],
                                   v128[0:w, tile, HD * v:HD * v + HD], start=g == 0, stop=g == len(parts) - 1)
                r.then_inc(pv_done, 1)

            def flip_out(c, p):
                pe.wait_ge(o_done, 2 * c + p + 1)
                tr(psum[:, 6 + p, P:2 * P], (obs if is_sample(c) else ob)[:, p, :], ident).then_inc(ot_done, 1)

            def layer_norm(n):
                if n == 2 * NCH + 1:
                    pe.wait_ge(conv_done, 2 * (DVE_TAPS[3] + T3))
                    pe.wait_ge(pool_conv, POOL_STEPS)
                    pe.wait_ge(ptb_done, 2 * NCH - 4)
                for g in {1: (0, 1), 3: (2,), 5: (3,), 6: (4,), 7: (5,)}.get(n - 2 * NCH, ()):
                    i = g % NT
                    if g >= 2:
                        pe.wait_ge(ln_read, g - 1)
                    if g >= NT:
                        pe.wait_ge(ln_sq, i + 1)
                    for j in range(CT):
                        r = mm(psum[:, 3 + 2 * (g % 2), 0:TN], ones, ext[:, j, tok(i)] if g < NT else lnsq[:, j, :],
                               start=j == 0, stop=j == CT - 1)
                    r.then_inc(ln_sum, 1)

            def step(c, p):
                for k, stage in ((0, scores), (3, flip_out), (2, weigh), (1, flip)):
                    u = earlier(c, p, k)
                    if u:
                        stage(*u)
                if isinstance(c, int):
                    layer_norm(2 * c + p)

            pe.wait_ge(evicted, B_OUT0)
            pe.wait_ge(aux_read, AX_R1)
            attention_steps(pe, step)

            pe.wait_ge(mixed, 2 * NCH + NB)
            pe.wait_ge(ln_read, 2 * NT)

            def normed_conv(k):
                if k == CT:
                    pe.wait_ge(ln_lo, NT)
            for j in range(2):
                unit(j, U_OUT0 + j + 1, j, B_OUT0 + j - 1, None if j else normed_conv)
            with pe.Fori(1, 4) as i:
                for s in range(2):
                    unit(s, 2 * i + (U_OUT0 + s + 1), s, 2 * i + (B_OUT0 + s - 1))
            ff(U_FF0, B_FF0, KT, (AX_R1, 1))

            unit(0, U_GATE + 1, B_GATE, B_GATE - 1, split_ready(2 * KT, (AX_R2, 2)))
            for j in range(3):
                unit((U_HEAD + j) % 2, U_HEAD + j + 1, B_HEAD + j, B_HEAD + j - 1)
            pe.wait_ge(gates_act, 4)
            for g in range(3):
                aux(AX_GT + g, [(P, P * i, P * i + P, rows[:, P * (4 * g + i):P * (4 * g + i + 1)])
                                for i in range(min(4, NLC + 1 - 4 * g))])
            pe.wait_ge(gate_rows, GATE_ROWS)
            aux(AX_WC, [(0, MH * 16, (ones[0:MH, :], wd[0:MH, :], True, True))])
            pe.wait_ge(aux_read, AX_R3)

            def head(h, last):
                def turn(n, src):
                    if n >= 2:
                        pe.wait_ge(vcp, 10 * h + (n - 1))
                    for j in range(2):
                        r = tr(psum[:, 6 + n % 2, P * j:P * j + P], src(j), ident)
                    r.then_inc(vtr, 1)

                for j in range(2, 6):
                    b = B_HEAD + j
                    if j > 2:
                        unit((U_HEAD + j) % 2, 8 * h + (U_HEAD + j + 1), b, 8 * h + (b - 1))
                    else:
                        pe.wait_ge(evicted, 8 * h + (B_HEAD + 2))
                    for n in range(2 * j - 4, 2 * j - 2 + (j == 5)):
                        turn(n, lambda i: mv[:, i, LC * n:LC * (n + 1)])
                pe.wait_ge(qsilu, 4 * h + 2)
                turn(NLC + 1, lambda i: mk[:, i, TP:T])
                b = B_HEAD + 6
                unit((U_HEAD + 6) % 2, 8 * h + (U_HEAD + 7), b, 8 * h + (b - 1))
                pe.wait_ge(vcp, 10 * h + 10)
                pe.wait_ge(qsilu, 4 * h + 4)
                pe.wait_ge(par_in, 16 * h + 16)

                def piece(m):
                    if last and m > 2:
                        return
                    i, j = (m, 7) if m < 3 else ((m - 3) // 2, 8 + (m - 3) % 2)
                    s = (U_HEAD + j) % 2
                    if i == 0:
                        pe.wait_ge(w_split, 8 * h + (U_HEAD + j + 1))
                    if m in (3, 8):
                        pe.wait_ge(evicted, 8 * h + (B_HEAD + (8 if m == 3 else 9)))
                    elif m > 0:
                        pe.wait_ge(piece_out, PIECES * h + (m - (m > 3)))
                    for k in range(KT):
                        for q, (w, a) in enumerate(((w_hi, a_hi), (w_hi, a_lo), (w_lo, a_hi))):
                            r = mm(psum[:, PIECE_BANK, 0:TN], w[:, s, k * P:(k + 1) * P], a[:, k, tok(i)],
                                   start=k == 0 and q == 0, stop=k == KT - 1 and q == 2)
                    r.then_inc(piece_done if i < 2 else block_done, 1)

                def scores(p):
                    c, s = SEQ[p], p % 2
                    if p >= 2:
                        pe.wait_ge(st_done, 9 * h + (p - 1))
                        pe.wait_ge(kw_done, 8 * h + (p - 1 if p < NLC else NLC - 1))
                    q = slice(LC * c, LC * (c + 1))
                    mm(psum[:, s, 0:P], head_par[0:MH, H_SEL:H_SEL + P], mneg[0:MH, q], start=True, stop=False)
                    mm(psum[:, s, 0:P], ident, mats[:, K_CAUS if c < NLC else K_BLK, :], start=False, stop=True)
                    for k in range(2):
                        r = mm(psum[:, s, P:2 * P], mk[:, k, q], mq[:, k, q], start=k == 0, stop=k == 1)
                    if c < NLC:
                        for k in range(2):
                            r = tr(psum[:, s, 2 * P + P * k:3 * P + P * k], mk[:, k, q], ident)
                    r.then_inc(es_done, 1)

                def intra(p):
                    pe.wait_ge(st_done, 9 * h + (p + 1))
                    if p >= 1:
                        pe.wait_ge(num_done, 9 * h + p)
                    if p >= 2:
                        pe.wait_ge(mix_done, 9 * h + (p - 1 + ONE))
                    mm(psum[:, 2, 0:MA], sT[:, p % 2, :], vaug[:, SEQ[p], :], start=True, stop=True)\
                        .then_inc(intra_done, 1)

                def stream(b, c, first):
                    s = b % NCS
                    pe.wait_ge(cs_in[s], 16 * CS_USES * h + 16 * (b // NCS + 1))
                    for k in range(2):
                        r = mm(psum[:, STREAM_BANK, 0:MA], qx[:, k, b, :], csl[:, s, MA * k:MA * (k + 1)],
                               start=b == 0 and k == 0, stop=b == NB - 1 and k == 1)
                    if b == NB - 1:
                        r.then_inc(ab_done, 1)
                    pe.wait_ge(kwm_done, 8 * h + (b + 1))
                    if first:
                        pe.wait_ge(cu_done, 9 * h + (c + 2))
                    else:
                        pe.wait_ge(csu_done, 8 * h + (b + ONE))
                    for k in range(2):
                        r = mm(psum[:, 4 + k, 0:MA], kwm[:, b % 2, P * k:P * k + P], vaug[:, NLC, :],
                               start=True, stop=True)
                    r.then_inc(csc_done, 1)

                def hidden_back(p):
                    pe.wait_ge(hn_done, 9 * h + (p + 1))
                    if p >= 1:
                        pe.wait_ge(mix_done, 9 * h + (p + ONE))
                    pe.wait_ge(num_done, 9 * h + min(p + 2, NLC + 1))
                    pe.wait_ge(tb_done, 9 * h + min(p + 2, NLC + 1))
                    for k in range(2):
                        r = tr(psum[:, 2 + k, HT:HT + P], hn[:, p % 2, P * k:P * k + P], ident)
                    r.then_inc(ht_done, 1)

                scores(0)
                pe.wait_ge(qx_done, h + 1)
                pe.wait_ge(evicted, 8 * h + (B_HEAD + 7))
                for p in range(NLC + 1):
                    c = SEQ[p]
                    q = slice(LC * c, LC * (c + 1))
                    if p < NLC:
                        scores(p + 1)
                        piece(p)
                    intra(p)
                    if c < NLC:
                        pe.wait_ge(cu_done, 9 * h + (c + 1))
                        if p >= 1:
                            pe.wait_ge(tb_done, 9 * h + p)
                        for k in range(2):
                            r = mm(psum[:, 3, 0:MA], mq[:, k, q], cst[:, k, :], start=k == 0, stop=k == 1)
                        r.then_inc(ab_done, 1)
                        pe.wait_ge(kw_done, 8 * h + (c + 1))
                        if c >= 1:
                            pe.wait_ge(csu_done, 8 * h + (min(c + (c == NLC - 1), NB) + ONE))
                        for k in range(2):
                            r = mm(psum[:, 4 + k, 0:MA], kw[:, c % 2, P * k:P * k + P], vaug[:, c, :],
                                   start=True, stop=True)
                        r.then_inc(c_done, 1)
                    for b in STREAMS[p]:
                        stream(b, c, b == STREAMS[p][0])
                    if p >= 1:
                        hidden_back(p - 1)
                piece(NLC)
                hidden_back(NLC)
                if not last:
                    pe.wait_ge(mix_done, 9 * h + (9 + ONE))
                    pe.wait_ge(csu_done, 8 * h + (8 + ONE))
                    b = B_HEAD + 10
                    unit((U_HEAD + 2) % 2, 8 * h + (U_HEAD + 11), b, 8 * h + (b - 1))

            with pe.Fori(0, MH - 1) as h:
                head(h, False)
            head(MH - 1, True)

            pe.wait_ge(mix_done, 9 * MH + ONE)
            pe.wait_ge(csu_done, 8 * MH + ONE)
            def heads_split(k):
                if k < KT - 2:
                    pe.wait_ge(back_split, k + 1)
                else:
                    pe.wait_ge(lo_done, 3 * KT + (k - KT + 3))

            for j in range(8):
                u, b = U_OUT1 + j, B_OUT1 + j
                unit(u % 2, u + 1, b, b - 1, heads_split if j == 0 else None)
            ff(U_FF1, B_FF1, 3 * KT + 2, (AX_R3, 3))
            token_sums(AX_R4, 4)

        @block.vector
        def _(dve):
            V = nc.vector
            for counted in [h_done, mix_done, csu_done, mix_out, cp_out] + cs_out + qh_out:
                dve.sem_inc(counted, ONE)

            def rest(m, k, n, src=None):
                dve.wait_ge(hi_done, n)
                src = x[:, k, :] if src is None else src
                V.scalar_tensor_tensor(out=a_lo[:, k, :], in0=src, scalar=1.0 if m is None else gain(m, k),
                                       in1=a_hi[:, k, :].bitcast(F32), op0=ALU.mult, op1=ALU.subtract)\
                    .then_inc(lo_done, 1)

            def add_squares(m, k):
                n = KT * m + k
                dve.wait_ge(sq_done, n + 1)
                q = (sq, hid)[k % 2]
                if k == 0:
                    V.tensor_copy(ssq[:, :], q).then_inc(ssq_done, 1)
                else:
                    dve.wait_ge(ssq_done, n)
                    V.tensor_tensor(ssq[:, :], ssq[:, :], q, ALU.add).then_inc(ssq_done, 1)

            def token_scale(n, m):
                for i in range(NT):
                    dve.wait_ge(aux_done, n + i + 1)
                    V.tensor_scalar(rbc[:, tok(i)], psum[:, 6 + (n + i) % 2, 0:TN], 1.0 / D, EPS, ALU.mult, ALU.add)\
                        .then_inc(aux_read, 1)
                dve.wait_ge(aux_read, n + NT)
                V.reciprocal(rbc[:, :], rbc[:, :]).then_inc(rsum_done, 1)
                dve.wait_ge(rbc_done, m + 1)

            def project(b, dst):
                dve.wait_ge(block_done, b + 1)
                V.tensor_tensor(by3(dst), out3(b), by3(rbc[:, :]), ALU.mult).then_inc(evicted, 1)

            def residual(b, count, k, x_ready=None):
                dve.wait_ge(block_done, count)
                if x_ready is not None:
                    dve.wait_ge(x_in[k], x_ready)
                V.tensor_tensor(by3(x[:, k, :]), out3(b), by3(x[:, k, :]), ALU.add).then_inc(evicted, 1)

            def ff(b0, m, last):
                hb = FK * FC * (b0 > B_GATE)

                def up(c, j):
                    dve.wait_ge(block_done, 12 * c + (b0 + j + 1))
                    dve.wait_ge(h_done, FK * c + (hb + j + ONE))
                    V.scalar_tensor_tensor(out=by3(hid), in0=out3(b0 + j), scalar=0.0, in1=by3(rbc[:, :]),
                                           op0=ALU.max, op1=ALU.mult).then_inc(evicted, 1)
                    dve.wait_ge(hsq_done, FK * c + (hb + j + 1))
                    V.tensor_tensor(h_lo[:, j, :], hid, h_hi[:, j, :].bitcast(F32), ALU.subtract).then_inc(h_done, 1)

                with dve.Fori(0, FC - 1) as c:
                    for j in range(FK):
                        up(c, j)
                    for k in range(KT):
                        residual(b0 + FK + k, 12 * c + (b0 + FK + k + 1), k)
                for j in range(FK):
                    up(FC - 1, j)
                for k in range(KT):
                    residual(b0 + FK + k, 12 * (FC - 1) + (b0 + FK + k + 1), k)
                    if not last:
                        rest(m, k, (m if m < 3 else m + 1) * KT + k + 1)
                    add_squares(m, k)

            dve.wait_ge(cols_in, 16)
            dve.wait_ge(mats_in, 16)
            for k in range(KT):
                rest(0, k, k + 1)
                add_squares(0, k)
            V.memset(ext[:, 2:CT + 2, 0:HIST], 0.0).then_inc(pads, 1)
            token_scale(AX_R0, 0)

            def glu(j):
                project(2 * j, za)
                project(2 * j + 1, zs)
                dve.wait_ge(sig_done, j + 1)
                e = ext[:, SLOT_IN[j], :]
                V.tensor_tensor(e[:, HIST:HIST + TP], za[:, 0:TP], zs[:, 0:TP], ALU.mult)
                V.tensor_tensor(sample(e[:, HIST + TP:EXT], HIST, HIST + TB), sample(za[:, TP:T], 0, TB),
                                sample(zs[:, TP:T], 0, TB), ALU.mult).then_inc(ext_done, 1)

            def conv(j, first, last):
                src, dst = ext[:, SLOT_IN[j], :], ext[:, j, :]
                sdst = sample(dst[:, TP:T], 0, TB)
                ssrc = src[:, HIST + TP:EXT].rearrange("p (b w) -> p b w", w=HIST + TB)
                n = 2 * DVE_TAPS[j]
                if first == 0:
                    w = cols[:, C_CW + CW * j:C_CW + CW * j + 1]
                    cb = cols[:, C_CB + j:C_CB + j + 1]
                    dve.wait_ge(ext_done, j + 1)
                    dve.wait_ge(pads, 1)
                    dve.wait_ge(hist_in, 16 * CT)
                    if j > 0:
                        dve.wait_ge(conv_done, n)
                        dve.wait_ge(conv_out[SLOT_IN.index(j)], 32)
                    V.tensor_scalar(dst[:, 0:TP], src[:, 0:TP], w, cb, ALU.mult, ALU.add).then_inc(conv_done, 1)
                    V.tensor_scalar(sdst, ssrc[:, :, 0:TB], w, cb, ALU.mult, ALU.add).then_inc(conv_done, 1)
                    first = 1
                with dve.Fori(first, last) as r:
                    w = cols[:, bass.ds(r + (C_CW + CW * j), 1)]
                    dve.wait_ge(conv_done, 2 * r + (n - 1))
                    V.scalar_tensor_tensor(out=dst[:, 0:TP], in0=src[:, bass.ds(r, TP)], scalar=w,
                                           in1=dst[:, 0:TP], op0=ALU.mult, op1=ALU.add).then_inc(conv_done, 1)
                    dve.wait_ge(conv_done, 2 * r + n)
                    V.scalar_tensor_tensor(out=sdst, in0=ssrc[:, :, bass.ds(r, TB)], scalar=w,
                                           in1=sdst, op0=ALU.mult, op1=ALU.add).then_inc(conv_done, 1)

            def rope(n, dst, tile):
                for i in range(NT):
                    dve.wait_ge(aux_done, n + i + 1)
                    V.tensor_tensor(za[:, tok(i)], psum[:, 6 + (n + i) % 2, 0:TN], sin[:, tok(i)], ALU.mult)\
                        .then_inc(aux_read, 1)
                    V.tensor_tensor(dst[:, tok(i)], dst[:, tok(i)], cos[:, tok(i)], ALU.mult).then_inc(rope_done, 1)
                    dve.wait_ge(aux_read, n + i + 1)
                    dve.wait_ge(rope_done, 2 * (NT * tile + i) + 1)
                    V.tensor_tensor(dst[:, tok(i)], dst[:, tok(i)], za[:, tok(i)], ALU.add).then_inc(rope_done, 1)

            glu(0)
            conv(0, 0, 13)
            glu(1)
            conv(0, 13, 28)
            glu(2)
            conv(0, 28, CW)
            conv(2, 0, 11)
            glu(3)
            conv(2, 11, 17)
            project(8, kT)
            conv(2, 17, 23)
            project(9, vT)
            conv(2, 23, 29)
            project(10, qT[:, 0, :])
            dve.wait_ge(cs_tab_in, 32)
            rope(AX_KROPE, kT, 0)
            for g in range(6):
                dve.wait_ge(aux_done, AX_V + g + 1)
                n, dst = (P, v128[:, 4 * g:4 * g + 4, :]) if g < 4 else (TB, v16[0:TB, 4 * g - 16:4 * g - 12, :])
                V.tensor_copy(dst, psum[0:n, 6 + g % 2, :].rearrange("p (a b) -> p a b", a=4)).then_inc(aux_read, 1)
            dve.wait_ge(cache_in, 16)
            dve.wait_ge(rope_done, 2 * NT)
            V.tensor_copy(kc[:, :, WIN:SK], sample(kT[:, TP:T], 0, TB)).then_inc(kc_done, 1)
            conv(2, 29, CW)
            conv(3, 0, 7)
            project(11, qT[:, 1, :])
            rope(AX_QROPE, qT[:, 0, :], 1)
            conv(3, 7, 10)
            project(12, qT[:, 2, :])
            rope(AX_QROPE + NT, qT[:, 1, :], 2)
            conv(3, 10, T3)
            project(13, qT[:, 3, :])
            rope(AX_QROPE + 2 * NT, qT[:, 2, :], 3)
            rope(AX_QROPE + 3 * NT, qT[:, 3, :], 4)

            rows_v = zs[:, :]

            def centre(i):
                dve.wait_ge(ln_sum, i + 1)
                for j in range(CT):
                    r = V.scalar_tensor_tensor(out=ext[:, j, tok(i)], in0=psum[:, 3 + 2 * (i % 2), 0:TN],
                                               scalar=-1.0 / (CT * P), in1=ext[:, j, tok(i)],
                                               op0=ALU.mult, op1=ALU.add)
                r.then_inc(ln_read, 1)

            def variance(i):
                n = NT + i
                dve.wait_ge(ln_sum, n + 1)
                V.tensor_scalar(rows_v[:, tok(i)], psum[:, 3 + 2 * (n % 2), 0:TN], 1.0 / (CT * P), EPS,
                                ALU.mult, ALU.add).then_inc(ln_read, 1)
                dve.wait_ge(ln_read, n + 1)
                V.reciprocal(rows_v[:, tok(i)], rows_v[:, tok(i)]).then_inc(ln_v, 1)

            def scaled(i):
                dve.wait_ge(ln_rstd, i + 1)
                V.tensor_tensor(ext[:, 0:CT, tok(i)], ext[:, 0:CT, tok(i)],
                                rows_v[:, tok(i)].unsqueeze(1).to_broadcast([P, CT, TN]), ALU.mult)\
                    .then_inc(ln_scaled, 1)

            def conv_split(i):
                dve.wait_ge(ln_y, CT * (i + 1))
                V.tensor_scalar(a_hi[:, CT:2 * CT, tok(i)], ext[:, 0:CT, tok(i)], 1.0, None, ALU.mult)\
                    .then_inc(ln_hi, 1)
                dve.wait_ge(ln_hi, i + 1)
                V.tensor_tensor(a_lo[:, CT:2 * CT, tok(i)], ext[:, 0:CT, tok(i)],
                                a_hi[:, CT:2 * CT, tok(i)].bitcast(F32), ALU.subtract).then_inc(ln_lo, 1)

            def stage(c, p):
                n = 2 * c + p
                if not first_two(n):
                    dve.wait_ge(s_done, n - 1)
                for v in range(2):
                    h_ = slice(HD * v, HD * v + HD)
                    r = V.tensor_scalar(qs[h_, v, 2 * p:2 * p + 2, :], qT[h_, 2 * p:2 * p + 2, bass.ds(CH * c, CH)],
                                        1.0, None, ALU.mult)
                r.then_inc(q_staged, 1)

            def maxima(c, p):
                n = 2 * c + p
                width, col = (1, 4) if is_sample(c) else (2, 2 * p)
                if is_sample(c):
                    src = psum[:, p, 0:SK].unsqueeze(1)
                else:
                    w = CH * (c + 1) if isinstance(c, int) and c < 2 else 3 * CH
                    src = psum[:, p, 0:384].rearrange("p (v k) -> p v k", v=2)[:, :, 0:w]
                dve.wait_ge(s_done, n + 1)
                if not first_two(n):
                    dve.wait_ge(p_done, n - 1)
                V.tensor_reduce(st[:, p, 0:width], src, AX, ALU.max).then_inc(stat_done, 1)
                dve.wait_ge(stat_done, n + (NSINK + 1))
                V.scalar_tensor_tensor(out=st[:, p, 2:2 + width], in0=st[:, p, 0:width], scalar=-ATT_SCALE,
                                       in1=nsink[:, col:col + width], op0=ALU.mult, op1=ALU.min).then_inc(m_done, 1)

            def denominators(c, p):
                n, width = 2 * c + p, 1 if is_sample(c) else 2
                dve.wait_ge(p_done, n + 1)
                V.tensor_tensor(st[:, p, 8:8 + width], st[:, p, 6:6 + width], st[:, p, 10:10 + width], ALU.add)\
                    .then_inc(den_done, 1)
                dve.wait_ge(den_done, 2 * n + 1)
                if not first_two(n):
                    dve.wait_ge(o_done, n - 1)
                V.reciprocal(st[:, p, 12:12 + width], st[:, p, 8:8 + width]).then_inc(den_done, 1)

            def output(c, p):
                n = 2 * c + p
                dve.wait_ge(pv_done, n + 1)
                dve.wait_ge(den_done, 2 * n + 2)
                if not first_two(n):
                    dve.wait_ge(ot_done, n - 1)
                if is_sample(c):
                    for v in range(2):
                        h_ = slice(HD * v, HD * v + HD)
                        r = V.tensor_scalar(obs[h_, p, h_], psum[h_, 6 + p, 0:HD], st[h_, p, 12:13], None, ALU.mult)
                else:
                    r = V.tensor_tensor(ob[:, p, :].rearrange("p (v d) -> p v d", v=2),
                                        psum[:, 6 + p, 0:P].rearrange("p (v d) -> p v d", v=2),
                                        st[:, p, 12:14].unsqueeze(2).to_broadcast([P, 2, HD]), ALU.mult)
                r.then_inc(o_done, 1)

            def mixed_in(c, p):
                n = 2 * c + p
                places = result_places(c, p)
                dve.wait_ge(ahi_done, n + 1)
                for h_, k, at, src in places:
                    r = V.tensor_tensor(a_lo[h_, k, at], src, a_hi[h_, k, at].bitcast(F32), ALU.subtract)
                r.then_inc(mixed, 1)

            def copy_last(c, p):
                if isinstance(c, int) and (c < 2 or c >= NCH):
                    return
                n = 2 * c + p
                dve.wait_ge(t_done, n + 1)
                dve.wait_ge(pv_done, n - 1)
                V.tensor_scalar(pT[0:CH, p, 2:4, :], psum[0:CH, 3 + 2 * p, 0:2 * P].rearrange("p (v q) -> p v q", v=2),
                                1.0, None, ALU.mult).then_inc(ptb_done, 1)

            def step(c, p):
                for k, part in ((0, maxima), (-1, stage), (1, denominators), (3, mixed_in), (2, output),
                                (1, copy_last)):
                    u = earlier(c, p, k)
                    if u and not (k == -1 and is_sample(u[0])):
                        part(*u)
                if isinstance(c, int):
                    i = 2 * c + p - 2 * NCH - 2
                    if 0 <= i < NT:
                        centre(i)
                    if 0 <= i - 4 < NT:
                        variance(i - 4)

            dve.wait_ge(rope_done, 2 * NT * 5)
            V.memset(qs[:, :, :, :], 0.0).then_inc(stat_done, 1)
            V.memset(obs[:, :, :], 0.0)
            V.tensor_scalar(nsink, cols[:, C_SINK:C_SINK + 5], -1.0, None, ALU.mult).then_inc(stat_done, 1)
            dve.wait_ge(stat_done, NSINK)
            V.tensor_copy(qss.rearrange("p b (j t) -> p b j t", j=4),
                          qT[:, :, TP:T].rearrange("p j (b t) -> p b j t", t=TB)).then_inc(q_staged, 1)
            stage(0, 0)
            attention_steps(dve, step)
            for i in range(NT):
                scaled(i)
            for i in range(NT):
                conv_split(i)

            for k in range(KT):
                residual(B_OUT0 + k, B_OUT0 + k + 1, k, 32)
                if k < KT - 1:
                    add_squares(1, k)
            for k in range(KT):
                rest(1, k, KT + k + 1)
            add_squares(1, KT - 1)
            token_scale(AX_R1, 1)
            ff(B_FF0, 2, False)

            token_scale(AX_R2, 2)
            rowc = [0]

            def row(ins):
                rowc[0] += 1
                ins.then_inc(gate_rows, 1)
                dve.wait_ge(gate_rows, rowc[0])

            def first_values(j):
                dve.wait_ge(spilled, 16 * KT)
                project(B_HEAD + j, mv[:, j, :])

            R4 = slice(0, MH)
            row(V.memset(gp[R4, :], 1.0))
            row(V.memset(gp[R4, 0:TP:LC], 0.0))
            row(V.memset(gp[R4, TP:T:TB], 0.0))
            V.memset(gd[R4, :], 0.0)
            V.memset(rows[:, :], 0.0)
            dve.wait_ge(block_done, B_GATE + 1)
            gsrc = out3(B_GATE)
            V.tensor_tensor(by3(gz)[0:64], gsrc[0:64], by3(rbc[:, :])[0:64], ALU.mult).then_inc(evicted, 1)
            dve.wait_ge(evicted, B_GATE + 1)
            row(V.tensor_scalar(gt[0:64, :], gz[0:64, :], cols[0:64, C_GB:C_GB + 1], None, ALU.add))
            row(V.tensor_scalar(gm[32:36, :], gt[32:36, :], 0.0, None, ALU.min))
            dve.wait_ge(gates_act, 1)
            row(V.tensor_tensor(glf[R4, :], gm[32:36, :], gz[32:36, :], ALU.subtract))
            first_values(0)
            row(V.tensor_tensor_scan(gb[R4, :], gp[R4, :], glf[R4, :], 0.0, ALU.mult, ALU.add))
            row(V.tensor_tensor(gg[R4, :], gt[R4, :], gb[R4, :], ALU.subtract))
            row(V.tensor_copy(gz[R4, :], gg[R4, :]))
            m0 = cols[R4, C_M0:C_M0 + NB]
            row(V.tensor_tensor(gz[R4, TP:T:TB], gg[R4, TP:T:TB], m0, ALU.max))
            row(V.tensor_copy(gd[R4, LC:TP:LC], gb[R4, LC - 1:TP - 1:LC]))
            row(V.memset(gd[R4, TP:T:TB], NEG))
            row(V.tensor_tensor_scan(gm[R4, :], gd[R4, :], gz[R4, :], 0.0, ALU.add, ALU.max))
            V.tensor_tensor(mend[R4, 0:8], gb[R4, LC - 1:TP:LC], gm[R4, LC - 1:TP:LC], ALU.add)
            row(V.tensor_tensor(mend[R4, 8:16], gb[R4, TP + TB - 1:T:TB], gm[R4, TP + TB - 1:T:TB], ALU.add))
            first_values(1)
            row(V.memset(gp[R4, 0:LC], 0.0))
            row(V.tensor_copy(gp[R4, LC:TP].rearrange("p (c t) -> p c t", t=LC),
                              mend[R4, 0:7].unsqueeze(2).to_broadcast([MH, NLC - 1, LC])))
            row(V.tensor_copy(gp[R4, TP:T].rearrange("p (c t) -> p c t", t=TB),
                              m0.unsqueeze(2).to_broadcast([MH, NB, TB])))
            row(V.tensor_copy(gd[R4, 0:TP].rearrange("p (c t) -> p c t", t=LC),
                              gm[R4, LC - 1:TP:LC].unsqueeze(2).to_broadcast([MH, NLC, LC])))
            row(V.tensor_copy(gd[R4, TP:T].rearrange("p (c t) -> p c t", t=TB),
                              gm[R4, TP + TB - 1:T:TB].unsqueeze(2).to_broadcast([MH, NB, TB])))
            V.tensor_scalar(mneg[R4, :], gm[R4, :], -1.0, None, ALU.mult)
            V.tensor_tensor(rows[0:4, :], gp[R4, :], gm[R4, :], ALU.subtract)
            V.tensor_tensor(rows[32:36, :], gg[R4, :], gd[R4, :], ALU.subtract)
            V.tensor_copy(rows[64:68, :], gg[R4, :])
            V.scalar_tensor_tensor(out=rows[96:100, :], in0=gb[R4, :], scalar=-1.0, in1=gm[R4, :],
                                   op0=ALU.mult, op1=ALU.subtract)
            V.tensor_tensor(wc16[R4, 0:8], gp[R4, 0:TP:LC], gd[R4, 0:TP:LC], ALU.subtract)
            row(V.tensor_tensor(wc16[R4, 8:16], gp[R4, TP:T:TB], gd[R4, TP:T:TB], ALU.subtract))
            assert rowc[0] == GATE_TO_EXP
            dve.wait_ge(gates_act, 4)
            row(V.tensor_tensor(wd[R4, :].rearrange("p (h i) -> p h i", h=MH), wc16[R4, :].unsqueeze(1).to_broadcast([MH, MH, 16]),
                                cols[R4, C_MH:C_MH + MH * 16].rearrange("p (h i) -> p h i", h=MH), ALU.mult))
            assert rowc[0] == GATE_ROWS
            for g in range(3):
                dve.wait_ge(aux_done, AX_GT + g + 1)
                k = min(4, NLC + 1 - 4 * g)
                V.tensor_copy(rtc[:, 4 * g:4 * g + k, :, :],
                              psum[:, 6 + (AX_GT + g) % 2, 0:P * k].rearrange("p (c q r) -> p c q r", c=k, q=4)[:, :, :, 0:MH])\
                    .then_inc(aux_read, 1)
            dve.wait_ge(aux_done, AX_WC + 1)
            V.tensor_copy(wcb[:, :, :], psum[:, 6 + AX_WC % 2, 0:MH * 16].rearrange("p (h i) -> p h i", h=MH))\
                .then_inc(aux_read, 1)
            dve.wait_ge(aux_read, AX_WC + 1)
            row(V.tensor_scalar(rtc[:, :, Q_WS, :], rtc[:, :, Q_WS, :], MD ** -0.5, None, ALU.mult))

            V.memset(qext[:, :, 0:QH], 0.0)
            V.memset(vaug[:, :, MD:MA], 1.0)
            row(V.memset(qx[:, :, :, :], 0.0))

            def head(h, last):
                dve.wait_ge(mix_done, 9 * h + ONE)
                V.tensor_scalar(rth[:, :, :], rtc[:, :, :, bass.ds(h, 1)].rearrange("p c q o -> p c (q o)"),
                                1.0, None, ALU.mult)
                V.tensor_scalar(wch[:, :], wcb[:, bass.ds(h, 1), :].rearrange("p o i -> p (o i)"),
                                1.0, None, ALU.mult).then_inc(head_set, 1)
                dve.wait_ge(head_set, 2 * h + 1)
                V.tensor_scalar(ws8[:, :], cols[:, C_BSEL:C_BSEL + NB], rth[:, NLC, Q_WS:Q_WS + 1], None, ALU.mult)\
                    .then_inc(head_set, 1)
                dve.wait_ge(cp_out, 16 * h + ONE)
                V.memset(cst[:, :, :], 0.0).then_inc(cu_done, 1)

                def qk_ext(j):
                    i, s = j - 2, j % 2
                    e, z = qext[:, s, :], out3(B_HEAD + j)
                    dve.wait_ge(block_done, 8 * h + (B_HEAD + j + 1))
                    dve.wait_ge(qh_in[i], 16 * h + 16)
                    dve.wait_ge(qh_out[(i + 2) % 4], 32 * h + (32 * (i >= 2) + ONE))
                    V.tensor_tensor(e[:, QH:QH + 2 * TN].rearrange("p (a b) -> p a b", a=2), z[:, 0:2, :],
                                    by3(rbc[:, :])[:, 0:2, :], ALU.mult)
                    V.tensor_tensor(e[:, QH + 2 * TN:QH + TP], z[:, 2, 0:TP - 2 * TN], rbc[:, 2 * TN:TP], ALU.mult)
                    V.tensor_tensor(sample(e[:, QH + TP:QEXT], QH, QH + TB), sample(z[:, 2, TP - 2 * TN:TN], 0, TB),
                                    sample(rbc[:, TP:T], 0, TB), ALU.mult).then_inc(evicted, 1)
                    dve.wait_ge(evicted, 8 * h + (B_HEAD + j + 1))
                    if i == 0:
                        dve.wait_ge(par_in, 16 * h + 16)
                    dst = mk[:, i, :] if i < 2 else mq[:, i - 2, :]
                    es_ = e[:, QH + TP:QEXT].rearrange("p (b w) -> p b w", w=QH + TB)
                    for r in range(QW):
                        w = head_par[:, H_W + QW * i + r:H_W + QW * i + r + 1]
                        for part, (o, a) in enumerate((
                                (dst[:, 0:TP], e[:, r:r + TP]),
                                (sample(dst[:, TP:T], 0, TB), es_[:, :, r:r + TB]))):
                            if r == 0:
                                V.tensor_scalar(o, a, w, head_par[:, H_B + i:H_B + i + 1], ALU.mult, ALU.add)\
                                    .then_inc(qconv, 1)
                            else:
                                dve.wait_ge(qconv, 32 * h + (8 * i + 2 * r + part - 1))
                                V.scalar_tensor_tensor(out=o, in0=a, scalar=w, in1=o, op0=ALU.mult, op1=ALU.add)\
                                    .then_inc(qconv, 1)

                for j in range(2, 6):
                    qk_ext(j)
                dve.wait_ge(qsilu, 4 * h + 4)
                for b in range(NB):
                    r = V.tensor_copy(qx[:, :, b, TB * b:TB * (b + 1)], mq[:, :, TP + TB * b:TP + TB * (b + 1)])
                r.then_inc(qx_done, 1)
                dve.wait_ge(block_done, 8 * h + (B_HEAD + 7))
                V.tensor_tensor(by3(mo[:, 0, :]), out3(B_HEAD + 6), by3(rbc[:, :]), ALU.mult).then_inc(evicted, 1)
                dve.wait_ge(mix_out, 16 * h + ONE)

                def piece(m):
                    if last and m > 2:
                        return
                    i, j = (m, 7) if m < 3 else ((m - 3) // 2, 8 + (m - 3) % 2)
                    if i < 2:
                        dve.wait_ge(piece_done, PIECES * h + (m + 1 - (m > 2)))
                    else:
                        dve.wait_ge(block_done, 8 * h + (B_HEAD + j + 1))
                    if m == 3:
                        dve.wait_ge(vcp, 10 * h + 9)
                    dst = mo[:, 1, tok(i)] if j == 7 else mv[:, j - 8, tok(i)]
                    V.tensor_tensor(dst, psum[:, PIECE_BANK, 0:TN], rbc[:, tok(i)], ALU.mult)\
                        .then_inc(piece_out if i < 2 else evicted, 1)

                def gated(p):
                    s = p % 2
                    dve.wait_ge(e_done, 9 * h + (p + 1))
                    if SEQ[p] < NLC:
                        dve.wait_ge(kw_done, 8 * h + (SEQ[p] + 1))
                    V.scalar_tensor_tensor(out=sT[:, s, :], in0=psum[:, s, P:2 * P], scalar=MD ** -0.5,
                                           in1=eM[:, s, :], op0=ALU.mult, op1=ALU.mult).then_inc(st_done, 1)

                def numerator(p):
                    s = p % 2
                    dve.wait_ge(intra_done, 9 * h + (p + 1))
                    dve.wait_ge(tb_done, 9 * h + (p + 1))
                    V.tensor_tensor(num[:, s, 0:MA], psum[:, 2, 0:MA], tB[:, s, 0:MA], ALU.add).then_inc(num_done, 1)
                    dve.wait_ge(num_done, 9 * h + (p + 1))
                    den = num[:, s, MD:MA]
                    V.scalar_tensor_tensor(out=sm[:, s, 0:1], in0=den, scalar=-1.0, in1=den, op0=ALU.mult,
                                           op1=ALU.max).then_inc(dn_done, 1)
                    dve.wait_ge(dn_done, 27 * h + (3 * p + 1))
                    V.tensor_scalar(sm[:, s, 1:2], sm[:, s, 0:1], rth[:, SEQ[p], Q_EM:Q_EM + 1], None, ALU.max)\
                        .then_inc(dn_done, 1)
                    dve.wait_ge(dn_done, 27 * h + (3 * p + 2))
                    V.reciprocal(sm[:, s, 2:3], sm[:, s, 1:2]).then_inc(dn_done, 1)

                def normed(p):
                    s = p % 2
                    dve.wait_ge(sc_done, 9 * h + (p + 1))
                    V.tensor_scalar(hn[:, s, :], num[:, s, 0:MD], sm[:, s, 6:7], 16.0, ALU.mult, ALU.mult)\
                        .then_inc(hn_done, 1)

                def gate_out(p):
                    c = SEQ[p]
                    q = slice(LC * c, LC * (c + 1))
                    dve.wait_ge(ht_done, 9 * h + (p + 1))
                    dve.wait_ge(osig, 4 * h + (LC * c // TN + 2))
                    for k in range(2):
                        r = V.scalar_tensor_tensor(out=mix[:, k, q], in0=psum[:, 2 + k, HT:HT + P],
                                                   scalar=head_par[:, H_G + k:H_G + k + 1], in1=mo[:, k, q],
                                                   op0=ALU.mult, op1=ALU.mult)
                    r.then_inc(mix_done, 1)

                def updated(b):
                    s = b % NCS
                    dve.wait_ge(csc_done, 8 * h + (b + 1))
                    m = csl[:, s, :].rearrange("p (k e) -> p k e", k=2)
                    V.scalar_tensor_tensor(out=m, in0=m, scalar=wch[:, 8 + b:9 + b], in1=psum[:, 4:6, 0:MA],
                                           op0=ALU.mult, op1=ALU.add).then_inc(csu_done, 1)

                gated(0)
                for p in range(NLC + 1):
                    c = SEQ[p]
                    if p < NLC:
                        gated(p + 1)
                        piece(p)
                    if c < NLC:
                        dve.wait_ge(c_done, 8 * h + (c + 1))
                        V.scalar_tensor_tensor(out=cst[:, :, :], in0=cst[:, :, :], scalar=wch[:, c:c + 1],
                                               in1=psum[:, 4:6, 0:MA], op0=ALU.mult, op1=ALU.add).then_inc(cu_done, 1)
                    numerator(p)
                    for b in STREAMS[p]:
                        updated(b)
                    if p >= 1:
                        gate_out(p - 1)
                    normed(p)
                piece(NLC)
                gate_out(NLC)

            with dve.Fori(0, MH - 1) as h:
                head(h, False)
            head(MH - 1, True)

            for k in range(2):
                rest(None, KT - 2 + k, 3 * KT + 1 + k, src=mix[:, k, :])
            for k in range(KT):
                residual(B_OUT1 + k, B_OUT1 + k + 1, k, 48)
                if k < KT - 1:
                    add_squares(3, k)
            for k in range(KT):
                rest(3, k, 3 * KT + 2 + k + 1)
            add_squares(3, KT - 1)
            token_scale(AX_R3, 3)
            ff(B_FF1, 4, True)

            token_scale(AX_R4, 4)
            for k in range(KT - POOL_Y):
                V.scalar_tensor_tensor(out=x[:, k, :], in0=x[:, k, :], scalar=gain(4, k), in1=rbc[:, :],
                                       op0=ALU.mult, op1=ALU.mult).then_inc(y_done, 1)

        @block.scalar
        def _(act):
            A = nc.scalar.activation
            dma = act.dma_start

            def high_part(m, k, src=None):
                src = x[:, k, :] if src is None else src
                A(a_hi[:, k, :], src, ACT.Copy, scale=1.0 if m is None else gain(m, k)).then_inc(hi_done, 1)

            def square(m, k):
                n = KT * m + k
                if n >= 2:
                    act.wait_ge(ssq_done, n - 1)
                A((sq, hid)[k % 2], x[:, k, :], ACT.Square).then_inc(sq_done, 1)

            def root(m):
                act.wait_ge(rsum_done, m + 1)
                A(rbc[:, :], rbc[:, :], ACT.Sqrt).then_inc(rbc_done, 1)

            def ff(b0, m, last):
                hb = FK * FC * (b0 > B_GATE)

                def up(c, j):
                    act.wait_ge(evicted, 12 * c + (b0 + j + 1))
                    A(h_hi[:, j, :], hid, ACT.Square)
                    A(hid, hid, ACT.Square).then_inc(hsq_done, 1)

                with act.Fori(0, FC) as c:
                    for j in range(FK):
                        up(c, j)
                for k in range(KT):
                    act.wait_ge(evicted, 12 * (FC - 1) + (b0 + FK + k + 1))
                    if not last:
                        high_part(m, k)
                    square(m, k)
                    if not last:
                        dma(t["x_spill"][k], x[:, k, :]).then_inc(spilled, 16)

            dma(cols[:, :], t["cols"]).then_inc(cols_in, 16)
            dma(mats[:, :, :], t["mats"]).then_inc(mats_in, 16)
            for k in range(KT):
                dma(x[:, k, :], t["x"][k]).then_inc(x_in[k], 16)
            dma(kc[:, :, 0:WIN], t["kcache"]).then_inc(cache_in, 16)

            act.wait_ge(cols_in, 16)
            for k in range(KT):
                act.wait_ge(x_in[k], 16)
                high_part(0, k)
                square(0, k)
            act.wait_ge(lo_done, KT)
            act.wait_ge(sq_done, KT)
            for j in range(CT):
                dma(ext[:, SLOT_IN[j], HIST + TP:EXT].rearrange("p (b w) -> p b w", w=HIST + TB)[:, :, 0:HIST],
                    t["conv_hist"][j]).then_inc(hist_in, 16)
            root(0)
            act.wait_ge(rbc_done, 1)
            dma(cos, t["cos"]).then_inc(cs_tab_in, 16)
            dma(sin, t["sin"]).then_inc(cs_tab_in, 16)

            for j in range(CT):
                act.wait_ge(evicted, 2 * j + 2)
                A(zs, zs, ACT.Sigmoid).then_inc(sig_done, 1)
                act.wait_ge(ext_done, j + 1)
                e = ext[:, SLOT_IN[j], :]
                dma(t["conv_p"][j], e[:, TP:TP + HIST]).then_inc(conv_out[j], 16)
                act.wait_ge(hist_in, 16 * CT)
                dma(t["conv_s"][j], e[:, HIST + TP:EXT].rearrange("p (b w) -> p b w", w=HIST + TB)[:, :, TB:])\
                    .then_inc(conv_out[j], 16)
            act.wait_ge(evicted, 10)
            dma(t["v_p"], vT[:, TP - WIN:TP]).then_inc(kv_out, 16)
            dma(t["v_s"], vT[:, TP:T]).then_inc(kv_out, 16)
            act.wait_ge(kc_done, 1)
            dma(t["k_p"], kT[:, TP - WIN:TP]).then_inc(kv_out, 16)
            dma(t["k_s"], kc[:, :, TB:SK]).then_inc(kv_out, 16)

            def probs(c, p):
                n = 2 * c + p
                act.wait_ge(m_done, n + 1)
                if not first_two(n):
                    act.wait_ge(t_done, n - 1)
                    act.wait_ge(den_done, 2 * n - 2)
                if is_sample(c):
                    cells = [(0, 0, SK)]
                else:
                    w = CH * (c + 1) if isinstance(c, int) and c < 2 else 3 * CH
                    cells = [(v, 192 * v, w) for v in range(2)]
                for v, a, w in cells:
                    A(pr[:, p, a:a + w], psum[:, p, a:a + w], ACT.Exp, bias=st[:, p, 2 + v:3 + v], scale=ATT_SCALE,
                      accum_out=st[:, p, 6 + v:7 + v])
                col = C_SINK + (4 if is_sample(c) else 2 * p)
                for v, _, _ in cells:
                    r = A(st[:, p, 10 + v:11 + v], cols[:, col + v:col + v + 1], ACT.Exp, bias=st[:, p, 2 + v:3 + v])
                r.then_inc(p_done, 1)

            def copy_first(c, p):
                n = 2 * c + p
                act.wait_ge(t_done, n + 1)
                if not first_two(n):
                    act.wait_ge(pv_done, n - 1)
                if is_sample(c):
                    A(pT[:, p, 0, :], psum[:, 2 + 2 * p, 0:P], ACT.Copy)
                    r = A(pT[0:TB, p, 1, :], psum[0:TB, 2 + 2 * p, P:2 * P], ACT.Copy)
                else:
                    w = CH if isinstance(c, int) and c == 0 else P
                    r = A(pT[0:w, p, 0:2, :], psum[0:w, 2 + 2 * p, 0:2 * P].rearrange("p (v q) -> p v q", v=2), ACT.Copy)
                r.then_inc(pt_done, 1)

            def result_high(c, p):
                n = 2 * c + p
                act.wait_ge(ot_done, n + 1)
                act.sem_inc(act_step, 1)
                for h_, k, at, src in result_places(c, p):
                    r = A(a_hi[h_, k, at], src, ACT.Copy)
                r.then_inc(ahi_done, 1)

            def step(c, p):
                for k, part in ((3, result_high), (0, probs), (1, copy_first)):
                    u = earlier(c, p, k)
                    if u:
                        part(*u)
                i = 2 * c + p - 2 * NCH - 4 if isinstance(c, int) else -1
                if 0 <= i < NT:
                    if i == 0:
                        for j in (1, 3):
                            act.wait_ge(conv_out[j], 32)
                    act.wait_ge(ln_read, i + 1)
                    if i > 0:
                        act.wait_ge(ln_sum, NT + i)
                    A(lnsq[:, :, :], ext[:, 0:CT, tok(i)], ACT.Square).then_inc(ln_sq, 1)

            attention_steps(act, step)

            for i in range(NT):
                act.wait_ge(ln_v, i + 1)
                A(zs[:, tok(i)], zs[:, tok(i)], ACT.Sqrt).then_inc(ln_rstd, 1)
            for i in range(NT):
                act.wait_ge(ln_scaled, i + 1)
                for j in range(CT):
                    A(ext[:, j, tok(i)], ext[:, j, tok(i)], ACT.Silu, bias=cols[:, C_LB + j:C_LB + j + 1],
                      scale=cols[:, C_LG + j:C_LG + j + 1]).then_inc(ln_y, 1)
            act.wait_ge(ln_lo, NT)
            act.wait_ge(kv_out, 16 * 4)
            for j in range(CT):
                act.wait_ge(conv_out[j], 32)
            for k in range(KT):
                dma(x[:, k, :], t["x"][k]).then_inc(x_in[k], 16)

            for k in range(KT - 1):
                act.wait_ge(evicted, B_OUT0 + k + 1)
                square(1, k)
            act.wait_ge(block_done, B_OUT0 + KT)
            for k in range(KT):
                if k == KT - 1:
                    act.wait_ge(evicted, B_OUT0 + KT)
                high_part(1, k)
            square(1, KT - 1)
            root(1)
            ff(B_FF0, 2, False)

            root(2)
            act.wait_ge(gate_rows, 5)
            A(gz[32:36, :], gt[32:36, :], ACT.Abs).then_inc(gact_own, 1)
            act.wait_ge(gact_own, 1)
            A(gz[32:36, :], gz[32:36, :], ACT.Exp, scale=-1.0).then_inc(gact_own, 1)
            act.wait_ge(gact_own, 2)
            A(gz[32:36, :], gz[32:36, :], ACT.Ln, bias=1.0).then_inc(gates_act, 1)
            act.wait_ge(gate_rows, GATE_TO_EXP)
            for q in (0, 32, 96):
                r = A(rows[q:q + MH, :], rows[q:q + MH, :], ACT.Exp)
                if q:
                    r.then_inc(gates_act, 1)
            A(wc16[0:MH, :], wc16[0:MH, :], ACT.Exp).then_inc(gates_act, 1)
            dma(t["m_out"], mend[0:MH, :]).then_inc(g_out, 16)
            act.wait_ge(gate_rows, GATE_ROWS + 2)

            def head(h, last):
                act.wait_ge(mix_done, 9 * h + ONE)
                dma(head_par[:, :], t["head_par"][h]).then_inc(par_in, 16)

                def history(i):
                    e = qext[:, i % 2, QH + TP:QEXT].rearrange("p (b w) -> p b w", w=QH + TB)
                    dma(e[:, :, 0:QH], t["qk_hist"][h, i]).then_inc(qh_in[i], 16)

                def sample_in(b):
                    s = b % NCS
                    act.wait_ge(cs_out[s], 16 * CS_USES * h + (16 * (b // NCS) + ONE))
                    dma(csl[:, s, :], t["mem_in"][h, b]).then_inc(cs_in[s], 16)

                for i in (2, 3):
                    act.wait_ge(qh_out[i], 32 * h + ONE)
                history(0)
                history(1)
                for b in range(NCS):
                    sample_in(b)
                def turned(n, dst):
                    act.wait_ge(vtr, 10 * h + (n + 1))
                    A(dst, psum[:, 6 + n % 2, 0:MD], ACT.Copy).then_inc(vcp, 1)

                for i in range(4):
                    j = i + 2
                    act.wait_ge(evicted, 8 * h + (B_HEAD + j + 1))
                    act.wait_ge(qh_in[i], 16 * h + 16)
                    e = qext[:, i % 2, :]
                    dma(t["qk_p"][h, i], e[:, TP:TP + QH]).then_inc(qh_out[i], 16)
                    dma(t["qk_s"][h, i], e[:, QH + TP:QEXT].rearrange("p (b w) -> p b w", w=QH + TB)[:, :, TB:])\
                        .then_inc(qh_out[i], 16)
                    for n in range(2 * i, 2 * i + 2 + (i == 3)):
                        turned(n, vaug[:, n, 0:MD])
                    if i == 3:
                        turned(NLC + 1, ks)
                    act.wait_ge(qconv, 32 * h + 8 * (i + 1))
                    dst = mk[:, i, :] if i < 2 else mq[:, i - 2, :]
                    A(dst, dst, ACT.Silu).then_inc(qsilu, 1)
                    if i < 2:
                        act.wait_ge(qh_out[i], 32 * h + (32 + ONE))
                        history(i + 2)
                act.wait_ge(evicted, 8 * h + (B_HEAD + 7))
                A(mo[:, 0, :], mo[:, 0, :], ACT.Sigmoid).then_inc(osig, 1)
                act.wait_ge(head_set, 2 * h + 2)

                def decay(p):
                    s = p % 2
                    act.wait_ge(es_done, 9 * h + (p + 1))
                    A(eM[:, s, :], psum[:, s, 0:P], ACT.Exp, bias=rth[:, SEQ[p], Q_G:Q_G + 1]).then_inc(e_done, 1)

                def keys(c):
                    s = c % 2
                    if c >= 2:
                        act.wait_ge(c_done, 8 * h + (c - 1))
                    z = (c if c < NLC - 1 else NLC) % 2
                    A(kw[:, s, :], psum[:, z, 2 * P:2 * P + MD], ACT.Copy, scale=rth[:, c, Q_WS:Q_WS + 1])\
                        .then_inc(kw_done, 1)

                def inter(p):
                    s, z = p % 2, 3 if SEQ[p] < NLC else STREAM_BANK
                    act.wait_ge(ab_done, 9 * h + (p + 1))
                    A(tB[:, s, 0:MA], psum[:, z, 0:MA], ACT.Copy, scale=rth[:, SEQ[p], Q_INT:Q_INT + 1])\
                        .then_inc(tb_done, 1)

                def sumsq(p):
                    s = p % 2
                    act.wait_ge(dn_done, 27 * h + (3 * p + 3))
                    A(junk, num[:, s, 0:MD], ACT.Square, scale=sm[:, s, 2:3], accum_out=sm[:, s, 3:4])\
                        .then_inc(ss_done, 1)

                def masked_keys(b):
                    if b >= 2:
                        act.wait_ge(csc_done, 8 * h + (b - 1))
                    A(kwm[:, b % 2, :], ks, ACT.Copy, scale=ws8[:, b:b + 1]).then_inc(kwm_done, 1)

                def sample_out(b):
                    s = b % NCS
                    act.wait_ge(csu_done, 8 * h + (b + 1 + ONE))
                    dma(t["mem_s"][h, b], csl[:, s, :]).then_inc(cs_out[s], 16)

                def ogate(m):
                    if m < 2:
                        act.wait_ge(piece_out, PIECES * h + (m + 1))
                    else:
                        act.wait_ge(evicted, 8 * h + (B_HEAD + 8))
                    A(mo[:, 1, tok(m)], mo[:, 1, tok(m)], ACT.Sigmoid).then_inc(osig, 1)

                decay(0)
                keys(0)
                masked_keys(0)
                for p in range(NLC + 1):
                    c = SEQ[p]
                    if p < NLC:
                        decay(p + 1)
                        if SEQ[p + 1] < NLC:
                            keys(SEQ[p + 1])
                    inter(p)
                    sumsq(p)
                    if p < 3:
                        ogate(p)
                    for b in (STREAMS[p + 1] if p < NLC else []):
                        masked_keys(b)
                    for b in (STREAMS[p - 1] if p else []):
                        sample_out(b)
                    if p >= 2:
                        for b in STREAMS[p - 2]:
                            if b + NCS < NB:
                                sample_in(b + NCS)
                    if last and LAST_O <= p < LAST_O + MH - 1:
                        act.wait_ge(block_done, B_OUT1)
                        act.wait_ge(mix_out, 16 * (MH - 1) + ONE)
                        g = p - LAST_O
                        dma(back[:, 2 * g:2 * g + 2, :], t["mix_spill"][g]).then_inc(mix_back[g], 16)
                act.wait_ge(cu_done, 9 * h + 9)
                dma(t["mem_p"][h], cst[:, :, :]).then_inc(cp_out, 16)
                act.wait_ge(mix_done, 9 * h + (9 + ONE))
                if not last:
                    dma(t["mix_spill"][h], mix[:, :, :]).then_inc(mix_out, 16)

            with act.Fori(0, MH - 1) as h:
                head(h, False)
            head(MH - 1, True)

            for k in range(2):
                high_part(None, KT - 2 + k, mix[:, k, :])
            for i in range(4):
                act.wait_ge(qh_out[i], 32 * MH + ONE)
            for k in range(KT):
                dma(x[:, k, :], t["x_spill"][k]).then_inc(x_in[k], 16)
            for s in range(NCS):
                act.wait_ge(cs_out[s], 16 * CS_USES * MH + ONE)
            act.wait_ge(cp_out, 16 * MH + ONE)
            for k in range(KT - 1):
                act.wait_ge(evicted, B_OUT1 + k + 1)
                square(3, k)
            act.wait_ge(block_done, B_OUT1 + KT)
            for k in range(KT):
                if k == KT - 1:
                    act.wait_ge(evicted, B_OUT1 + KT)
                high_part(3, k)
            square(3, KT - 1)
            root(3)
            ff(B_FF1, 4, True)

            root(4)
            for k in range(KT - POOL_Y):
                act.wait_ge(y_done, k + 1)
                dma(t["y"][k], x[:, k, :]).then_inc(y_out, 16)
            for i in range(POOL_Y):
                k = KT - POOL_Y + i
                act.wait_ge(y_pool, i + 1)
                A(x[:, k, :], x[:, k, :], ACT.Copy, scale=gain(4, k)).then_inc(y_scaled, 1)
                act.wait_ge(y_scaled, i + 1)
                dma(t["y"][k], x[:, k, :]).then_inc(y_out, 16)
            act.wait_ge(y_out, 16 * KT)
            act.wait_ge(g_out, 16)


F = "float32"
_OUTS = {
    "y": (KT, P, T), "conv_p": (CT, P, HIST), "conv_s": (CT, P, NB, HIST), "v_p": (P, WIN), "v_s": (P, NB * TB),
    "v_old": (WIN - TB, NB, P), "k_p": (P, WIN), "k_s": (P, NB, WIN), "qk_p": (MH, 4, P, QH),
    "qk_s": (MH, 4, P, NB, QH), "mem_p": (MH, P, 2, MA), "mem_s": (MH, NB, P, 2 * MA), "m_out": (MH, 16),
    "x_spill": (KT, P, T), "mix_spill": (MH, P, 2, T),
}


def _lay_out(i):
    import numpy as np

    def by_k(w):
        n = w.shape[1] // P
        return w.reshape(KT, P, n, P).transpose(2, 1, 0, 3).reshape(n, P, KT * P)

    def channels(v):
        return np.asarray(v).reshape(-1, P).T

    a = {}
    x = np.concatenate([i["x_prompt"][0], i["x_sample"].reshape(NB * TB, D)])
    a["x"] = x.T.reshape(KT, P, T)
    w = i["w_in_even"][0]
    half = CT * P
    glu = w[:, 768:].reshape(D, 2, CT, P).transpose(0, 2, 1, 3).reshape(D, 2 * half)
    q = w[:, :512].reshape(D, 2, 4, HD).transpose(0, 2, 1, 3).reshape(D, 512)
    wo = i["w_out_even"][0]
    wo = np.concatenate([wo[:512].reshape(2, 4, HD, D).transpose(1, 0, 2, 3).reshape(512, D), wo[512:]])
    units = [by_k(glu), by_k(w[:, 512:768]), by_k(q), by_k(wo)]

    def ffn(layer):
        w1 = by_k(i["w_ff1"][layer]).reshape(FC, FK, P, KT * P)
        w2 = i["w_ff2"][layer].reshape(FC, FK, P, 4, 2, P).transpose(0, 3, 2, 4, 1, 5).reshape(FC, 4, P, KT * P)
        return np.concatenate([w1, w2], axis=1).reshape(FC * 8, P, KT * P)
    units.append(ffn(0))
    w = i["w_in_odd"][0]
    gates = np.zeros((D, P), w.dtype)
    gates[:, 0:MH] = w[:, 4 * D:4 * D + MH]
    gates[:, 32:32 + MH] = w[:, 4 * D + MH:]
    heads = w[:, :4 * D].reshape(D, 4, MH, MD)[:, [2, 1, 0, 3]].transpose(0, 2, 1, 3).reshape(D, 4 * D)
    units += [by_k(gates), by_k(heads), by_k(i["w_out_odd"][0]), ffn(1)]
    a["wall"] = np.concatenate(units)
    c = np.zeros((P, NCOL), np.float32)
    for n, g in enumerate([i["norm_mix_g"][0], i["norm_ffn_g"][0], i["norm_mix_g"][1], i["norm_ffn_g"][1],
                           i["norm_out_g"]]):
        c[:, C_G + KT * n:C_G + KT * (n + 1)] = channels(g)
    c[:, C_CW:C_CB] = i["conv_w"][0].reshape(CW, CT, P).transpose(2, 1, 0).reshape(P, CT * CW)
    c[:, C_CB:C_CB + CT] = channels(i["conv_b"][0])
    c[:, C_LG:C_LG + CT] = channels(i["conv_ln_g"][0])
    c[:, C_LB:C_LB + CT] = channels(i["conv_ln_b"][0])
    sink = i["attn_sink"][0]
    for p in range(2):
        for v in range(2):
            c[:, C_SINK + 2 * p + v] = np.repeat(sink[4 * v + 2 * p:4 * v + 2 * p + 2], CH)
    c[:, C_SINKS] = np.repeat(sink, TB)
    c[0:MH, C_GB] = i["gate_b_i"][0]
    c[32:32 + MH, C_GB] = i["gate_b_f"][0]
    c[:, C_BSEL:C_BSEL + NB] = np.repeat(np.eye(NB, dtype=np.float32), TB, axis=0)
    c[0:MH, C_M0:C_M0 + NB] = i["state_mlstm_m"][0].T
    c[:, C_POW] = MD * EPS
    c[:, C_POW + 1] = -0.5
    c[0:MH, C_MH:C_MH + MH * 16] = np.repeat(np.eye(MH, dtype=np.float32), 16, axis=1)
    a["cols"] = c
    m = np.zeros((P, NK, P), np.float32)
    m[:, K_ID] = np.eye(P)
    m[:, K_ONE] = 1
    for base in (0, HD):
        for r in range(8):
            m[base + 8 + r, K_PERM, base + r] = -1
            m[base + r, K_PERM, base + 8 + r] = 1
    at = np.arange(P)
    causal = at[:, None] <= at[None, :]
    m[:, K_CAUS] = np.where(causal, 0, NEG)
    m[:, K_BLK] = np.where(causal & (at[:, None] // TB == at[None, :] // TB), 0, NEG)
    a["mats"] = m
    pos = np.concatenate([np.arange(TP), np.tile(1024 + np.arange(TB), NB)]).astype(np.float32)
    inv = np.float32(500000.0) ** (-np.arange(8, dtype=np.float32) / np.float32(8))
    ang = inv[:, None] * pos[None, :]
    cos, sin = np.ones((P, T), np.float32), np.zeros((P, T), np.float32)
    for base in (0, 8, HD, HD + 8):
        cos[base:base + 8] = np.cos(ang)
        sin[base:base + 8] = np.sin(ang)
    a["cos"], a["sin"] = cos, sin
    a["kcache"] = i["cache_swa_k"][0].transpose(2, 3, 0, 1).reshape(P, NB, WIN)
    a["vcache"] = i["cache_swa_v"][0].transpose(1, 0, 2, 3).reshape(WIN, NB, P)
    a["conv_hist"] = i["state_conv"][0].reshape(NB, HIST, CT, P).transpose(2, 3, 0, 1)

    def by_head(v):
        v = np.asarray(v).reshape(v.shape[:-1] + (2, MH, 2, P))
        v = np.flip(v, -4)
        n = v.ndim
        v = np.moveaxis(v, (n - 3, n - 4, n - 2, n - 1), (0, 1, 2, 3))
        return v.reshape((MH, 4, P) + v.shape[4:])
    a["qk_hist"] = by_head(i["state_qk_conv"][0])
    hp = np.zeros((MH, P, NH), np.float32)
    hp[:, :, H_W:H_W + 16] = by_head(i["qk_conv_w"][0]).transpose(0, 2, 1, 3).reshape(MH, P, 16)
    hp[:, :, H_B:H_B + 4] = by_head(i["qk_conv_b"][0]).transpose(0, 2, 1)
    hp[:, :, H_G:H_G + 2] = i["mlstm_norm_g"][0].reshape(MH, 2, P).transpose(0, 2, 1)
    for h in range(MH):
        hp[h, h, H_SEL:] = 1
    a["head_par"] = hp
    mem = np.concatenate([i["state_mlstm_C"][0].transpose(0, 1, 3, 2), i["state_mlstm_n"][0][..., None]], axis=-1)
    a["mem_in"] = mem.reshape(NB, MH, 2, P, MA).transpose(1, 0, 3, 2, 4).reshape(MH, NB, P, 2 * MA)
    return {k: np.ascontiguousarray(v) for k, v in a.items()}


def _put_back(r):
    import numpy as np

    y = r["y"].reshape(D, T).T
    out = [y[:TP][None], y[TP:].reshape(NB, TB, D)]

    def heads(v):
        return v.T.reshape(1, 1, -1, 2, HD)
    kp, vp = heads(r["k_p"]), heads(r["v_p"])
    cp = r["conv_p"].transpose(2, 0, 1).reshape(1, 1, HIST, CT * P)

    def from_heads(v):
        v = v.reshape((MH, 2, 2, P) + v.shape[3:])
        n = v.ndim
        v = np.moveaxis(v, (0, 1, 2, 3), (n - 3, n - 4, n - 2, n - 1))
        v = np.flip(v, -4)
        return v.reshape(v.shape[:-4] + (2 * D,))
    qp = from_heads(r["qk_p"]).reshape(1, 1, QH, 2 * D)
    qs = from_heads(r["qk_s"]).reshape(1, NB, QH, 2 * D)
    mp = r["mem_p"].transpose(0, 2, 1, 3).reshape(1, 1, MH, MD, MA)
    ms = r["mem_s"].reshape(MH, NB, P, 2, MA).transpose(1, 0, 3, 2, 4).reshape(1, NB, MH, MD, MA)
    m = r["m_out"]
    ks = r["k_s"].reshape(2, HD, NB, WIN).transpose(2, 3, 0, 1)[None]
    vs = np.concatenate([r["v_old"].transpose(1, 0, 2), r["v_s"].reshape(P, NB, TB).transpose(1, 2, 0)], axis=1)
    vs = vs.reshape(1, NB, WIN, 2, HD)
    cs = r["conv_s"].transpose(2, 3, 0, 1).reshape(1, NB, HIST, CT * P)
    out += [kp, vp, cp, qp, mp[..., :MD].swapaxes(-1, -2), mp[..., MD], m[:, 7].reshape(1, 1, MH),
            ks, vs, cs, qs, ms[..., :MD].swapaxes(-1, -2), ms[..., MD], m[:, 8:].T.reshape(1, NB, MH)]
    return tuple(np.ascontiguousarray(o) for o in out)


def kernel(**inputs):
    import numpy as np
    import concourse.bacc as bacc
    from concourse.bass_utils import run_bass_kernel_spmd

    arrays = _lay_out({k: np.asarray(v) for k, v in inputs.items()})
    nc = bacc.Bacc("TRN2", target_bir_lowering=False, num_devices=1)
    t = {}
    for name, a in arrays.items():
        t[name] = nc.dram_tensor("in_" + name, a.shape, F32, kind="ExternalInput").ap()
    for name, shape in _OUTS.items():
        t[name] = nc.dram_tensor("out_" + name, shape, F32, kind="ExternalOutput").ap()
    build(nc, t)
    r = run_bass_kernel_spmd(nc, [{"in_" + k: v for k, v in arrays.items()}], core_ids=[0])
    return _put_back({name: r.results[0]["out_" + name] for name in _OUTS})
```
